# Optimizing a Trainium2 kernel written in Bass

```python
import functools
import jax, jax.numpy as jnp
from jax import lax
import numpy as np

D_MODEL = 1024
BATCH = 1
SEQ = 128
DEPTH = 2
DEC_BATCH = 1
DEC_SEQ = 1024
PAST_LEN = 128

GRID_W = 64
HEAD_DIM = 64
H_ATTN = 6
KV_ATTN = 2
H_MLSTM = 4
H_NBHD = 6
D_FF = 4 * D_MODEL
Q_BLOCK = 128
MLSTM_CHUNK = 64
NA_ROWS = 8
NA_COLS = 16
ROPE_THETA = 10000.0
EPS = 1e-6
N_MOD = 6

W_ATTN = H_ATTN * HEAD_DIM
W_KV = KV_ATTN * HEAD_DIM
W_MLSTM = H_MLSTM * HEAD_DIM
W_NBHD = H_NBHD * HEAD_DIM
MIX_WIDTH = W_ATTN + W_MLSTM + W_NBHD
N_GATES = 4 * H_MLSTM
IN_SPLITS = (W_ATTN, W_KV, W_KV, W_MLSTM, W_MLSTM, W_MLSTM, W_MLSTM, N_GATES, W_NBHD, W_NBHD, W_NBHD)
IN_WIDTH = sum(IN_SPLITS)

kernel_name = "hybrid_diffusion_gqa_mlstm_natten_step"

def rms_norm(x, g):
    xf = x.astype(jnp.float32)
    y = xf * lax.rsqrt(jnp.mean(xf * xf, axis=-1, keepdims=True) + EPS)
    return (y * g.astype(jnp.float32)).astype(x.dtype)

def split_heads(a, n_heads):
    return a.reshape(a.shape[:-1] + (n_heads, HEAD_DIM))

def split_projection(z):
    parts, start = [], 0
    for w in IN_SPLITS:
        parts.append(z[..., start:start + w])
        start += w
    return parts

def axial_rope(x, row, col):
    half = HEAD_DIM // 2
    quarter = half // 2
    inv_freq = ROPE_THETA ** (-jnp.arange(quarter, dtype=jnp.float32) / quarter)

    def rotate(xp, pos):
        ang = pos.astype(jnp.float32)[:, None] * inv_freq[None, :]
        cos = jnp.cos(ang)[None, :, None, :]
        sin = jnp.sin(ang)[None, :, None, :]
        x1, x2 = xp[..., :quarter], xp[..., quarter:]
        return jnp.concatenate([x1 * cos - x2 * sin, x2 * cos + x1 * sin], axis=-1)

    xf = x.astype(jnp.float32)
    return jnp.concatenate([rotate(xf[..., :half], row), rotate(xf[..., half:], col)], axis=-1).astype(x.dtype)

def gqa_attention(q, k, v):
    B, Sq, H, Dh = q.shape
    n_kv = k.shape[2]
    G = H // n_kv
    nb = Sq // Q_BLOCK
    qb = jnp.moveaxis(q.reshape(B, nb, Q_BLOCK, n_kv, G, Dh), 1, 0)
    scale = Dh ** -0.5

    def block(qblk):
        s = jnp.einsum('bqngd,bsnd->bngqs', qblk, k, preferred_element_type=jnp.float32) * scale
        p = jax.nn.softmax(s, axis=-1).astype(v.dtype)
        return jnp.einsum('bngqs,bsnd->bqngd', p, v)

    o = lax.map(block, qb)
    return jnp.moveaxis(o, 0, 1).reshape(B, Sq, H * Dh)

def neighbourhood_attention(q, k, v, k_ctx, v_ctx, rel_bias):
    B, S, H, Dh = q.shape
    rows = S // GRID_W
    kr = min(NA_ROWS, rows)
    scale = Dh ** -0.5
    qg = q.reshape(B, rows, GRID_W, H, Dh)
    kg = k.reshape(B, rows, GRID_W, H, Dh)
    vg = v.reshape(B, rows, GRID_W, H, Dh)
    col = jnp.arange(GRID_W)
    col_start = jnp.clip(col - NA_COLS // 2, 0, GRID_W - NA_COLS)
    col_idx = col_start[:, None] + jnp.arange(NA_COLS)[None, :]
    dc = col_idx - col[:, None] + (NA_COLS - 1)
    n_nb = kr * NA_COLS

    def one_row(args):
        q_r, r = args
        rs = jnp.clip(r - kr // 2, 0, rows - kr)
        k_slab = lax.dynamic_slice_in_dim(kg, rs, kr, axis=1)
        v_slab = lax.dynamic_slice_in_dim(vg, rs, kr, axis=1)
        k_nb = k_slab[:, :, col_idx]
        v_nb = v_slab[:, :, col_idx]
        dr = rs + jnp.arange(kr) - r + (NA_ROWS - 1)
        bias = rel_bias[:, dr][:, :, dc].transpose(0, 2, 1, 3).astype(jnp.float32)
        s_nb = jnp.einsum('bwhd,bawchd->bhwac', q_r, k_nb, preferred_element_type=jnp.float32) * scale + bias[None]
        s_ctx = jnp.einsum('bwhd,bphd->bhwp', q_r, k_ctx, preferred_element_type=jnp.float32) * scale
        s = jnp.concatenate([s_nb.reshape(B, H, GRID_W, n_nb), s_ctx], axis=-1)
        p = jax.nn.softmax(s, axis=-1).astype(v.dtype)
        p_nb = p[..., :n_nb].reshape(B, H, GRID_W, kr, NA_COLS)
        p_ctx = p[..., n_nb:]
        return (jnp.einsum('bhwac,bawchd->bwhd', p_nb, v_nb)
                + jnp.einsum('bhwp,bphd->bwhd', p_ctx, v_ctx))

    o = lax.map(one_row, (jnp.moveaxis(qg, 1, 0), jnp.arange(rows)))
    return jnp.moveaxis(o, 0, 1).reshape(B, S, H * Dh)

def mlstm_chunkwise(q, k, v, i_pre, log_f, C0, n0, m0):
    B, S, H, Dh = q.shape
    L = MLSTM_CHUNK
    nc = S // L

    def chunks(a):
        return jnp.moveaxis(a.reshape((B, nc, L) + a.shape[2:]), 1, 0)

    causal = jnp.tril(jnp.ones((L, L), dtype=bool))

    def step(carry, xs):
        C, n, m = carry
        qc, kc, vc, ic, fc = xs
        b = jnp.cumsum(fc, axis=1).transpose(0, 2, 1)
        ig = ic.transpose(0, 2, 1)
        d = jnp.where(causal, b[..., :, None] - b[..., None, :] + ig[..., None, :], -jnp.inf)
        inter = b + m[..., None]
        m_t = jnp.maximum(inter, jnp.max(d, axis=-1))
        w = jnp.einsum('blhd,bshd->bhls', qc, kc) * jnp.exp(d - m_t[..., None])
        w_inter = jnp.exp(inter - m_t)
        num = (jnp.einsum('bhls,bshd->blhd', w, vc)
               + jnp.einsum('bhl,blhk,bhkd->blhd', w_inter, qc, C))
        den = jnp.sum(w, axis=-1) + w_inter * jnp.einsum('blhk,bhk->bhl', qc, n)
        den = jnp.maximum(jnp.abs(den), jnp.exp(-m_t))
        h = num / den.transpose(0, 2, 1)[..., None]
        b_last = b[..., -1]
        g = b_last[..., None] - b + ig
        m_new = jnp.maximum(b_last + m, jnp.max(g, axis=-1))
        a = jnp.exp(g - m_new[..., None])
        decay = jnp.exp(b_last + m - m_new)
        C_new = decay[..., None, None] * C + jnp.einsum('bhs,bshk,bshd->bhkd', a, kc, vc)
        n_new = decay[..., None] * n + jnp.einsum('bhs,bshk->bhk', a, kc)
        return (C_new, n_new, m_new), h

    (C, n, m), h = lax.scan(step, (C0, n0, m0),
                            (chunks(q), chunks(k), chunks(v), chunks(i_pre), chunks(log_f)))
    return jnp.moveaxis(h, 0, 1).reshape(B, S, H, Dh), C, n, m

def mlstm_bidirectional(q, k, v, gates, C0, n0, m0):
    f32 = jnp.float32
    q = q.astype(f32)
    k = k.astype(f32) * HEAD_DIM ** -0.5
    v = v.astype(f32)
    g = gates.astype(f32).reshape(gates.shape[:-1] + (4, H_MLSTM))
    i_f, lf_f = g[..., 0, :], jax.nn.log_sigmoid(g[..., 1, :])
    i_b, lf_b = g[..., 2, :], jax.nn.log_sigmoid(g[..., 3, :])
    C0, n0, m0 = C0.astype(f32), n0.astype(f32), m0.astype(f32)
    h_f, Cf, nf, mf = mlstm_chunkwise(q, k, v, i_f, lf_f, C0[:, 0], n0[:, 0], m0[:, 0])
    rev = lambda a: jnp.flip(a, axis=1)
    h_b, Cb, nb, mb = mlstm_chunkwise(rev(q), rev(k), rev(v), rev(i_b), rev(lf_b), C0[:, 1], n0[:, 1], m0[:, 1])
    return (h_f + rev(h_b), jnp.stack([Cf, Cb], axis=1), jnp.stack([nf, nb], axis=1),
            jnp.stack([mf, mb], axis=1))

def mlstm_output(h, o_pre, out_norm):
    hn = rms_norm(h, out_norm)
    return (jax.nn.sigmoid(o_pre.astype(jnp.float32)) * hn.reshape(hn.shape[:2] + (W_MLSTM,))).astype(o_pre.dtype)

def context_mixer(h, w_in, q_norm, k_norm, gate_bias, out_norm, w_out):
    B = h.shape[0]
    qa, ka, va, qb, kb, vb, ob, gb, qc, kc, vc = split_projection(h @ w_in)
    qa = rms_norm(split_heads(qa, H_ATTN), q_norm)
    ka = rms_norm(split_heads(ka, KV_ATTN), k_norm)
    va = split_heads(va, KV_ATTN)
    out_a = gqa_attention(qa, ka, va)
    zC = jnp.zeros((B, 2, H_MLSTM, HEAD_DIM, HEAD_DIM), jnp.float32)
    zn = jnp.zeros((B, 2, H_MLSTM, HEAD_DIM), jnp.float32)
    zm = jnp.zeros((B, 2, H_MLSTM), jnp.float32)
    hb, C, n, m = mlstm_bidirectional(split_heads(qb, H_MLSTM), split_heads(kb, H_MLSTM),
                                      split_heads(vb, H_MLSTM), gb + gate_bias, zC, zn, zm)
    out_b = mlstm_output(hb, ob, out_norm)
    kc = split_heads(kc, H_NBHD)
    vc = split_heads(vc, H_NBHD)
    out_c = gqa_attention(split_heads(qc, H_NBHD), kc, vc)
    out = jnp.concatenate([out_a, out_b, out_c], axis=-1) @ w_out
    return out, (ka, va, kc, vc, C, n, m)

def latent_mixer(h, ck_a, cv_a, ck_c, cv_c, sC, sn, sm, w_in, q_norm, k_norm, gate_bias, out_norm, rel_bias, w_out):
    S = h.shape[1]
    pos = jnp.arange(S)
    row, col = pos // GRID_W, pos % GRID_W
    qa, ka, va, qb, kb, vb, ob, gb, qc, kc, vc = split_projection(h @ w_in)
    qa = axial_rope(rms_norm(split_heads(qa, H_ATTN), q_norm), row, col)
    ka = axial_rope(rms_norm(split_heads(ka, KV_ATTN), k_norm), row, col)
    out_a = gqa_attention(qa, jnp.concatenate([ka, ck_a.astype(ka.dtype)], axis=1),
                          jnp.concatenate([split_heads(va, KV_ATTN), cv_a.astype(va.dtype)], axis=1))
    hb, _, _, _ = mlstm_bidirectional(split_heads(qb, H_MLSTM), split_heads(kb, H_MLSTM),
                                      split_heads(vb, H_MLSTM), gb + gate_bias, sC, sn, sm)
    out_b = mlstm_output(hb, ob, out_norm)
    out_c = neighbourhood_attention(split_heads(qc, H_NBHD), split_heads(kc, H_NBHD), split_heads(vc, H_NBHD),
                                    ck_c.astype(qc.dtype), cv_c.astype(qc.dtype), rel_bias)
    out = jnp.concatenate([out_a, out_b, out_c], axis=-1) @ w_out
    return out, ()

def modulation(cond, w_ada, b_ada):
    return jnp.split(jax.nn.silu(cond) @ w_ada + b_ada, N_MOD, axis=-1)

def squared_relu_mlp(h, w_up, w_down):
    return jnp.square(jax.nn.relu(h @ w_up)) @ w_down

def trunk_layer(x, mods, mixer, g_pre_mix, g_post_mix, g_pre_ffn, g_post_ffn, w_up, w_down):
    sh1, sc1, gt1, sh2, sc2, gt2 = mods
    mix_out, extras = mixer(rms_norm(x, g_pre_mix) * (1 + sc1) + sh1)
    x = x + gt1 * rms_norm(mix_out, g_post_mix)
    h = rms_norm(x, g_pre_ffn) * (1 + sc2) + sh2
    x = x + gt2 * rms_norm(squared_relu_mlp(h, w_up, w_down), g_post_ffn)
    return x, extras

def setup_inputs(seed: int = 0) -> dict:
    key = jax.random.key(seed)
    ks = jax.random.split(key, 26)
    f32 = jnp.float32
    nrm = lambda k, shape, s=1.0: s * jax.random.normal(k, shape, f32)
    fbias = jnp.linspace(3.0, 6.0, H_MLSTM, dtype=f32)
    zb = jnp.zeros((H_MLSTM,), f32)
    gate_base = jnp.concatenate([zb, fbias, zb, fbias])
    return {
        "x_prompt": nrm(ks[0], (BATCH, SEQ, D_MODEL)),
        "x_sample": nrm(ks[1], (DEC_BATCH, DEC_SEQ, D_MODEL)),
        "c": nrm(ks[2], (DEC_BATCH, D_MODEL)),
        "cache_k_attn": nrm(ks[3], (DEC_BATCH, DEPTH, PAST_LEN, KV_ATTN, HEAD_DIM)),
        "cache_v_attn": nrm(ks[4], (DEC_BATCH, DEPTH, PAST_LEN, KV_ATTN, HEAD_DIM)),
        "cache_k_nbhd": nrm(ks[5], (DEC_BATCH, DEPTH, PAST_LEN, H_NBHD, HEAD_DIM)),
        "cache_v_nbhd": nrm(ks[6], (DEC_BATCH, DEPTH, PAST_LEN, H_NBHD, HEAD_DIM)),
        "state_mlstm_C": nrm(ks[7], (DEC_BATCH, DEPTH, 2, H_MLSTM, HEAD_DIM, HEAD_DIM), 0.1),
        "state_mlstm_n": nrm(ks[8], (DEC_BATCH, DEPTH, 2, H_MLSTM, HEAD_DIM), 0.1),
        "state_mlstm_m": nrm(ks[9], (DEC_BATCH, DEPTH, 2, H_MLSTM)),
        "c_ctx": nrm(ks[10], (D_MODEL,)),
        "w_ada": nrm(ks[11], (DEPTH, D_MODEL, N_MOD * D_MODEL), 0.5 * D_MODEL ** -0.5),
        "b_ada": nrm(ks[12], (DEPTH, N_MOD * D_MODEL), 0.01),
        "g_pre_mix": 1.0 + nrm(ks[13], (DEPTH, D_MODEL), 0.02),
        "g_post_mix": 1.0 + nrm(ks[14], (DEPTH, D_MODEL), 0.02),
        "g_pre_ffn": 1.0 + nrm(ks[15], (DEPTH, D_MODEL), 0.02),
        "g_post_ffn": 1.0 + nrm(ks[16], (DEPTH, D_MODEL), 0.02),
        "w_in": nrm(ks[17], (DEPTH, D_MODEL, IN_WIDTH), D_MODEL ** -0.5),
        "q_norm_attn": 1.0 + nrm(ks[18], (DEPTH, HEAD_DIM), 0.02),
        "k_norm_attn": 1.0 + nrm(ks[19], (DEPTH, HEAD_DIM), 0.02),
        "mlstm_gate_bias": gate_base[None, :] + nrm(ks[20], (DEPTH, N_GATES), 0.1),
        "mlstm_out_norm": 1.0 + nrm(ks[21], (DEPTH, H_MLSTM, HEAD_DIM), 0.02),
        "nbhd_rel_bias": nrm(ks[22], (DEPTH, H_NBHD, 2 * NA_ROWS - 1, 2 * NA_COLS - 1), 0.1),
        "w_out": nrm(ks[23], (DEPTH, MIX_WIDTH, D_MODEL), MIX_WIDTH ** -0.5),
        "w_ffn_up": nrm(ks[24], (DEPTH, D_MODEL, D_FF), D_MODEL ** -0.5),
        "w_ffn_down": nrm(ks[25], (DEPTH, D_FF, D_MODEL), D_FF ** -0.5),
    }

def reference(x_prompt, x_sample, c, cache_k_attn, cache_v_attn, cache_k_nbhd, cache_v_nbhd,
              state_mlstm_C, state_mlstm_n, state_mlstm_m, c_ctx, w_ada, b_ada,
              g_pre_mix, g_post_mix, g_pre_ffn, g_post_ffn, w_in, q_norm_attn, k_norm_attn,
              mlstm_gate_bias, mlstm_out_norm, nbhd_rel_bias, w_out, w_ffn_up, w_ffn_down):
    xp = x_prompt
    ctx = []
    for l in range(DEPTH):
        mods = modulation(c_ctx, w_ada[l], b_ada[l])
        mixer = functools.partial(context_mixer, w_in=w_in[l], q_norm=q_norm_attn[l], k_norm=k_norm_attn[l],
                                  gate_bias=mlstm_gate_bias[l], out_norm=mlstm_out_norm[l], w_out=w_out[l])
        xp, extras = trunk_layer(xp, mods, mixer, g_pre_mix[l], g_post_mix[l], g_pre_ffn[l], g_post_ffn[l],
                                 w_ffn_up[l], w_ffn_down[l])
        ctx.append(extras)
    new_k_attn = jnp.stack([e[0] for e in ctx], axis=1)
    new_v_attn = jnp.stack([e[1] for e in ctx], axis=1)
    new_k_nbhd = jnp.stack([e[2] for e in ctx], axis=1)
    new_v_nbhd = jnp.stack([e[3] for e in ctx], axis=1)
    new_mlstm_C = jnp.stack([e[4] for e in ctx], axis=1)
    new_mlstm_n = jnp.stack([e[5] for e in ctx], axis=1)
    new_mlstm_m = jnp.stack([e[6] for e in ctx], axis=1)

    xs = x_sample
    for l in range(DEPTH):
        mods = [m[:, None, :] for m in modulation(c, w_ada[l], b_ada[l])]
        mixer = functools.partial(latent_mixer, ck_a=cache_k_attn[:, l], cv_a=cache_v_attn[:, l],
                                  ck_c=cache_k_nbhd[:, l], cv_c=cache_v_nbhd[:, l],
                                  sC=state_mlstm_C[:, l], sn=state_mlstm_n[:, l], sm=state_mlstm_m[:, l],
                                  w_in=w_in[l], q_norm=q_norm_attn[l], k_norm=k_norm_attn[l],
                                  gate_bias=mlstm_gate_bias[l], out_norm=mlstm_out_norm[l],
                                  rel_bias=nbhd_rel_bias[l], w_out=w_out[l])
        xs, _ = trunk_layer(xs, mods, mixer, g_pre_mix[l], g_post_mix[l], g_pre_ffn[l], g_post_ffn[l],
                            w_ffn_up[l], w_ffn_down[l])

    return (xp, xs, new_k_attn, new_v_attn, new_k_nbhd, new_v_nbhd, new_mlstm_C, new_mlstm_n, new_mlstm_m)


_drawn_inputs = setup_inputs


def setup_inputs(seed=0):
    import zlib

    import numpy as np

    out = dict(_drawn_inputs(seed))
    spreads = {}
    factors = {'cache_k_attn': 5.156,
     'cache_v_attn': 4.011,
     'state_mlstm_C': 3.485,
     'state_mlstm_n': 8.0,
     'state_mlstm_m': 3.94,
     'g_post_mix': 5.877,
     'g_pre_ffn': 5.81,
     'g_post_ffn': 6.257,
     'q_norm_attn': 8.0,
     'k_norm_attn': 2.896,
     'mlstm_out_norm': 8.0,
     'nbhd_rel_bias': 8.0}
    for name, (base, spread) in spreads.items():
        noise = np.random.default_rng([zlib.crc32(name.encode()), seed]).standard_normal(out[name].shape)
        drawn = base * np.exp(spread * noise) if base else spread * noise
        out[name] = __import__('jax').numpy.asarray(drawn.astype(out[name].dtype))
    for name, factor in factors.items():
        out[name] = (out[name] * factor).astype(out[name].dtype)
    return out
```

```python
from contextlib import ExitStack

import concourse.bass as bass
import concourse.mybir as mybir
import numpy as np

ALU = mybir.AluOpType
ACT = mybir.ActivationFunctionType
AX = mybir.AxisListType
F32 = mybir.dt.float32
F32R = mybir.dt.float32r

P = 128
D = 1024
KD = D // P
DEPTH = 2
LAT = 8
NT = LAT + 1
PROMPT = LAT
TOK = NT * P
CTX_SLOT = 8
PROMPT_SLOT = 9
NSLOT = 10
HD = 64
GRID_W = 64
ROWS = 16
NA_ROWS = 8
NA_COLS = 16
EPS = 1e-6
SCALE = HD ** -0.5
NEG = -1e30
LOWEST = -3e38
OFF_A, OFF_B, OFF_C = 0, 640, 1680
W_C = 384
D_FF = 4096
HID = 256
VA = HD + 1
WIN_ROWS = 10
WIN = WIN_ROWS * GRID_W
WIN_TYPES = 5
BIAS_U = 18
BIAS_DR = 20
BIAS_W = 2 * GRID_W - 1


def window_start_row(t):
    return min(max(2 * t - 4, 0), ROWS - WIN_ROWS)


def window_type(t):
    return {0: 0, 1: 1, 6: 3, 7: 4}.get(t, 2)


def key_slot(t):
    return PROMPT_SLOT if t == PROMPT else t


def shape_constants():
    f = np.float32
    ident = np.eye(P, dtype=f)
    quarter = HD // 4
    inv = (10000.0 ** (-np.arange(quarter, dtype=f) / quarter)).astype(f)
    pos = np.arange(LAT * P)
    cos = np.zeros((LAT * P, 2, 2, quarter), f)
    sin = np.zeros((LAT * P, 2, 2, quarter), f)
    for half, x in enumerate((pos // GRID_W, pos % GRID_W)):
        ang = x.astype(f)[:, None] * inv[None, :]
        cos[:, half, 0] = cos[:, half, 1] = np.cos(ang)
        sin[:, half, 0] = -np.sin(ang)
        sin[:, half, 1] = np.sin(ang)
    cos = cos.reshape(LAT, P, HD).transpose(1, 0, 2)
    sin = sin.reshape(LAT, P, HD).transpose(1, 0, 2)
    s = np.arange(P)
    causal = np.zeros((P, 2, P), f)
    causal[:, 0] = np.where(s[:, None] <= s[None, :], 0, NEG)
    causal[:, 1] = np.where(s[:, None] >= s[None, :], 0, NEG)
    window = np.full((P, WIN_TYPES, WIN_ROWS, GRID_W), NEG, f)
    for t in (0, 1, 2, 6, 7):
        for p in range(P):
            r, c = 2 * t + p // GRID_W, p % GRID_W
            rs = min(max(r - NA_ROWS // 2, 0), ROWS - NA_ROWS) - window_start_row(t)
            cs = min(max(c - NA_COLS // 2, 0), GRID_W - NA_COLS)
            window[p, window_type(t), rs:rs + NA_ROWS, cs:cs + NA_COLS] = 0
    neg_select = np.zeros((36, 4, P), f)
    diagonal = np.zeros((36, 4, NT), f)
    for j in range(4):
        for b in (0, 32):
            neg_select[b + j, j] = -1
            diagonal[b + j, j] = 1
    blocks = np.zeros((P, 2, 2, VA), f)
    blocks[:HD, :, 0] = 1
    blocks[HD:, :, 1] = 1
    cond_select = np.zeros((2, 2, P), f)
    cond_select[0, 0] = cond_select[1, 1] = 1
    return {
        "ident": ident, "cos": cos.copy(), "sin": sin.copy(), "causal": causal,
        "window": window.reshape(P, WIN_TYPES * WIN), "neg_select": neg_select,
        "diagonal": diagonal, "blocks": blocks.reshape(P, 4 * VA), "cond_select": cond_select,
    }


class Steps:

    def __init__(self, eng, sem):
        self.eng, self.sem, self.n = eng, sem, 0

    def __call__(self, ins):
        self.n += 1
        ins.then_inc(self.sem, 1)
        self.eng.wait_ge(self.sem, self.n)


def build(nc, I, O):
    sems = {}
    with ExitStack() as ctx:
        sem_stack = ExitStack()
        dve_step = act_step = pool_step = None

        def sem(name):
            if name not in sems:
                sems[name] = sem_stack.enter_context(nc.semaphore(name))
            return sems[name]

        def open_section():
            nonlocal dve_step, act_step, pool_step
            dve_step = Steps(nc.vector, sem("dve_steps"))
            act_step = Steps(nc.scalar, sem("act_steps"))
            pool_step = Steps(nc.gpsimd, sem("pool_steps"))

        def close_section():
            numbers = sorted(s.num for s in sems.values())
            first = 0
            for i, n in enumerate(numbers):
                if i + 1 == len(numbers) or numbers[i + 1] != n + 1:
                    nc.all_engine_barrier(sems_to_clear=range(numbers[first], n + 1))
                    first = i + 1
            sem_stack.close()
            sems.clear()

        def sb(name, shape, stack=ctx, dtype=F32):
            return stack.enter_context(nc.sbuf_tensor(name, shape, dtype))

        def dram(name, shape):
            return nc.dram_tensor(name, shape, F32, kind="Internal").ap()

        ps = ctx.enter_context(nc.psum_tensor("ps", [P, 8, 512], F32))
        psf = ps[:, :, :].rearrange("p b n -> p (b n)")

        x_dram = dram("x_residual", (TOK, D))
        bias_pitch = BIAS_DR * BIAS_W
        bias_dram = dram("bias_by_column", (DEPTH, 6, GRID_W * bias_pitch))
        bias_copied = ctx.enter_context(nc.semaphore("bias_copied"))

        ident = sb("ident_sb", [P, P])
        causal = sb("causal_sb", [P, 2, P])
        neg_select = sb("neg_select_sb", [36, 4, P])
        diagonal = sb("diagonal_sb", [36, 4, NT])
        blocks = sb("blocks_sb", [P, 4 * VA])
        cond_select = sb("cond_select_sb", [2, 2, P])
        ones = sb("ones", [36, P])
        zeros = sb("zeros", [36, P])
        minus_half = sb("minus_half", [P, NT * 4])
        condT = sb("condT", [P, KD, 2])
        cond_e = sb("cond_e", [P, KD, 2])
        modT = sb("modT", [P, 4, KD, 2])
        gate = sb("gate", [P, 2, 2, D])
        mix = sb("mix", [P, NT, D])
        small = sb("small", [P, 256])

        with nc.Block() as block:
            @block.sync
            def _(sp):
                for k, t in (("ident", ident[:, :]), ("causal", causal[:, :, :]), ("neg_select", neg_select[:, :, :]),
                             ("diagonal", diagonal[:, :, :]), ("blocks", blocks[:, :]),
                             ("cond_select", cond_select[:, :, :])):
                    sp.dma_start(t, I[k]).then_inc(sem("constants_loaded"), 16)
                sp.dma_start(x_dram[0:LAT * P, :], I["x_sample"]).then_inc(sem("residual_copied"), 16)
                sp.dma_start(x_dram[LAT * P:TOK, :], I["x_prompt"]).then_inc(sem("residual_copied"), 16)
                for l in range(DEPTH):
                    for h in range(6):
                        sp.dma_start(bias_dram[l, h].rearrange("(c j) -> c j", c=GRID_W),
                                     I["bias_rows"][l, h:h + 1, :].to_broadcast([GRID_W, bias_pitch])).then_inc(bias_copied, 16)
                sp.wait_ge(sem("constants_loaded"), 6 * 16)
                sp.wait_ge(sem("residual_copied"), 2 * 16)

            @block.gpsimd
            def _(pool):
                pool.memset(ones[:, :], 1.0)
                pool.memset(zeros[:, :], 0.0)
                pool.memset(small[:, :], 0.0)
                pool.memset(minus_half[:, :], -0.5)

            @block.scalar
            def _(act):
                act.dma_start(condT[:, :, :], I["condT"]).then_inc(sem("cond_loaded"), 16)
                act.wait_ge(sem("cond_loaded"), 16)
                act.activation(cond_e[:, :, :], condT[:, :, :], ACT.Exp, scale=-1.0).then_inc(sem("cond_exp"), 1)

            @block.vector
            def _(dve):
                step = Steps(dve, sem("silu_steps"))
                dve.wait_ge(sem("cond_exp"), 1)
                step(dve.tensor_scalar(cond_e[:, :, :], cond_e[:, :, :], 1.0, None, ALU.add))
                step(dve.reciprocal(cond_e[:, :, :], cond_e[:, :, :]))
                step(dve.tensor_tensor(condT[:, :, :], condT[:, :, :], cond_e[:, :, :], ALU.mult))

        close_section()
        with nc.Fori(0, DEPTH) as l:

            def modulation():
                NC_ = 6 * D // 512
                RING = 3
                with ExitStack() as own:
                    w = sb("w_ada_ring", [P, RING, KD, 512], own)
                    row = sb("mod_row", [2, 6 * D], own)
                    gpost = sb("gpost_row", [2, 2, D], own)
                    gpre = sb("gpreT", [P, 2, KD], own)
                    w_dram = I["w_ada"][l].rearrange("(k p) n -> p k n", p=P)
                    with nc.Block() as block:
                        @block.sync
                        def _(sp):
                            sp.dma_start(row[:, :], I["b_ada"][bass.ds(l, 1), :].to_broadcast([2, 6 * D])).then_inc(sem("mod_rows_loaded"), 16)
                            for s in range(2):
                                sp.dma_start(gpost[:, s, :], I["g_post"][bass.ds(l, 1), s, :].to_broadcast([2, D])).then_inc(sem("mod_rows_loaded"), 16)
                            sp.dma_start(gpre[:, :, :], I["g_preT"][l]).then_inc(sem("mod_rows_loaded"), 16)
                            for c in range(NC_):
                                if c >= RING:
                                    sp.wait_ge(sem("w_ada_used"), c - RING + 1)
                                sp.dma_start(w[:, c % RING, :, :], w_dram[:, :, c * 512:(c + 1) * 512]).then_inc(sem(f"w_ada_loaded{c % RING}"), 16)

                        @block.tensor
                        def _(pe):
                            for c in range(NC_):
                                pe.wait_ge(sem(f"w_ada_loaded{c % RING}"), 16 * (c // RING + 1))
                                if c >= 2:
                                    pe.wait_ge(sem("mod_row_added"), c - 1)
                                for k in range(KD):
                                    mm = pe.matmul(ps[0:2, c % 2, :], condT[:, k, :], w[:, c % RING, k, :],
                                                   start=(k == 0), stop=(k == KD - 1))
                                mm.then_inc(sem("w_ada_used"), 1)
                            pe.wait_ge(sem("mod_row_added"), NC_)
                            for i, v in enumerate((0, 1, 3, 4)):
                                for k in range(KD):
                                    mm = pe.transpose(ps[:, 2, (i * KD + k) * 2:(i * KD + k) * 2 + 2],
                                                      row[:, v * D + k * P:v * D + (k + 1) * P], ident[0:2, 0:2])
                            mm.then_inc(sem("mods_transposed"), 1)
                            pe.wait_ge(sem("gates_scaled"), 1)
                            for i in range(8):
                                s, c, n = i // 4, i // 2 % 2, i % 2
                                if i >= 4:
                                    pe.wait_ge(sem("gate_copied"), i - 3)
                                v = (2, 5)[s]
                                pe.matmul(ps[:, 3 + i % 4, :], cond_select[:, c, :],
                                          row[:, v * D + n * 512:v * D + (n + 1) * 512],
                                          start=True, stop=True).then_inc(sem("gate_spread"), 1)

                        @block.vector
                        def _(dve):
                            dve.wait_ge(sem("mod_rows_loaded"), 64)
                            for c in range(NC_):
                                dve.wait_ge(sem("w_ada_used"), c + 1)
                                dve.tensor_tensor(row[:, c * 512:(c + 1) * 512], ps[0:2, c % 2, :],
                                                  row[:, c * 512:(c + 1) * 512], ALU.add).then_inc(sem("mod_row_added"), 1)
                            dve.wait_ge(sem("mod_row_added"), NC_)
                            dve_step(dve.tensor_tensor(row[:, 2 * D:3 * D], row[:, 2 * D:3 * D], gpost[:, 0, :], ALU.mult))
                            dve.tensor_tensor(row[:, 5 * D:6 * D], row[:, 5 * D:6 * D], gpost[:, 1, :],
                                              ALU.mult).then_inc(sem("gates_scaled"), 1)
                            dve.wait_ge(sem("mods_transposed"), 1)
                            mt = ps[:, 2, 0:8 * KD].rearrange("p (v k c) -> p v k c", v=4, c=2)
                            dve_step(dve.tensor_copy(modT[:, :, :, :], mt))
                            for s in range(2):
                                for c in range(2):
                                    dve_step(dve.scalar_tensor_tensor(modT[:, 2 * s + 1, :, c], mt[:, 2 * s + 1, :, c], 1.0,
                                                                      gpre[:, s, :], ALU.add, ALU.mult))

                        @block.scalar
                        def _(act):
                            for i in range(8):
                                s, c, n = i // 4, i // 2 % 2, i % 2
                                act.wait_ge(sem("gate_spread"), i + 1)
                                act.copy(gate[:, s, c, n * 512:(n + 1) * 512], ps[:, 3 + i % 4, :]).then_inc(sem("gate_copied"), 1)

            def residual_norm(tag, sub, norm):
                with ExitStack() as own:
                    xt = sb(f"{tag}_x_tiles", [P, 3, D], own)
                    junk = sb(f"{tag}_norm_junk", [P, D], own)
                    xn = sb(f"{tag}_x_normed", [P, 2, D], own)
                    full = sb(f"{tag}_h_full", [P, 2, KD, P], own) if norm == 1 else None
                    hi_done, lo_done = sem(f"{tag}_hi_done"), sem(f"{tag}_lo_done")

                    def modulated(t, k):
                        return full[:, t % 2, k, :] if norm == 1 else hT[:, k, t * P:(t + 1) * P]
                    ssq = small[:, 0:NT]
                    rstd = small[:, NT:2 * NT]
                    ssq2 = small[:, 2 * NT:3 * NT]
                    rstd2 = small[:, 3 * NT:4 * NT]
                    loaded = [sem(f"{tag}_x_loaded{i}") for i in range(3)]
                    stored = [sem(f"{tag}_x_stored{i}") for i in range(3)]
                    y_sq, y_rstd = sem(f"{tag}_y_squares"), sem(f"{tag}_y_rstd")
                    x_new, x_sq, x_rstd = sem(f"{tag}_x_new"), sem(f"{tag}_x_squares"), sem(f"{tag}_x_rstd")
                    normed, turned = sem(f"{tag}_normed"), sem(f"{tag}_turned")
                    mod_d, mod_a = sem(f"{tag}_modulated_dve"), sem(f"{tag}_modulated_act")
                    with nc.Block() as block:
                        @block.sync
                        def _(sp):
                            for t in range(NT + 2):
                                if t < NT:
                                    if t >= 3:
                                        if sub is not None:
                                            sp.wait_ge(stored[t % 3], 16 * (t // 3))
                                        if norm is not None:
                                            sp.wait_ge(normed, t - 2)
                                    sp.dma_start(xt[:, t % 3, :], x_dram[t * P:(t + 1) * P, :]).then_inc(loaded[t % 3], 16)
                                if sub is not None and t >= 2:
                                    u = t - 2
                                    sp.wait_ge(x_new, u + 1)
                                    sp.dma_start(x_dram[u * P:(u + 1) * P, :], xt[:, u % 3, :]).then_inc(stored[u % 3], 16)
                            if sub is not None:
                                for i in range(3):
                                    sp.wait_ge(stored[i], 16 * 3)

                        @block.scalar
                        def _(act):
                            def squares_y(t):
                                act_step(act.activation(junk[:, :], mix[:, t, :], ACT.Square, accum_out=ssq[:, t:t + 1]))
                                act.sem_inc(y_sq, 1)

                            def squares_x(t):
                                if sub is None:
                                    act.wait_ge(loaded[t % 3], 16 * (t // 3 + 1))
                                else:
                                    act.wait_ge(x_new, t + 1)
                                act_step(act.activation(junk[:, :], xt[:, t % 3, :], ACT.Square, accum_out=ssq2[:, t:t + 1]))
                                act.sem_inc(x_sq, 1)

                            def modulate(t):
                                c = 1 if t == PROMPT else 0
                                act.wait_ge(turned, t + 1)
                                if norm == 1 and t >= 2:
                                    act.wait_ge(lo_done, t - 1)
                                for k in range(4, KD):
                                    a = act.activation(modulated(t, k), psf[:, t % 2 * 1024 + k * P:t % 2 * 1024 + (k + 1) * P],
                                                       ACT.Identity, bias=modT[:, 2 * norm, k, c:c + 1],
                                                       scale=modT[:, 2 * norm + 1, k, c:c + 1])
                                a.then_inc(mod_a, 1)
                                if norm == 1:
                                    act.wait_ge(mod_a, t + 1)
                                    act.wait_ge(mod_d, t + 1)
                                    act.copy(hi[:, :, t * P:(t + 1) * P], full[:, t % 2, :, :]).then_inc(hi_done, 1)

                            for t in range(NT + 2):
                                if sub is not None and t < NT:
                                    squares_y(t)
                                if norm is not None and 1 <= t <= NT:
                                    squares_x(t - 1)
                                if norm is not None and t >= 2:
                                    modulate(t - 2)

                        @block.gpsimd
                        def _(pool):
                            def inverse_root(s, r, t, ready, done):
                                pool.wait_ge(ready, t + 1)
                                pool_step(pool.tensor_scalar(r[:, t:t + 1], s[:, t:t + 1], 1.0 / D, EPS, ALU.mult, ALU.add))
                                pool.tensor_tensor(r[:, t:t + 1], r[:, t:t + 1], minus_half[:, 0:1], ALU.pow).then_inc(done, 1)

                            for t in range(NT + 1):
                                if sub is not None and t < NT:
                                    inverse_root(ssq, rstd, t, y_sq, y_rstd)
                                if norm is not None and t >= 1:
                                    inverse_root(ssq2, rstd2, t - 1, x_sq, x_rstd)

                        @block.vector
                        def _(dve):
                            def add_residual(t):
                                dve.wait_ge(y_rstd, t + 1)
                                dve.wait_ge(loaded[t % 3], 16 * (t // 3 + 1))
                                dve_step(dve.scalar_tensor_tensor(mix[:, t, :], mix[:, t, :], rstd[:, t:t + 1],
                                                                  gate[:, sub, 1 if t == PROMPT else 0, :], ALU.mult, ALU.mult))
                                dve.tensor_tensor(xt[:, t % 3, :], xt[:, t % 3, :], mix[:, t, :], ALU.add).then_inc(x_new, 1)

                            def normalise(t):
                                dve.wait_ge(x_rstd, t + 1)
                                if sub is not None:
                                    dve.wait_ge(x_new, t + 1)
                                if t >= 2:
                                    dve.wait_ge(turned, t - 1)
                                dve.tensor_scalar(xn[:, t % 2, :], xt[:, t % 3, :], rstd2[:, t:t + 1], None, ALU.mult).then_inc(normed, 1)

                            def modulate(t):
                                c = 1 if t == PROMPT else 0
                                dve.wait_ge(turned, t + 1)
                                if norm == 1 and t >= 2:
                                    dve.wait_ge(lo_done, t - 1)
                                for k in range(4):
                                    a = dve.tensor_scalar(modulated(t, k), psf[:, t % 2 * 1024 + k * P:t % 2 * 1024 + (k + 1) * P],
                                                          modT[:, 2 * norm + 1, k, c:c + 1], modT[:, 2 * norm, k, c:c + 1],
                                                          ALU.mult, ALU.add)
                                a.then_inc(mod_d, 1)

                            def low_part(t):
                                dve.wait_ge(hi_done, t + 1)
                                tt = slice(t * P, (t + 1) * P)
                                dve.tensor_tensor(lo[:, :, tt], full[:, t % 2, :, :], hi[:, :, tt].bitcast(F32), ALU.subtract).then_inc(lo_done, 1)

                            for t in range(NT + 3):
                                if sub is not None and t < NT:
                                    add_residual(t)
                                if norm is not None and 1 <= t <= NT:
                                    normalise(t - 1)
                                if norm == 1 and t >= 3:
                                    low_part(t - 3)
                                if norm is not None and 2 <= t < NT + 2:
                                    modulate(t - 2)

                        @block.tensor
                        def _(pe):
                            if norm is None:
                                return
                            for t in range(NT):
                                pe.wait_ge(normed, t + 1)
                                if t >= 2:
                                    pe.wait_ge(mod_d, t - 1)
                                    pe.wait_ge(mod_a, t - 1)
                                for k in range(KD):
                                    mm = pe.transpose(psf[:, t % 2 * 1024 + k * P:t % 2 * 1024 + (k + 1) * P],
                                                      xn[:, t % 2, k * P:(k + 1) * P], ident[:, :])
                                mm.then_inc(turned, 1)

            def attention(tag, units, own, n_bias_cols):
                nu = len(units)
                P_sb = sb(f"{tag}_probs", [P, 2, NT * P], own)
                PT = sb(f"{tag}_probsT", [P, 2, NT * P], own)
                Ssb = sb(f"{tag}_scores", [P, 2, n_bias_cols], own) if n_bias_cols else None
                biased = sb(f"{tag}_bias_tiles", [P, 2, n_bias_cols], own) if n_bias_cols else None
                nmax = small[:, 64:68]
                den = small[:, 68:72]
                rden = small[:, 72:76]
                groups, count = [], [0, 0]
                for i, u in enumerate(units):
                    g0 = []
                    for g in range((u["n"] // P + 2) // 3):
                        e = len(groups) % 2
                        count[e] += 1
                        g0.append((len(groups), e, count[e], 3 * g, min(3 * g + 3, u["n"] // P)))
                        groups.append(g0[-1])
                    u["groups"] = g0
                copied = [sem(f"{tag}_probsT_copied_act"), sem(f"{tag}_probsT_copied_dve")]
                S_ready, max_ready, exp_done = sem(f"{tag}_scores_ready"), sem(f"{tag}_max_ready"), sem(f"{tag}_exp_done")
                turned, pv_done, out_done = sem(f"{tag}_probs_turned"), sem(f"{tag}_pv_done"), sem(f"{tag}_out_done")
                bias_ready = sem(f"{tag}_bias_ready")
                bias_count = [0]
                for u in units:
                    if u["bias"] is not None:
                        bias_count[0] += 1
                        u["bias_n"] = bias_count[0]

                def S(i, a, b):
                    return psf[:, i % 2 * 1536 + a:i % 2 * 1536 + b]

                def PTp(i, k, z):
                    at = (i % 2 * 3 + k // 3) * 512 + k % 3 * P
                    return psf[:, at:at + (z - k) * P]

                def out_p(i):
                    return ps[:, 6 + i % 2, 0:P]

                def tensor(pe):
                    def scores(i):
                        if i >= 2:
                            for gi, e, n, a, b in units[i - 2]["groups"]:
                                pe.wait_ge(copied[e], n)
                        for kT, c0 in units[i]["keys"]:
                            mm = pe.matmul(S(i, c0, c0 + kT.shape[1]), units[i]["q"], kT, start=True, stop=True)
                        mm.then_inc(S_ready, 1)

                    def turn(i):
                        pe.wait_ge(exp_done, i + 1)
                        for gi, e, n, a, b in units[i]["groups"]:
                            for k in range(a, b):
                                mm = pe.transpose(PTp(i, k, k + 1), P_sb[:, i % 2, k * P:(k + 1) * P], ident[:, :])
                            mm.then_inc(turned, 1)

                    def apply(i):
                        u = units[i]
                        if i >= 2:
                            pe.wait_ge(out_done, i - 1)
                        for gi, e, n, a, b in u["groups"]:
                            pe.wait_ge(copied[e], n)
                            for k in range(a, b):
                                mm = pe.matmul(out_p(i), PT[:, i % 2, k * P:(k + 1) * P], u["v"][k],
                                               start=(k == 0), stop=(k == u["n"] // P - 1))
                        mm.then_inc(pv_done, 1)

                    scores(0)
                    scores(1)
                    for i in range(nu):
                        turn(i)
                        if i >= 1:
                            apply(i - 1)
                        if i + 2 < nu:
                            scores(i + 2)
                    apply(nu - 1)

                def copy_groups(eng, e, i):
                    for gi, ge, n, a, b in units[i]["groups"]:
                        if ge != e:
                            continue
                        eng.wait_ge(turned, gi + 1)
                        src, dst = PTp(i, a, b), PT[:, i % 2, a * P:b * P]
                        ins = eng.copy(dst, src) if e == 0 else eng.tensor_copy(dst, src)
                        ins.then_inc(copied[e], 1)

                def scalar(act):
                    def exp(i):
                        n = units[i]["n"]
                        act.wait_ge(max_ready, i + 1)
                        if i >= 2:
                            act.wait_ge(turned, units[i - 2]["groups"][-1][0] + 1)
                        src = S(i, 0, n) if units[i]["bias"] is None else Ssb[:, i % 2, 0:n]
                        act.activation(P_sb[:, i % 2, 0:n], src, ACT.Exp, bias=nmax[:, i % 4:i % 4 + 1],
                                       accum_out=den[:, i % 4:i % 4 + 1]).then_inc(exp_done, 1)
                    exp(0)
                    for i in range(nu):
                        copy_groups(act, 0, i)
                        if i + 1 < nu:
                            exp(i + 1)

                def vector(dve):
                    def maximum(i):
                        u = units[i]
                        dve.wait_ge(S_ready, i + 1)
                        if u["bias"] is None:
                            dve.tensor_reduce(nmax[:, i % 4:i % 4 + 1], S(i, 0, u["n"]), AX.X, ALU.max, negate=True).then_inc(max_ready, 1)
                        else:
                            dve.wait_ge(bias_ready, u["bias_n"])
                            if i >= 2:
                                dve.wait_ge(exp_done, i - 1)
                            dve_step(dve.tensor_tensor_reduce(Ssb[:, i % 2, :], S(i, 0, u["n"]), biased[:, u["bias_n"] % 2, :], 1.0, LOWEST,
                                                              ALU.add, ALU.max, nmax[:, i % 4:i % 4 + 1]))
                            dve.tensor_scalar(nmax[:, i % 4:i % 4 + 1], nmax[:, i % 4:i % 4 + 1], -1.0, None, ALU.mult).then_inc(max_ready, 1)

                    def output(i):
                        dve.wait_ge(exp_done, i + 1)
                        dve_step(dve.reciprocal(rden[:, i % 4:i % 4 + 1], den[:, i % 4:i % 4 + 1]))
                        dve.wait_ge(pv_done, i + 1)
                        dve.tensor_scalar(units[i]["out"], out_p(i)[:, units[i]["cols"]], rden[:, i % 4:i % 4 + 1], None,
                                          ALU.mult).then_inc(out_done, 1)
                    maximum(0)
                    maximum(1)
                    for i in range(nu):
                        copy_groups(dve, 1, i)
                        if i >= 1:
                            output(i - 1)
                        if i + 2 < nu:
                            maximum(i + 2)
                    output(nu - 1)

                return tensor, scalar, vector, biased, bias_ready, max_ready

            w_in = I["w_in"][l].rearrange("(k p) n -> p k n", p=P)

            def mixer_a():
                with ExitStack() as own:
                    Z = sb("a_z", [P, NT, 512], own)
                    QK = sb("a_qkT", [P, 4, NSLOT * P], own)
                    V = sb("a_v", [P, NSLOT, P], own)
                    g = sb("a_g", [P, 8, HD], own)
                    ctx_k = sb("a_ctx_k", [P, P], own)
                    with ExitStack() as inner:
                        sq = sb("a_sq", [P, 2, 512], inner)
                        r1 = sb("a_r1", [P, 2, 512], inner)
                        r2 = sb("a_r2", [P, 512], inner)
                        zr = sb("a_zr", [P, 2, 512], inner)
                        cos = sb("cos_sb", [P, LAT, HD], inner)
                        sin = sb("sin_sb", [P, LAT, HD], inner)
                        ss = small[:, 96:96 + NT * 8].rearrange("p (t h) -> p t h", h=8)
                        rs = small[:, 168:168 + NT * 8].rearrange("p (t h) -> p t h", h=8)
                        cuts = ((OFF_A, 384), (OFF_A + 384, 256))
                        with nc.Block() as block:
                            @block.sync
                            def _(sp):
                                for c, (o, n) in enumerate(cuts):
                                    sp.dma_start(ring[:, c, :, 0:n], w_in[:, :, o:o + n]).then_inc(sem(f"a_w_loaded{c}"), 16)
                                sp.dma_start(ctx_k[:, :], I["cache_k_attn"][l]).then_inc(sem("a_ctx_k_loaded"), 16)
                                sp.dma_start(V[:, CTX_SLOT, :], I["cache_v_attn"][l]).then_inc(sem("a_ctx_v_loaded"), 16)
                                sp.dma_start(cos[:, :, :], I["cos"]).then_inc(sem("a_rotary_loaded"), 16)
                                sp.dma_start(sin[:, :, :], I["sin"]).then_inc(sem("a_rotary_loaded"), 16)
                                for h in range(8):
                                    src = I["q_norm"] if h < 6 else I["k_norm"]
                                    sp.dma_start(g[:, h, :], src[bass.ds(l, 1), :].to_broadcast([P, HD])).then_inc(sem("a_g_loaded"), 16)
                                sp.wait_ge(sem("a_normed"), NT)
                                sp.dma_start(O["new_k_attn"][l], Z[:, PROMPT, 384:512]).then_inc(sem("a_cache_stored"), 16)
                                sp.wait_ge(sem("a_v_copied"), NT)
                                sp.dma_start(O["new_v_attn"][l], V[:, PROMPT_SLOT, :]).then_inc(sem("a_cache_stored"), 16)
                                sp.wait_ge(sem("a_ctx_v_loaded"), 16)
                                sp.wait_ge(sem("a_cache_stored"), 32)

                            @block.tensor
                            def _(pe):
                                for c, (o, n) in enumerate(cuts):
                                    pe.wait_ge(sem(f"a_w_loaded{c}"), 16)
                                    for t in range(NT):
                                        j = c * NT + t
                                        if j >= 4:
                                            pe.wait_ge(sem("a_projected_copied"), j - 3)
                                        for k in range(KD):
                                            mm = pe.matmul(ps[:, j % 4, 0:n], hT[:, k, t * P:(t + 1) * P], ring[:, c, k, 0:n],
                                                           start=(k == 0), stop=(k == KD - 1))
                                        mm.then_inc(sem("a_projected"), 1)
                                pe.wait_ge(sem("a_ctx_k_loaded"), 16)
                                pe.transpose(ps[:, 6, 0:P], ctx_k[:, :], ident[:, :]).then_inc(sem("a_ctx_turned"), 1)
                                for t in range(NT):
                                    pe.wait_ge(sem("a_rotated"), t + 1)
                                    if t >= 2:
                                        pe.wait_ge(sem("a_qk_copied"), t - 1)
                                    for m in range(4):
                                        mm = pe.transpose(ps[:, 4 + t % 2, m * P:(m + 1) * P], zr[:, t % 2, m * P:(m + 1) * P], ident[:, :])
                                    mm.then_inc(sem("a_qk_turned"), 1)

                            @block.scalar
                            def _(act):
                                for j in range(2 * NT):
                                    t = j % NT
                                    act.wait_ge(sem("a_projected"), j + 1)
                                    if j < NT:
                                        act.copy(Z[:, t, 0:384], ps[:, j % 4, 0:384]).then_inc(sem("a_projected_copied"), 1)
                                    else:
                                        act.copy(Z[:, t, 384:512], ps[:, j % 4, 0:P]).then_inc(sem("a_k_copied"), 1)
                                        act.copy(V[:, key_slot(t), :], ps[:, j % 4, P:2 * P]).then_inc(sem("a_v_copied"), 1)
                                        act.wait_ge(sem("a_v_copied"), t + 1)
                                        act.wait_ge(sem("a_k_copied"), t + 1)
                                        act.sem_inc(sem("a_projected_copied"), 1)
                                act.wait_ge(sem("a_ctx_turned"), 1)
                                act.copy(QK[:, 3, CTX_SLOT * P:(CTX_SLOT + 1) * P], ps[:, 6, 0:P])
                                for t in range(NT):
                                    act.wait_ge(sem("a_qk_turned"), t + 1)
                                    act.copy(QK[:, :, key_slot(t) * P:(key_slot(t) + 1) * P],
                                             ps[:, 4 + t % 2, :].rearrange("p (m n) -> p m n", m=4)).then_inc(sem("a_qk_copied"), 1)

                            @block.gpsimd
                            def _(pool):
                                for t in range(NT + 1):
                                    if t < NT:
                                        pool.wait_ge(sem("a_k_copied"), t + 1)
                                        if t >= 2:
                                            pool.wait_ge(sem("a_squares_summed"), t - 1)
                                        pool.tensor_tensor(sq[:, t % 2, :], Z[:, t, :], Z[:, t, :], ALU.mult).then_inc(sem("a_squared"), 1)
                                    if t >= 1:
                                        u = t - 1
                                        pool.wait_ge(sem("a_squares_summed"), t)
                                        pool_step(pool.tensor_scalar(rs[:, u, :], ss[:, u, :], 1.0 / HD, EPS, ALU.mult, ALU.add))
                                        pool.tensor_tensor(rs[:, u, :], rs[:, u, :], minus_half[:, 0:8], ALU.pow).then_inc(sem("a_rstd"), 1)

                            @block.vector
                            def _(dve):
                                dve.wait_ge(sem("a_g_loaded"), 8 * 16)
                                dve.wait_ge(sem("a_rotary_loaded"), 32)
                                dve_step(dve.tensor_scalar(g[:, 0:6, :], g[:, 0:6, :], SCALE, None, ALU.mult))

                                def norm_and_rotate(t):
                                    z = Z[:, t, :].rearrange("p (h d) -> p h d", d=HD)
                                    dve.wait_ge(sem("a_rstd"), t + 1)
                                    dve_step(dve.tensor_tensor(z, z, rs[:, t, :].unsqueeze(2).to_broadcast([P, 8, HD]), ALU.mult))
                                    dve.tensor_tensor(z, z, g[:, :, :], ALU.mult).then_inc(sem("a_normed"), 1)
                                    dve.wait_ge(sem("a_normed"), t + 1)
                                    if t >= 2:
                                        dve.wait_ge(sem("a_qk_turned"), t - 1)
                                    outq = zr[:, t % 2, 0:384].rearrange("p (g n d) -> p n g d", n=2, d=HD)
                                    outk = zr[:, t % 2, 384:512]
                                    if t == PROMPT:
                                        dve_step(dve.tensor_copy(outq, Z[:, t, 0:384].rearrange("p (n g d) -> p n g d", n=2, d=HD)))
                                        dve.tensor_copy(outk, Z[:, t, 384:512]).then_inc(sem("a_rotated"), 1)
                                        return
                                    a = r1[:, t % 2, :].rearrange("p (h d) -> p h d", d=HD)
                                    dve_step(dve.tensor_tensor(a, z, cos[:, t:t + 1, :].to_broadcast([P, 8, HD]), ALU.mult))
                                    q16 = HD // 4
                                    for part in range(2):
                                        src = Z[:, t, :].rearrange("p (h f s d) -> p h f s d", f=2, s=2, d=q16)[:, :, :, 1 - part, :]
                                        dst = r2[:, :].rearrange("p (h f s d) -> p h f s d", f=2, s=2, d=q16)[:, :, :, part, :]
                                        tab = sin[:, t:t + 1, :].rearrange("p a (f s d) -> p a f s d", f=2, s=2)[:, :, :, part, :]
                                        dve_step(dve.tensor_tensor(dst, src, tab.to_broadcast([P, 8, 2, q16]), ALU.mult))
                                    dve_step(dve.tensor_tensor(outq, r1[:, t % 2, 0:384].rearrange("p (n g d) -> p n g d", n=2, d=HD),
                                                               r2[:, 0:384].rearrange("p (n g d) -> p n g d", n=2, d=HD), ALU.add))
                                    dve.tensor_tensor(outk, r1[:, t % 2, 384:512], r2[:, 384:512], ALU.add).then_inc(sem("a_rotated"), 1)

                                for t in range(NT + 1):
                                    if t < NT:
                                        dve.wait_ge(sem("a_squared"), t + 1)
                                        dve.tensor_reduce(ss[:, t, :], sq[:, t % 2, :].rearrange("p (h d) -> p h d", d=HD),
                                                          AX.X, ALU.add).then_inc(sem("a_squares_summed"), 1)
                                    if t >= 1:
                                        norm_and_rotate(t - 1)

                    units = []
                    for t in [PROMPT] + list(range(LAT)):
                        s = key_slot(t)
                        for h in range(6):
                            n = h // 3
                            rows = slice(n * HD, (n + 1) * HD)
                            if t == PROMPT:
                                keys, vs, nk = [(QK[rows, 3, s * P:(s + 1) * P], 0)], [s], P
                            else:
                                keys = [(QK[rows, 3, 0:512], 0), (QK[rows, 3, 512:1024], 512), (QK[rows, 3, 1024:1152], 1024)]
                                vs, nk = list(range(9)), 9 * P
                            units.append({"q": QK[rows, h % 3, s * P:(s + 1) * P], "keys": keys, "n": nk,
                                          "v": [V[:, x, :] for x in vs], "cols": rows, "bias": None,
                                          "out": mix[:, t, h * HD:(h + 1) * HD]})
                    tensor, scalar, vector, _, _, _ = attention("attn_a", units, own, 0)
                    with nc.Block() as block:
                        block.tensor(tensor)
                        block.scalar(scalar)
                        block.vector(vector)

            def mixer_c(pair):
                tag = f"c{pair}"
                with ExitStack() as own:
                    QK = sb(f"{tag}_qkT", [P, 2, NSLOT * P], own)
                    V = sb(f"{tag}_v", [P, NSLOT, P], own)
                    ctx_k = sb(f"{tag}_ctx_k", [P, P], own)
                    k_nat = sb(f"{tag}_k_prompt", [P, P], own)
                    T = sb(f"{tag}_bias", [P, 2, BIAS_U * GRID_W], own)
                    window = sb(f"{tag}_window", [P, WIN_TYPES, WIN], own)
                    slot = pair % 2
                    with nc.Block() as block:
                        @block.sync
                        def _(sp):
                            for m in range(3):
                                o = OFF_C + m * 384 + pair * P
                                sp.dma_start(ring[:, slot, :, m * P:(m + 1) * P], w_in[:, :, o:o + P]).then_inc(sem(f"{tag}_w_loaded"), 16)
                            sp.dma_start(ctx_k[:, :], I["cache_k_nbhd"][l, :, pair * P:(pair + 1) * P]).then_inc(sem(f"{tag}_ctx_k_loaded"), 16)
                            sp.dma_start(V[:, CTX_SLOT, :], I["cache_v_nbhd"][l, :, pair * P:(pair + 1) * P]).then_inc(sem(f"{tag}_tables_loaded"), 16)
                            sp.dma_start(window[:, :, :], I["window"].rearrange("p (w n) -> p w n", w=WIN_TYPES)).then_inc(sem(f"{tag}_tables_loaded"), 16)
                            sp.wait_ge(bias_copied, 6 * DEPTH * 16)
                            for j in range(2):
                                by_column = bias_dram[l, 2 * pair + j, GRID_W - 1:GRID_W - 1 + GRID_W * (bias_pitch - 1)].rearrange("(c j) -> c j", c=GRID_W)
                                for r in range(2):
                                    rows = by_column[:, (1 - r) * BIAS_W:(1 - r + BIAS_U) * BIAS_W].rearrange("c (u k) -> c u k", k=BIAS_W)
                                    sp.dma_start(T[r * HD:(r + 1) * HD, j, :].rearrange("p (u k) -> p u k", k=GRID_W),
                                                 rows[:, :, 0:GRID_W]).then_inc(sem(f"{tag}_tables_loaded"), 16)
                            sp.wait_ge(sem(f"{tag}_v_copied"), NT)
                            sp.dma_start(O["new_v_nbhd"][l, :, pair * P:(pair + 1) * P], V[:, PROMPT_SLOT, :]).then_inc(sem(f"{tag}_cache_stored"), 16)
                            sp.wait_ge(sem(f"{tag}_k_prompt_copied"), 1)
                            sp.dma_start(O["new_k_nbhd"][l, :, pair * P:(pair + 1) * P], k_nat[:, :]).then_inc(sem(f"{tag}_cache_stored"), 16)
                            sp.wait_ge(sem(f"{tag}_tables_loaded"), 6 * 16)
                            sp.wait_ge(sem(f"{tag}_cache_stored"), 32)

                        @block.tensor
                        def _(pe):
                            pe.wait_ge(sem(f"{tag}_w_loaded"), 48)
                            for j in range(6):
                                m, n = j // 3, j % 3
                                if j >= 3:
                                    pe.wait_ge(sem(f"{tag}_qk_copied"), j - 2)
                                for k in range(KD):
                                    mm = pe.matmul(ps[:, j % 3, 0:384], ring[:, slot, k, m * P:(m + 1) * P], hT[:, k, n * 384:(n + 1) * 384],
                                                   start=(k == 0), stop=(k == KD - 1))
                                mm.then_inc(sem(f"{tag}_qk_projected"), 1)
                            for t in range(NT):
                                if t >= 3:
                                    pe.wait_ge(sem(f"{tag}_v_copied"), t - 2)
                                for k in range(KD):
                                    mm = pe.matmul(ps[:, 3 + t % 3, 0:P], hT[:, k, t * P:(t + 1) * P], ring[:, slot, k, 2 * P:3 * P],
                                                   start=(k == 0), stop=(k == KD - 1))
                                mm.then_inc(sem(f"{tag}_v_projected"), 1)
                            pe.wait_ge(sem(f"{tag}_ctx_k_loaded"), 16)
                            pe.transpose(ps[:, 6, 0:P], ctx_k[:, :], ident[:, :]).then_inc(sem(f"{tag}_ctx_turned"), 1)
                            pe.wait_ge(sem(f"{tag}_qk_copied"), 6)
                            pe.transpose(ps[:, 7, 0:P], QK[:, 1, PROMPT_SLOT * P:NSLOT * P], ident[:, :]).then_inc(sem(f"{tag}_k_prompt_turned"), 1)

                        @block.scalar
                        def _(act):
                            for j in range(6):
                                m, n = j // 3, j % 3
                                act.wait_ge(sem(f"{tag}_qk_projected"), j + 1)
                                s = SCALE if m == 0 else 1.0
                                if n < 2:
                                    act.mul(QK[:, m, n * 384:(n + 1) * 384], ps[:, j % 3, 0:384], s).then_inc(sem(f"{tag}_qk_copied"), 1)
                                else:
                                    act_step(act.mul(QK[:, m, 768:1024], ps[:, j % 3, 0:256], s))
                                    act.mul(QK[:, m, PROMPT_SLOT * P:NSLOT * P], ps[:, j % 3, 256:384], s).then_inc(sem(f"{tag}_qk_copied"), 1)
                            act.wait_ge(sem(f"{tag}_ctx_turned"), 1)
                            act.copy(QK[:, 1, CTX_SLOT * P:(CTX_SLOT + 1) * P], ps[:, 6, 0:P])
                            act.wait_ge(sem(f"{tag}_k_prompt_turned"), 1)
                            act.copy(k_nat[:, :], ps[:, 7, 0:P]).then_inc(sem(f"{tag}_k_prompt_copied"), 1)

                        @block.vector
                        def _(dve):
                            for t in range(NT):
                                dve.wait_ge(sem(f"{tag}_v_projected"), t + 1)
                                dve.tensor_copy(V[:, key_slot(t), :], ps[:, 3 + t % 3, 0:P]).then_inc(sem(f"{tag}_v_copied"), 1)

                    units = []
                    for t in [PROMPT] + list(range(LAT)):
                        s = key_slot(t)
                        for j in range(2):
                            rows = slice(j * HD, (j + 1) * HD)
                            w0 = window_start_row(t) * GRID_W if t != PROMPT else 0
                            if t == PROMPT:
                                keys, vs, nk = [(QK[rows, 1, s * P:(s + 1) * P], 0)], [s], P
                            else:
                                keys = [(QK[rows, 1, w0:w0 + 512], 0), (QK[rows, 1, w0 + 512:w0 + WIN], 512),
                                        (QK[rows, 1, CTX_SLOT * P:(CTX_SLOT + 1) * P], WIN)]
                                vs, nk = [w0 // P + x for x in range(WIN // P)] + [CTX_SLOT], WIN + P
                            units.append({"q": QK[rows, 0, s * P:(s + 1) * P], "keys": keys, "n": nk,
                                          "v": [V[:, x, :] for x in vs], "cols": rows,
                                          "bias": None if t == PROMPT else (t, j),
                                          "out": mix[:, t, 640 + (2 * pair + j) * HD:640 + (2 * pair + j + 1) * HD]})
                    tensor, scalar, vector, biased, bias_ready, max_ready = attention(f"attn_{tag}", units, own, WIN + P)
                    with nc.Block() as block:
                        block.tensor(tensor)
                        block.scalar(scalar)
                        block.vector(vector)

                        @block.gpsimd
                        def _(pool):
                            pool_step(pool.memset(biased[:, :, WIN:WIN + P], 0.0))
                            for i, u in enumerate(units):
                                if u["bias"] is None:
                                    continue
                                t, j = u["bias"]
                                if u["bias_n"] > 2:
                                    pool.wait_ge(max_ready, i - 1)
                                u0 = window_start_row(t) - 2 * t + NA_ROWS
                                pool.tensor_tensor(biased[:, u["bias_n"] % 2, 0:WIN], T[:, j, u0 * GRID_W:u0 * GRID_W + WIN],
                                                   window[:, window_type(t), :], ALU.add).then_inc(bias_ready, 1)

            def mixer_b():
                with ExitStack() as own:
                    qT = sb("b_qT", [P, 2, TOK], own)
                    kT = sb("b_kT", [P, 2, TOK], own)
                    K = sb("b_k", [P, NT, 256], own)
                    OG = sb("b_og", [P, NT, 272], own)
                    V = sb("b_v", [P, NT, 4, VA], own)
                    HB = sb("b_h_backward", [P, NT, 256], own)
                    cols = sb("b_columns", [P, 4, 2, NT, 4], own)
                    decay = sb("b_decay", [P, 2, 2, NT], own)
                    state = sb("b_state", [P, 2, 2, 2 * VA], own)
                    state_p = sb("b_state_prompt", [P, 2, 2, 2 * VA], own)
                    gn = sb("b_out_norm", [P, 256], own)
                    cuts = ((OFF_B, 256), (OFF_B + 256, 256), (OFF_B + 512, 256), (OFF_B + 768, 272))
                    gbias = small[:, 96:112]

                    with nc.Block() as block:
                        @block.sync
                        def _(sp):
                            for c, (o, n) in enumerate(cuts):
                                if c >= 2:
                                    sp.wait_ge(sem("b_w_used"), c - 1)
                                sp.dma_start(ring[:, c % 2, :, 0:n], w_in[:, :, o:o + n]).then_inc(sem(f"b_w_loaded{c % 2}"), 16)
                            sp.dma_start(gbias, I["gate_bias"][bass.ds(l, 1), :].to_broadcast([P, 16])).then_inc(sem("b_rows_loaded"), 16)
                            sp.dma_start(gn[:, :], I["out_norm"][bass.ds(l, 1), :].to_broadcast([P, 256])).then_inc(sem("b_rows_loaded"), 16)
                            sp.wait_ge(sem("b_state_cleared"), 1)
                            for d in range(2):
                                for h in range(4):
                                    pr, j = h // 2, h % 2
                                    rows = slice(j * HD, (j + 1) * HD)
                                    sp.dma_start(state[rows, d, pr, j * VA:j * VA + HD], I["state_C"][l, d, h]).then_inc(sem("b_state_loaded"), 16)
                                    sp.dma_start(state[rows, d, pr, j * VA + HD:(j + 1) * VA], I["state_n"][l, d, h]).then_inc(sem("b_state_loaded"), 16)
                            sp.wait_ge(sem("b_rows_loaded"), 32)
                            sp.wait_ge(sem("b_state_loaded"), 16 * 16)

                        @block.gpsimd
                        def _(pool):
                            pool_step(pool.memset(state[:, :, :, :], 0.0))
                            pool.sem_inc(sem("b_state_cleared"), 1)
                            pool.memset(state_p[:, :, :, :], 0.0)
                            pool.memset(V[:, :, :, HD:VA], 1.0)

                        @block.tensor
                        def _(pe):
                            pe.wait_ge(sem("b_w_loaded0"), 16)
                            for j in range(6):
                                m, n = j // 3, j % 3
                                if j >= 4:
                                    pe.wait_ge(sem("b_copied"), j - 3)
                                for k in range(KD):
                                    mm = pe.matmul(ps[:, j % 4, 0:384], ring[:, 0, k, m * P:(m + 1) * P], hT[:, k, n * 384:(n + 1) * 384],
                                                   start=(k == 0), stop=(k == KD - 1))
                                mm.then_inc(sem("b_projected"), 1)
                            mm = None
                            pe.wait_ge(sem("b_projected"), 6)
                            pe.sem_inc(sem("b_w_used"), 1)
                            for c in range(1, 4):
                                pe.wait_ge(sem(f"b_w_loaded{c % 2}"), 16 * (c // 2 + 1))
                                n = cuts[c][1]
                                for t in range(NT):
                                    j = 6 + (c - 1) * NT + t
                                    pe.wait_ge(sem("b_copied"), j - 3)
                                    for k in range(KD):
                                        mm = pe.matmul(ps[:, j % 4, 0:n], hT[:, k, t * P:(t + 1) * P], ring[:, c % 2, k, 0:n],
                                                       start=(k == 0), stop=(k == KD - 1))
                                    mm.then_inc(sem("b_projected"), 1)
                                pe.wait_ge(sem("b_projected"), 6 + c * NT)
                                pe.sem_inc(sem("b_w_used"), 1)
                            for t in range(NT):
                                if t >= 2:
                                    pe.wait_ge(sem("b_kT_copied"), t - 1)
                                for m in range(2):
                                    mm = pe.transpose(ps[:, 4 + t % 2, m * P:(m + 1) * P], K[:, t, m * P:(m + 1) * P], ident[:, :])
                                mm.then_inc(sem("b_k_turned"), 1)

                        @block.scalar
                        def _(act):
                            for j in range(6 + 3 * NT):
                                act.wait_ge(sem("b_projected"), j + 1)
                                if j < 6:
                                    m, n = j // 3, j % 3
                                    a = act.copy(qT[:, m, n * 384:(n + 1) * 384], ps[:, j % 4, 0:384])
                                else:
                                    c, t = (j - 6) // NT + 1, (j - 6) % NT
                                    if c == 1:
                                        a = act.mul(K[:, t, :], ps[:, j % 4, 0:256], SCALE)
                                    elif c == 2:
                                        a = act.copy(V[:, t, :, 0:HD], ps[:, j % 4, 0:256].rearrange("p (h d) -> p h d", d=HD))
                                    else:
                                        a = act.copy(OG[:, t, :], ps[:, j % 4, 0:272])
                                a.then_inc(sem("b_copied"), 1)

                        @block.vector
                        def _(dve):
                            for t in range(NT):
                                dve.wait_ge(sem("b_k_turned"), t + 1)
                                dve.tensor_copy(kT[:, :, t * P:(t + 1) * P], ps[:, 4 + t % 2, 0:256].rearrange("p (m n) -> p m n", m=2)
                                                ).then_inc(sem("b_kT_copied"), 1)

                    hflat = hT[:, :, :].rearrange("p k t -> p (k t)")

                    def rows_of(i):
                        return hflat[0:36, i * TOK:(i + 1) * TOK]
                    B_, A_, M_, WI, AE, FA, FM = (rows_of(i) for i in range(7))
                    LF = B_
                    small_rows = hflat[0:36, 7 * TOK:7 * TOK + 64]
                    m_in = small_rows[:, 0:NT]
                    m_out = small_rows[:, 16:16 + NT]
                    dec = small_rows[:, 32:32 + NT]
                    dec_diag = hflat[0:36, 7 * TOK + 64:7 * TOK + 64 + 4 * NT]
                    gI = hflat[:, 7 * TOK + 128:7 * TOK + 128 + 9 * 36].rearrange("p (t c) -> p t c", c=36)
                    gF = hflat[:, 7 * TOK + 128 + 9 * 36:7 * TOK + 128 + 18 * 36].rearrange("p (t c) -> p t c", c=36)
                    with ExitStack() as inner:
                        raw = sb("b_gates", [P, NT, 16], inner)
                        e1 = sb("b_gate_e", [P, NT, 8], inner)
                        FW = sb("b_rows_wi", [36, TOK], inner)
                        with nc.Block() as block:
                            @block.sync
                            def _(sp):
                                sp.wait_ge(sem("b_m_cleared"), 1)
                                for d in range(2):
                                    sp.dma_start(m_in[32 * d:32 * d + 4, 0:1], I["state_m"][l, d]).then_inc(sem("b_m0_loaded"), 16)
                                sp.wait_ge(sem("b_m0_loaded"), 32)
                                sp.wait_ge(sem("b_stabiliser_done"), 1)
                                for d in range(2):
                                    sp.dma_start(O["new_m"][l, d], m_out[32 * d:32 * d + 4, PROMPT:NT]).then_inc(sem("b_m_stored"), 16)
                                sp.wait_ge(sem("b_m_stored"), 32)

                            @block.gpsimd
                            def _(pool):
                                pool_step(pool.memset(hflat[:, 0:8 * TOK], 0.0))
                                pool.sem_inc(sem("b_m_cleared"), 1)
                                pool.sem_inc(sem("b_rows_cleared"), 1)

                            @block.scalar
                            def _(act):
                                act.wait_ge(sem("b_gate_abs"), 1)
                                act_step(act.activation(e1[:, :, :], e1[:, :, :], ACT.Exp, scale=-1.0))
                                act.activation(e1[:, :, :], e1[:, :, :], ACT.Ln, bias=1.0).then_inc(sem("b_gate_ln"), 1)
                                act.wait_ge(sem("b_arguments"), 1)
                                act_step(act.activation(WI, WI, ACT.Exp))
                                act_step(act.activation(AE, AE, ACT.Exp))
                                act_step(act.activation(B_, B_, ACT.Exp))
                                act_step(act.activation(dec, dec, ACT.Exp))
                                act.sem_inc(sem("b_exponentials"), 1)

                            @block.vector
                            def _(dve):
                                dve.wait_ge(sem("b_rows_cleared"), 1)
                                dve_step(dve.tensor_tensor(raw[:, :, :], OG[:, :, 256:272], gbias.unsqueeze(1).to_broadcast([P, NT, 16]), ALU.add))
                                r4 = raw[:, :, :].rearrange("p t (d g h) -> p t d g h", d=2, g=2)
                                e4 = e1[:, :, :].rearrange("p t (d h) -> p t d h", d=2)
                                dve_step(dve.scalar_tensor_tensor(e4, r4[:, :, :, 1, :], -1.0, r4[:, :, :, 1, :], ALU.mult, ALU.max))
                                dve.sem_inc(sem("b_gate_abs"), 1)
                                dve.wait_ge(sem("b_gate_ln"), 1)
                                for d in range(2):
                                    dve_step(dve.tensor_copy(gI[:, :, 32 * d:32 * d + 4], r4[:, :, d, 0, :]))
                                    dve_step(dve.scalar_tensor_tensor(gF[:, :, 32 * d:32 * d + 4], r4[:, :, d, 1, :], 0.0, e4[:, :, d, :],
                                                                      ALU.min, ALU.subtract))
                                dve.sem_inc(sem("b_gates_ready"), 1)
                                dve.wait_ge(sem("b_gates_turned"), 1)
                                for b, dst in ((0, A_), (3, LF)):
                                    src = psf[0:36, b * 512:b * 512 + TOK]
                                    dve_step(dve.tensor_copy(dst[0:4, :], src[0:4, :]))
                                    for a, z in ((0, LAT * P), (LAT * P, TOK)):
                                        dve_step(dve.tensor_copy(dst[32:36, a:z], src[32:36, a:z][:, ::-1]))
                                dve.wait_ge(sem("b_m0_loaded"), 32)
                                for c in range(NT):
                                    s = slice(c * P, (c + 1) * P)
                                    last = slice((c + 1) * P - 1, (c + 1) * P)
                                    dve_step(dve.tensor_tensor_scan(B_[:, s], LF[:, s], zeros[:, :], 0.0, ALU.add, ALU.add))
                                    dve_step(dve.tensor_tensor(A_[:, s], A_[:, s], B_[:, s], ALU.subtract))
                                    dve_step(dve.tensor_tensor_scan(M_[:, s], A_[:, s], A_[:, s], m_in[:, c:c + 1], ALU.max, ALU.max))
                                    dve_step(dve.tensor_tensor(m_out[:, c:c + 1], B_[:, last], M_[:, last], ALU.add))
                                    if c < LAT - 1:
                                        dve_step(dve.tensor_copy(m_in[:, c + 1:c + 2], m_out[:, c:c + 1]))
                                dve.sem_inc(sem("b_stabiliser_done"), 1)
                                M3, A3, W3, E3 = (x.rearrange("p (t n) -> p t n", n=P) for x in (M_, A_, WI, AE))
                                mlast = M3[:, :, P - 1]
                                dve_step(dve.tensor_tensor(W3, m_in.unsqueeze(2).to_broadcast([36, NT, P]), M3, ALU.subtract))
                                dve_step(dve.tensor_tensor(E3, A3, mlast.unsqueeze(2).to_broadcast([36, NT, P]), ALU.subtract))
                                dve_step(dve.scalar_tensor_tensor(B_, B_, -1.0, M_, ALU.mult, ALU.subtract))
                                dve_step(dve.tensor_tensor(dec, m_in, mlast, ALU.subtract))
                                dve.sem_inc(sem("b_arguments"), 1)

                                def in_token_order(dst, src):
                                    dve_step(dve.tensor_copy(dst[0:4, :], src[0:4, :]))
                                    for a, z in ((0, LAT * P), (LAT * P, TOK)):
                                        dve_step(dve.tensor_copy(dst[32:36, a:z], src[32:36, a:z][:, ::-1]))
                                in_token_order(FA, A_)
                                in_token_order(FM, M_)
                                dve.wait_ge(sem("b_exponentials"), 1)
                                in_token_order(FW[:, :], WI)
                                in_token_order(A_, AE)
                                in_token_order(M_, B_)
                                dve_step(dve.tensor_tensor(dec_diag.rearrange("p (j c) -> p j c", j=4), diagonal[:, :, :],
                                                           dec.unsqueeze(1).to_broadcast([36, 4, NT]), ALU.mult))
                                dve.sem_inc(sem("b_rows_ready"), 1)
                                dve.wait_ge(sem("b_columns_turned"), 1)
                                for q in range(4):
                                    for d in range(2):
                                        dve.tensor_copy(cols[:, q, d, :, :],
                                                        ps[:, q // 2 * 2 + d, q % 2 * 64:q % 2 * 64 + 4 * NT].rearrange("p (t h) -> p t h", t=NT))
                                for d in range(2):
                                    src = ps[:, 4 + d, 0:4 * NT].rearrange("p (j c) -> p j c", j=4)
                                    for j in range(2):
                                        rows = slice(j * HD, (j + 1) * HD)
                                        dve.tensor_copy(decay[rows, d, :, :], src[rows, j:4:2, :])

                            @block.tensor
                            def _(pe):
                                pe.wait_ge(sem("b_gates_ready"), 1)
                                for b, g_ in ((0, gI), (3, gF)):
                                    for t in range(NT):
                                        mm = pe.transpose(psf[0:36, b * 512 + t * P:b * 512 + (t + 1) * P], g_[:, t, :], ident[:, :])
                                mm.then_inc(sem("b_gates_turned"), 1)
                                pe.wait_ge(sem("b_rows_ready"), 1)
                                for q, src in enumerate((FA, FW[:, :], M_, A_)):
                                    for t in range(NT):
                                        for d in range(2):
                                            o = q % 2 * 64 + t * 4
                                            r = slice(32 * d, 32 * d + 4)
                                            pe.transpose(ps[:, q // 2 * 2 + d, o:o + 4], src[r, t * P:(t + 1) * P], ident[r, r])
                                for d in range(2):
                                    r = slice(32 * d, 32 * d + 4)
                                    mm = pe.matmul(ps[:, 4 + d, 0:4 * NT], ones[r, :], dec_diag[r, :], start=True, stop=True)
                                mm.then_inc(sem("b_columns_turned"), 1)

                    E4 = sb("b_e", [P, 2, 512], own)
                    W4 = sb("b_w", [P, 2, 512], own)
                    J4 = sb("b_inter", [P, 4 * VA], own)
                    N4 = sb("b_num", [P, 4 * VA], own)
                    KS = sb("b_ks", [P, 256], own)
                    U4 = sb("b_update", [P, 4 * VA], own)
                    dn = small[:, 112:116]
                    rdn = small[:, 116:120]
                    work = []
                    for c in range(LAT):
                        work += [(0, c, c), (1, LAT - 1 - c, c)]
                    work += [(0, PROMPT, PROMPT), (1, PROMPT, PROMPT)]
                    qA, qWI, qEM, qAE = range(4)

                    def place(h):
                        return (h % 2 * 2 + h // 2) * P
                    with nc.Block() as block:
                        @block.tensor
                        def _(pe):
                            def scores(i):
                                d, t, c = work[i]
                                if i >= 2:
                                    pe.wait_ge(sem("b_weighted"), i - 1)
                                tt = slice(t * P, (t + 1) * P)
                                for h in range(4):
                                    r = slice(h % 2 * HD, (h % 2 + 1) * HD)
                                    pe.matmul(ps[:, i % 2 * 2 + h % 2, h // 2 * P:(h // 2 + 1) * P], kT[r, h // 2, tt], qT[r, h // 2, tt], start=True, stop=True)
                                r = slice(32 * d, 32 * d + 4)
                                if i >= 1:
                                    pe.wait_ge(sem("b_masked"), i)
                                for h in range(4):
                                    mm = pe.matmul(ps[:, 4, place(h):place(h) + P], neg_select[r, h, :], FM[r, tt], start=True, stop=True)
                                mm.then_inc(sem("b_scores"), 1)

                            def apply(i):
                                d, t, c = work[i]
                                st = state_p if t == PROMPT else state
                                tt = slice(t * P, (t + 1) * P)
                                if i >= 1:
                                    pe.wait_ge(sem("b_combined"), i)
                                if i >= 2 and t != PROMPT:
                                    pe.wait_ge(sem("b_state_new"), i - 1)
                                for pr in range(2):
                                    pe.matmul(ps[:, 6, pr * 2 * VA:(pr + 1) * 2 * VA], qT[:, pr, tt], st[:, d, pr, :], start=True, stop=True)
                                pe.wait_ge(sem("b_weighted"), i + 1)
                                for h in range(4):
                                    mm = pe.matmul(ps[:, 5, h * VA:(h + 1) * VA], W4[:, i % 2, place(h):place(h) + P], V[:, t, h, :], start=True, stop=True)
                                mm.then_inc(sem("b_applied"), 1)
                                pe.wait_ge(sem("b_keys_scaled"), i + 1)
                                if i >= 1:
                                    pe.wait_ge(sem("b_update_read"), i)
                                for pr in range(2):
                                    mm = pe.matmul(ps[:, 7, pr * 2 * VA:(pr + 1) * 2 * VA], KS[:, pr * P:(pr + 1) * P],
                                                   V[:, t, 2 * pr:2 * pr + 2, :].rearrange("p h d -> p (h d)"), start=True, stop=True)
                                mm.then_inc(sem("b_updated"), 1)
                            scores(0)
                            for i in range(len(work)):
                                if i + 1 < len(work):
                                    scores(i + 1)
                                apply(i)

                        @block.scalar
                        def _(act):
                            for i, (d, t, c) in enumerate(work):
                                act.wait_ge(sem("b_masked"), i + 1)
                                for h in range(4):
                                    a = act.activation(E4[:, i % 2, place(h):place(h) + P], E4[:, i % 2, place(h):place(h) + P], ACT.Exp,
                                                       bias=cols[:, qA, d, t, h:h + 1])
                                a.then_inc(sem("b_exp"), 1)

                        @block.gpsimd
                        def _(pool):
                            for i, (d, t, c) in enumerate(work):
                                if i >= 1:
                                    pool.wait_ge(sem("b_updated"), i)
                                pool.tensor_tensor(KS[:, :].rearrange("p (h d) -> p h d", d=HD), K[:, t, :].rearrange("p (h d) -> p h d", d=HD),
                                                   cols[:, qAE, d, t, :].unsqueeze(2).to_broadcast([P, 4, HD]), ALU.mult).then_inc(sem("b_keys_scaled"), 1)

                        @block.vector
                        def _(dve):
                            def mask(i):
                                d, t, c = work[i]
                                dve.wait_ge(sem("b_scores"), i + 1)
                                if i >= 2:
                                    dve.wait_ge(sem("b_weighted"), i - 1)
                                dve.tensor_tensor(E4[:, i % 2, :].rearrange("p (h t) -> p h t", h=4), ps[:, 4, :].rearrange("p (h t) -> p h t", h=4),
                                                  causal[:, d:d + 1, :].to_broadcast([P, 4, P]), ALU.add).then_inc(sem("b_masked"), 1)

                            mask(0)
                            for i, (d, t, c) in enumerate(work):
                                if i + 1 < len(work):
                                    mask(i + 1)
                                dve.wait_ge(sem("b_exp"), i + 1)
                                if i >= 2:
                                    dve.wait_ge(sem("b_applied"), i - 1)
                                dve.tensor_tensor(W4[:, i % 2, :].rearrange("p (j n) -> p j n", j=2), ps[:, i % 2 * 2:i % 2 * 2 + 2, 0:256],
                                                  E4[:, i % 2, :].rearrange("p (j n) -> p j n", j=2), ALU.mult).then_inc(sem("b_weighted"), 1)
                                dve.wait_ge(sem("b_applied"), i + 1)
                                J3 = J4[:, :].rearrange("p (h d) -> p h d", d=VA)
                                N3 = N4[:, :].rearrange("p (h d) -> p h d", d=VA)
                                dve_step(dve.tensor_tensor(J3, ps[:, 6, 0:4 * VA].rearrange("p (h d) -> p h d", d=VA),
                                                           cols[:, qWI, d, t, :].unsqueeze(2).to_broadcast([P, 4, VA]), ALU.mult))
                                dve_step(dve.tensor_tensor(N4[:, :], ps[:, 5, 0:4 * VA], J4[:, :], ALU.add))
                                dve.sem_inc(sem("b_combined"), 1)
                                dve_step(dve.scalar_tensor_tensor(dn, N3[:, :, HD], -1.0, N3[:, :, HD], ALU.mult, ALU.max))
                                dve_step(dve.tensor_tensor(dn, dn, cols[:, qEM, d, t, :], ALU.max))
                                dve_step(dve.reciprocal(rdn, dn))
                                dst = (HB[:, t, :] if d else mix[:, t, 384:640]).rearrange("p (h d) -> p h d", d=HD)
                                dve.tensor_tensor(dst, N3[:, :, 0:HD], rdn.unsqueeze(2).to_broadcast([P, 4, HD]), ALU.mult)
                                dve.wait_ge(sem("b_updated"), i + 1)
                                dve_step(dve.tensor_tensor(U4[:, :], ps[:, 7, 0:4 * VA], blocks[:, :], ALU.mult))
                                dve.sem_inc(sem("b_update_read"), 1)
                                st = state_p if t == PROMPT else state
                                for pr in range(2):
                                    dve_step(dve.scalar_tensor_tensor(st[:, d, pr, :], st[:, d, pr, :], decay[:, d, pr, c:c + 1],
                                                                      U4[:, pr * 2 * VA:(pr + 1) * 2 * VA], ALU.mult, ALU.add))
                                dve.sem_inc(sem("b_state_new"), 1)

                        @block.sync
                        def _(sp):
                            sp.wait_ge(sem("b_state_new"), len(work))
                            for d in range(2):
                                for h in range(4):
                                    pr, j = h // 2, h % 2
                                    rows = slice(j * HD, (j + 1) * HD)
                                    sp.dma_start(O["new_C"][l, d, h], state_p[rows, d, pr, j * VA:j * VA + HD]).then_inc(sem("b_state_stored"), 16)
                                    sp.dma_start(O["new_n"][l, d, h], state_p[rows, d, pr, j * VA + HD:(j + 1) * VA]).then_inc(sem("b_state_stored"), 16)
                            sp.wait_ge(sem("b_state_stored"), 16 * 16)

                    with nc.Block() as block:
                        junk = E4
                        ss = small[:, 120:120 + 4 * NT].rearrange("p (t h) -> p t h", h=4)
                        rs = small[:, 160:160 + 4 * NT].rearrange("p (t h) -> p t h", h=4)

                        @block.scalar
                        def _(act):
                            for t in range(NT):
                                act.activation(OG[:, t, 0:256], OG[:, t, 0:256], ACT.Exp, scale=-1.0).then_inc(sem("b_sigmoid_exp"), 1)

                        @block.gpsimd
                        def _(pool):
                            pool.wait_ge(sem("b_out_summed"), NT)
                            pool_step(pool.tensor_scalar(rs, ss, 1.0 / HD, EPS, ALU.mult, ALU.add))
                            pool_step(pool.tensor_tensor(rs, rs, minus_half[:, 0:4 * NT].rearrange("p (t h) -> p t h", h=4), ALU.pow))
                            pool.sem_inc(sem("b_out_rstd"), 1)

                        @block.vector
                        def _(dve):
                            for t in range(NT):
                                h = mix[:, t, 384:640]
                                dve_step(dve.tensor_tensor(h, h, HB[:, t, :], ALU.add))
                                dve_step(dve.tensor_tensor(junk[:, t % 2, 0:256], h, h, ALU.mult))
                                dve_step(dve.tensor_reduce(ss[:, t, :], junk[:, t % 2, 0:256].rearrange("p (h d) -> p h d", d=HD), AX.X, ALU.add))
                                dve.sem_inc(sem("b_out_summed"), 1)
                                dve.wait_ge(sem("b_sigmoid_exp"), t + 1)
                                o = OG[:, t, 0:256]
                                dve_step(dve.tensor_scalar(o, o, 1.0, None, ALU.add))
                                dve_step(dve.reciprocal(o, o))
                                dve_step(dve.tensor_tensor(o, o, gn[:, :], ALU.mult))
                                dve_step(dve.tensor_tensor(h, h, o, ALU.mult))
                            dve.wait_ge(sem("b_out_rstd"), 1)
                            for t in range(NT):
                                h3 = mix[:, t, 384:640].rearrange("p (h d) -> p h d", d=HD)
                                dve.tensor_tensor(h3, h3, rs[:, t, :].unsqueeze(2).to_broadcast([P, 4, HD]), ALU.mult)

            def out_projection():
                CUT = 256
                NCUT = D // CUT
                w_out = I["w_out"][l].rearrange("(k p) n -> p k n", p=P)
                with ExitStack() as own:
                    raw = sb("w_out_raw", [P, 2, KD, CUT], own)
                    w_hi = sb("w_out_hi", [P, 2, KD, CUT], own, F32R)
                    w_lo = sb("w_out_lo", [P, 2, KD, CUT], own, F32R)
                    with nc.Block() as block:
                        @block.sync
                        def _(sp):
                            for c in range(NCUT):
                                if c >= 2:
                                    sp.wait_ge(sem("o_w_lo"), c - 1)
                                sp.dma_start(raw[:, c % 2, :, :], w_out[:, :, c * CUT:(c + 1) * CUT]).then_inc(sem(f"o_w_loaded{c % 2}"), 16)

                        @block.tensor
                        def _(pe):
                            for t in range(NT):
                                if t >= 2:
                                    pe.wait_ge(sem("o_mix_lo"), t - 1)
                                for k in range(KD):
                                    mm = pe.transpose(psf[:, t % 2 * 1024 + k * P:t % 2 * 1024 + (k + 1) * P], mix[:, t, k * P:(k + 1) * P], ident[:, :])
                                mm.then_inc(sem("o_mix_turned"), 1)
                            for c in range(NCUT):
                                pe.wait_ge(sem("o_w_lo"), c + 1)
                                for t in range(NT):
                                    j = c * NT + t
                                    if c == 0:
                                        pe.wait_ge(sem("o_mix_lo"), t + 1)
                                    if j >= 4:
                                        pe.wait_ge(sem("o_copied"), j - 3)
                                    tt = slice(t * P, (t + 1) * P)
                                    for k in range(KD):
                                        for a, b in ((hi, w_hi), (hi, w_lo), (lo, w_hi)):
                                            mm = pe.matmul(ps[:, 4 + j % 4, 0:CUT], a[:, k, tt], b[:, c % 2, k, :],
                                                           start=(k == 0 and a is hi and b is w_hi), stop=(k == KD - 1 and a is lo))
                                    mm.then_inc(sem("o_projected"), 1)

                        @block.vector
                        def _(dve):
                            def weights(c):
                                dve.wait_ge(sem("o_w_hi"), c + 1)
                                dve.tensor_tensor(w_lo[:, c % 2, :, :], raw[:, c % 2, :, :], w_hi[:, c % 2, :, :].bitcast(F32),
                                                  ALU.subtract).then_inc(sem("o_w_lo"), 1)
                            weights(0)
                            for t in range(NT):
                                tt = slice(t * P, (t + 1) * P)
                                dve.wait_ge(sem("o_mix_hi"), t + 1)
                                dve.tensor_tensor(lo[:, :, tt], psf[:, t % 2 * 1024:t % 2 * 1024 + 1024].rearrange("p (k n) -> p k n", n=P),
                                                  hi[:, :, tt].bitcast(F32), ALU.subtract).then_inc(sem("o_mix_lo"), 1)
                            for c in range(1, NCUT):
                                weights(c)

                        @block.scalar
                        def _(act):
                            def weights(c):
                                act.wait_ge(sem(f"o_w_loaded{c % 2}"), 16 * (c // 2 + 1))
                                if c >= 2:
                                    act.wait_ge(sem("o_projected"), (c - 1) * NT)
                                act.copy(w_hi[:, c % 2, :, :], raw[:, c % 2, :, :]).then_inc(sem("o_w_hi"), 1)
                            weights(0)
                            for t in range(NT):
                                act.wait_ge(sem("o_mix_turned"), t + 1)
                                act.copy(hi[:, :, t * P:(t + 1) * P],
                                         psf[:, t % 2 * 1024:t % 2 * 1024 + 1024].rearrange("p (k n) -> p k n", n=P)).then_inc(sem("o_mix_hi"), 1)
                            weights(1)
                            for j in range(NCUT * NT):
                                c, t = j // NT, j % NT
                                act.wait_ge(sem("o_projected"), j + 1)
                                act.copy(mix[:, t, c * CUT:(c + 1) * CUT], ps[:, 4 + j % 4, 0:CUT]).then_inc(sem("o_copied"), 1)
                                if t == NT - 1 and 1 <= c + 1 and c + 2 < NCUT:
                                    weights(c + 2)

            def mlp():
                NG = D_FF // HID
                KH = HID // P
                UP = 3 * KH
                DOWN = 2 * NT
                w_up = I["w_ffn_up"][l].rearrange("(k p) n -> p k n", p=P)
                w_down = I["w_ffn_down"][l].rearrange("(g k p) n -> g p k n", p=P, k=KH)
                with ExitStack() as own:
                    raw_up = sb("w_up_raw", [P, KD, HID], own)
                    raw_down = sb("w_down_raw", [P, KH, D], own)
                    up_hi, up_lo = (sb(f"w_up_{x}", [P, KD, HID], own, F32R) for x in ("hi", "lo"))
                    down_hi, down_lo = (sb(f"w_down_{x}", [P, KH, D], own, F32R) for x in ("hi", "lo"))
                    u_hi, u_lo = (sb(f"u_{x}", [P, KH, TOK], own, F32R) for x in ("hi", "lo"))
                    relu = sb("relu", [P, 2, 384], own)
                    square = sb("square", [P, 2, 384], own)
                    with nc.Block() as block:
                        @block.sync
                        def _(sp):
                            for g in range(NG):
                                if g >= 1:
                                    sp.wait_ge(sem("m_up_lo"), g)
                                sp.dma_start(raw_up[:, :, :], w_up[:, :, g * HID:(g + 1) * HID]).then_inc(sem("m_up_loaded"), 16)
                                if g >= 1:
                                    sp.wait_ge(sem("m_down_lo"), g)
                                sp.dma_start(raw_down[:, :, :], w_down[g]).then_inc(sem("m_down_loaded"), 16)

                        @block.gpsimd
                        def _(pool):
                            pool.memset(mix[:, :, :], 0.0).then_inc(sem("m_out_cleared"), 1)
                            with pool.Fori(0, NG) as g:
                                pool.wait_ge(sem("m_up_hi"), g + 1)
                                pool.tensor_tensor(up_lo[:, :, :], raw_up[:, :, :], up_hi[:, :, :].bitcast(F32), ALU.subtract).then_inc(sem("m_up_lo"), 1)
                                pool.wait_ge(sem("m_down_hi"), g + 1)
                                pool.tensor_tensor(down_lo[:, :, :], raw_down[:, :, :], down_hi[:, :, :].bitcast(F32), ALU.subtract).then_inc(sem("m_down_lo"), 1)

                        @block.tensor
                        def _(pe):
                            with pe.Fori(0, NG) as g:
                                pe.wait_ge(sem("m_up_lo"), g + 1)
                                for j in range(UP):
                                    n, m = j // KH, j % KH
                                    if j >= 3:
                                        pe.wait_ge(sem("m_relu"), g * UP + j - 2)
                                    for k in range(KD):
                                        for a, b in ((up_hi, hi), (up_hi, lo), (up_lo, hi)):
                                            mm = pe.matmul(ps[:, j % 3, 0:384], a[:, k, m * P:(m + 1) * P], b[:, k, n * 384:(n + 1) * 384],
                                                           start=(k == 0 and a is up_hi and b is hi), stop=(k == KD - 1 and a is up_lo))
                                    mm.then_inc(sem("m_up_done"), 1)
                                pe.wait_ge(sem("m_down_lo"), g + 1)
                                pe.wait_ge(sem("m_added"), g * DOWN)
                                for j in range(DOWN):
                                    t, n = j // 2, j % 2
                                    if j % 6 == 0:
                                        pe.wait_ge(sem("m_u_lo"), g * UP + KH * (t // 3 + 1))
                                    if j >= 5:
                                        pe.wait_ge(sem("m_added"), g * DOWN + j - 4)
                                    for k in range(KH):
                                        for a, b in ((u_hi, down_hi), (u_hi, down_lo), (u_lo, down_hi)):
                                            mm = pe.matmul(ps[:, 3 + j % 5, :], a[:, k, t * P:(t + 1) * P], b[:, k, n * 512:(n + 1) * 512],
                                                           start=(k == 0 and a is u_hi and b is down_hi), stop=(k == KH - 1 and a is u_lo))
                                    mm.then_inc(sem("m_down_done"), 1)

                        @block.scalar
                        def _(act):
                            with act.Fori(0, NG) as g:
                                act.wait_ge(sem("m_up_loaded"), 16 * g + 16)
                                act.wait_ge(sem("m_up_done"), g * UP)
                                act.copy(up_hi[:, :, :], raw_up[:, :, :]).then_inc(sem("m_up_hi"), 1)
                                act.wait_ge(sem("m_down_loaded"), 16 * g + 16)
                                act.wait_ge(sem("m_down_done"), g * DOWN)
                                act.copy(down_hi[:, :, :], raw_down[:, :, :]).then_inc(sem("m_down_hi"), 1)
                                for j in range(UP):
                                    n, m = j // KH, j % KH
                                    act.wait_ge(sem("m_up_done"), g * UP + j + 1)
                                    if j >= 2:
                                        act.wait_ge(sem("m_u_lo"), g * UP + j - 1)
                                    act.activation(relu[:, j % 2, :], ps[:, j % 3, 0:384], ACT.Relu).then_inc(sem("m_relu"), 1)
                                    act.wait_ge(sem("m_relu"), g * UP + j + 1)
                                    act.activation(square[:, j % 2, :], relu[:, j % 2, :], ACT.Square).then_inc(sem("m_square"), 1)
                                    act.wait_ge(sem("m_square"), g * UP + j + 1)
                                    act.copy(u_hi[:, m, n * 384:(n + 1) * 384], square[:, j % 2, :]).then_inc(sem("m_u_hi"), 1)

                        @block.vector
                        def _(dve):
                            dve.wait_ge(sem("m_out_cleared"), 1)
                            with dve.Fori(0, NG) as g:
                                for j in range(UP):
                                    n, m = j // KH, j % KH
                                    dve.wait_ge(sem("m_u_hi"), g * UP + j + 1)
                                    dve.tensor_tensor(u_lo[:, m, n * 384:(n + 1) * 384], square[:, j % 2, :],
                                                      u_hi[:, m, n * 384:(n + 1) * 384].bitcast(F32), ALU.subtract).then_inc(sem("m_u_lo"), 1)
                                for j in range(DOWN):
                                    t, n = j // 2, j % 2
                                    y = mix[:, t, n * 512:(n + 1) * 512]
                                    dve.wait_ge(sem("m_down_done"), g * DOWN + j + 1)
                                    dve.tensor_tensor(y, y, ps[:, 3 + j % 5, :], ALU.add).then_inc(sem("m_added"), 1)

            open_section()
            modulation()
            mixer_memory = ExitStack()
            hT = sb("hT", [P, KD, TOK], mixer_memory)
            residual_norm("pre_mix", None, 0)
            ring = sb("ring", [P, 2, KD, W_C], mixer_memory)
            mixer_a()
            close_section()
            for pair in range(3):
                open_section()
                mixer_c(pair)
                close_section()
            open_section()
            mixer_b()
            close_section()
            mixer_memory.close()
            mlp_memory = ExitStack()
            hi = sb("h_hi", [P, KD, TOK], mlp_memory, F32R)
            lo = sb("h_lo", [P, KD, TOK], mlp_memory, F32R)
            open_section()
            out_projection()
            residual_norm("mix", 0, 1)
            mlp()
            mlp_memory.close()
            residual_norm("mlp", 1, None)
            close_section()

        with nc.Block() as block:
            @block.sync
            def _(sp):
                sp.dma_start(O["y_sample"], x_dram[0:LAT * P, :]).then_inc(sem("outputs_stored"), 16)
                sp.dma_start(O["y_prompt"], x_dram[LAT * P:TOK, :]).then_inc(sem("outputs_stored"), 16)
                sp.wait_ge(sem("outputs_stored"), 32)
        sem_stack.close()


OUTS = (
    ("y_prompt", (P, D), (1, P, D)),
    ("y_sample", (LAT * P, D), (1, LAT * P, D)),
    ("new_k_attn", (DEPTH, P, 2 * HD), (1, DEPTH, P, 2, HD)),
    ("new_v_attn", (DEPTH, P, 2 * HD), (1, DEPTH, P, 2, HD)),
    ("new_k_nbhd", (DEPTH, P, 6 * HD), (1, DEPTH, P, 6, HD)),
    ("new_v_nbhd", (DEPTH, P, 6 * HD), (1, DEPTH, P, 6, HD)),
    ("new_C", (DEPTH, 2, 4, HD, HD), (1, DEPTH, 2, 4, HD, HD)),
    ("new_n", (DEPTH, 2, 4, HD, 1), (1, DEPTH, 2, 4, HD)),
    ("new_m", (DEPTH, 2, 4, 1), (1, DEPTH, 2, 4)),
)


def kernel(**inputs):
    import concourse.bacc as bacc
    from concourse.bass_utils import run_bass_kernel_spmd

    a = {k: np.asarray(v) for k, v in inputs.items()}
    bias_rows = np.zeros((DEPTH, 6, BIAS_DR, BIAS_W), np.float32)
    bias_rows[:, :, 2:17, GRID_W - NA_COLS:GRID_W + NA_COLS - 1] = a["nbhd_rel_bias"]

    def transposed(v):
        v = v.reshape(v.shape[:-1] + (KD, P))
        return np.moveaxis(v, -1, 0)

    laid = {
        "x_sample": a["x_sample"].reshape(LAT * P, D),
        "x_prompt": a["x_prompt"].reshape(P, D),
        "condT": transposed(np.stack([a["c"].reshape(D), a["c_ctx"]])).transpose(0, 2, 1),
        "w_ada": a["w_ada"], "b_ada": a["b_ada"],
        "g_preT": transposed(np.stack([a["g_pre_mix"], a["g_pre_ffn"]], 1)).transpose(1, 0, 2, 3),
        "g_post": np.stack([a["g_post_mix"], a["g_post_ffn"]], 1),
        "w_in": a["w_in"], "w_out": a["w_out"], "w_ffn_up": a["w_ffn_up"], "w_ffn_down": a["w_ffn_down"],
        "q_norm": a["q_norm_attn"], "k_norm": a["k_norm_attn"],
        "gate_bias": a["mlstm_gate_bias"], "out_norm": a["mlstm_out_norm"].reshape(DEPTH, 256),
        "bias_rows": bias_rows.reshape(DEPTH, 6, BIAS_DR * BIAS_W),
        "cache_k_attn": a["cache_k_attn"].reshape(DEPTH, P, 2 * HD),
        "cache_v_attn": a["cache_v_attn"].reshape(DEPTH, P, 2 * HD),
        "cache_k_nbhd": a["cache_k_nbhd"].reshape(DEPTH, P, 6 * HD),
        "cache_v_nbhd": a["cache_v_nbhd"].reshape(DEPTH, P, 6 * HD),
        "state_C": a["state_mlstm_C"].reshape(DEPTH, 2, 4, HD, HD),
        "state_n": a["state_mlstm_n"].reshape(DEPTH, 2, 4, HD, 1),
        "state_m": a["state_mlstm_m"].reshape(DEPTH, 2, 4, 1),
        **shape_constants(),
    }
    laid = {k: np.ascontiguousarray(v) for k, v in laid.items()}
    nc = bacc.Bacc("TRN2", target_bir_lowering=False, num_devices=1)
    ins = {k: nc.dram_tensor(f"in_{k}", v.shape, F32, kind="ExternalInput").ap() for k, v in laid.items()}
    outs = {k: nc.dram_tensor(f"out_{k}", s, F32, kind="ExternalOutput").ap() for k, s, _ in OUTS}
    with nc.allow_non_contiguous_dma(reason="single columns of the mLSTM state"):
        build(nc, ins, outs)
    r = run_bass_kernel_spmd(nc, [{f"in_{k}": v for k, v in laid.items()}], core_ids=[0])
    return tuple(np.asarray(r.results[0][f"out_{k}"]).reshape(full) for k, _, full in OUTS)
```

```python
from contextlib import ExitStack

import concourse.bass as bass
import concourse.mybir as mybir
import numpy as np

ALU = mybir.AluOpType
ACT = mybir.ActivationFunctionType
AX = mybir.AxisListType
F32 = mybir.dt.float32
F32R = mybir.dt.float32r

P = 128
D = 1024
KD = D // P
DEPTH = 2
LAT = 8
NT = LAT + 1
PROMPT = LAT
TOK = NT * P
CTX_SLOT = 8
PROMPT_SLOT = 9
NSLOT = 10
HD = 64
GRID_W = 64
ROWS = 16
NA_ROWS = 8
NA_COLS = 16
EPS = 1e-6
SCALE = HD ** -0.5
NEG = -1e30
LOWEST = -3e38
OFF_A, OFF_B, OFF_C = 0, 640, 1680
W_C = 384
D_FF = 4096
HID = 256
VA = HD + 1
WIN_ROWS = 10
WIN = WIN_ROWS * GRID_W
WIN_TYPES = 5
BIAS_U = 18
BIAS_DR = 20
BIAS_W = 2 * GRID_W - 1


def window_start_row(t):
    return min(max(2 * t - 4, 0), ROWS - WIN_ROWS)


def window_type(t):
    return {0: 0, 1: 1, 6: 3, 7: 4}.get(t, 2)


def key_slot(t):
    return PROMPT_SLOT if t == PROMPT else t


def shape_constants():
    f = np.float32
    ident = np.eye(P, dtype=f)
    quarter = HD // 4
    inv = (10000.0 ** (-np.arange(quarter, dtype=f) / quarter)).astype(f)
    pos = np.arange(LAT * P)
    cos = np.zeros((LAT * P, 2, 2, quarter), f)
    sin = np.zeros((LAT * P, 2, 2, quarter), f)
    for half, x in enumerate((pos // GRID_W, pos % GRID_W)):
        ang = x.astype(f)[:, None] * inv[None, :]
        cos[:, half, 0] = cos[:, half, 1] = np.cos(ang)
        sin[:, half, 0] = -np.sin(ang)
        sin[:, half, 1] = np.sin(ang)
    cos = cos.reshape(LAT, P, HD).transpose(1, 0, 2)
    sin = sin.reshape(LAT, P, HD).transpose(1, 0, 2)
    s = np.arange(P)
    causal = np.zeros((P, 2, P), f)
    causal[:, 0] = np.where(s[:, None] <= s[None, :], 0, NEG)
    causal[:, 1] = np.where(s[:, None] >= s[None, :], 0, NEG)
    window = np.full((P, WIN_TYPES, WIN_ROWS, GRID_W), NEG, f)
    for t in (0, 1, 2, 6, 7):
        for p in range(P):
            r, c = 2 * t + p // GRID_W, p % GRID_W
            rs = min(max(r - NA_ROWS // 2, 0), ROWS - NA_ROWS) - window_start_row(t)
            cs = min(max(c - NA_COLS // 2, 0), GRID_W - NA_COLS)
            window[p, window_type(t), rs:rs + NA_ROWS, cs:cs + NA_COLS] = 0
    neg_select = np.zeros((P, 2, 4, P), f)
    diagonal = np.zeros((36, 4, NT), f)
    for j in range(4):
        for d in range(2):
            neg_select[32 * d + j, d, j] = -1
            diagonal[32 * d + j, j] = 1
    cond_select = np.zeros((2, 2, P), f)
    cond_select[0, 0] = cond_select[1, 1] = 1
    return {
        "ident": ident, "cos": cos.copy(), "sin": sin.copy(), "causal": causal,
        "window": window.reshape(P, WIN_TYPES * WIN), "neg_select": neg_select,
        "diagonal": diagonal, "cond_select": cond_select,
    }


class Steps:

    def __init__(self, eng, sem):
        self.eng, self.sem, self.n = eng, sem, 0

    def __call__(self, ins):
        self.n += 1
        ins.then_inc(self.sem, 1)
        self.eng.wait_ge(self.sem, self.n)


def build(nc, I, O):
    sems = {}
    with ExitStack() as ctx:
        sem_stack = ExitStack()
        dve_step = act_step = pool_step = None

        def sem(name):
            if name not in sems:
                sems[name] = sem_stack.enter_context(nc.semaphore(name))
            return sems[name]

        def open_section():
            nonlocal dve_step, act_step, pool_step
            dve_step = Steps(nc.vector, sem("dve_steps"))
            act_step = Steps(nc.scalar, sem("act_steps"))
            pool_step = Steps(nc.gpsimd, sem("pool_steps"))

        def close_section():
            numbers = sorted(s.num for s in sems.values())
            first = 0
            for i, n in enumerate(numbers):
                if i + 1 == len(numbers) or numbers[i + 1] != n + 1:
                    nc.all_engine_barrier(sems_to_clear=range(numbers[first], n + 1))
                    first = i + 1
            sem_stack.close()
            sems.clear()

        def sb(name, shape, stack=ctx, dtype=F32):
            return stack.enter_context(nc.sbuf_tensor(name, shape, dtype))

        def dram(name, shape):
            return nc.dram_tensor(name, shape, F32, kind="Internal").ap()

        ps = ctx.enter_context(nc.psum_tensor("ps", [P, 8, 512], F32))
        psf = ps[:, :, :].rearrange("p b n -> p (b n)")

        x_dram = dram("x_residual", (TOK, D))
        bias_pitch = BIAS_DR * BIAS_W
        bias_dram = dram("bias_by_column", (DEPTH, 6, GRID_W * bias_pitch))
        bias_copied = ctx.enter_context(nc.semaphore("bias_copied"))

        ident = sb("ident_sb", [P, P])
        causal = sb("causal_sb", [P, 2, P])
        neg_select = sb("neg_select_sb", [P, 2, 4, P])
        diagonal = sb("diagonal_sb", [36, 4, NT])
        cond_select = sb("cond_select_sb", [2, 2, P])
        ones = sb("ones", [36, P])
        minus_half = sb("minus_half", [P, NT * 4])
        condT = sb("condT", [P, KD, 2])
        cond_e = sb("cond_e", [P, KD, 2])
        modT = sb("modT", [P, 4, KD, 2])
        gate = sb("gate", [P, 2, 2, D])
        mix = sb("mix", [P, NT, D])
        small = sb("small", [P, 256])

        with nc.Block() as block:
            @block.sync
            def _(sp):
                for k, t in (("ident", ident[:, :]), ("causal", causal[:, :, :]), ("neg_select", neg_select[:, :, :, :]),
                             ("diagonal", diagonal[:, :, :]),
                             ("cond_select", cond_select[:, :, :])):
                    sp.dma_start(t, I[k]).then_inc(sem("constants_loaded"), 16)
                sp.dma_start(x_dram[0:LAT * P, :], I["x_sample"]).then_inc(sem("residual_copied"), 16)
                sp.dma_start(x_dram[LAT * P:TOK, :], I["x_prompt"]).then_inc(sem("residual_copied"), 16)
                for l in range(DEPTH):
                    for h in range(6):
                        sp.dma_start(bias_dram[l, h].rearrange("(c j) -> c j", c=GRID_W),
                                     I["bias_rows"][l, h:h + 1, :].to_broadcast([GRID_W, bias_pitch])).then_inc(bias_copied, 16)
                sp.wait_ge(sem("constants_loaded"), 5 * 16)
                sp.wait_ge(sem("residual_copied"), 2 * 16)

            @block.gpsimd
            def _(pool):
                pool.memset(ones[:, :], 1.0)
                pool.memset(small[:, :], 0.0)
                pool.memset(minus_half[:, :], -0.5)

            @block.scalar
            def _(act):
                act.dma_start(condT[:, :, :], I["condT"]).then_inc(sem("cond_loaded"), 16)
                act.wait_ge(sem("cond_loaded"), 16)
                act.activation(cond_e[:, :, :], condT[:, :, :], ACT.Exp, scale=-1.0).then_inc(sem("cond_exp"), 1)

            @block.vector
            def _(dve):
                step = Steps(dve, sem("silu_steps"))
                dve.wait_ge(sem("cond_exp"), 1)
                step(dve.tensor_scalar(cond_e[:, :, :], cond_e[:, :, :], 1.0, None, ALU.add))
                step(dve.reciprocal(cond_e[:, :, :], cond_e[:, :, :]))
                step(dve.tensor_tensor(condT[:, :, :], condT[:, :, :], cond_e[:, :, :], ALU.mult))

        close_section()
        with nc.Fori(0, DEPTH) as l:

            w_in = I["w_in"][l].rearrange("(k p) n -> p k n", p=P)

            A_CUTS = ((OFF_A + 384, 256), (OFF_A, 384))
            B_CUTS = ((OFF_B, 256), (OFF_B + 768, 272), (OFF_B + 256, 256), (OFF_B + 512, 256))

            def load_cuts(sp, cuts):
                for c, (o, n) in enumerate(cuts):
                    sp.dma_start(ring[:, c, :, 0:n], w_in[:, :, o:o + n]).then_inc(sem("next_w_loaded"), 16)
                sp.wait_ge(sem("next_w_loaded"), 16 * len(cuts))

            def load_c_weights(sp, pair):
                for m in range(3):
                    o = OFF_C + m * 384 + pair * P
                    sp.dma_start(ring[:, pair % 2, :, m * P:(m + 1) * P], w_in[:, :, o:o + P]).then_inc(sem("next_c_w_loaded"), 16)
                sp.wait_ge(sem("next_c_w_loaded"), 48)

            class Modulation:
                CHUNK = 256
                HALVES = CHUNK // P

                def __init__(self, tag, vectors, w, own):
                    self.tag, self.w, self.ring = tag, w, w.shape[1]
                    self.chunks = [(v, q) for v in vectors for q in range(D // self.CHUNK)]
                    self.n = len(self.chunks)
                    self.w_dram = I["w_ada"][l].rearrange("(k p) n -> p k n", p=P)
                    self.gpre = sb(f"{tag}_g_preT", [P, 2, KD], own)
                    gates = [c for c in range(self.n) if self.is_gate(c)]
                    self.gate_count = {c: i + 1 for i, c in enumerate(gates)}
                    self.rows_in = sb(f"{tag}_rows_in", [2, self.ring, 2, self.CHUNK], own)
                    self.row = sb(f"{tag}_row", [2, 2, self.CHUNK], own)
                    self.rows_loads, loads = [], [0] * self.ring
                    for c in range(self.n):
                        loads[c % self.ring] += 2 if self.is_gate(c) else 1
                        self.rows_loads.append(loads[c % self.ring])

                def sem(self, name):
                    return sem(f"{self.tag}_{name}")

                def is_gate(self, c):
                    return self.chunks[c][0] in (2, 5)

                def row_out(self, c):
                    return ps[0:2, 6 + c % 2, 0:self.CHUNK]

                def load_gain(self, sp):
                    sp.dma_start(self.gpre[:, :, :], I["g_preT"][l]).then_inc(self.sem("gain_loaded"), 16)

                def load(self, sp, c):
                    v, q = self.chunks[c]
                    cols = slice(v * D + q * self.CHUNK, v * D + (q + 1) * self.CHUNK)
                    if c >= self.ring:
                        sp.wait_ge(self.sem("multiplied"), c - self.ring + 1)
                    sp.dma_start(self.w[:, c % self.ring, :, :], self.w_dram[:, :, cols]).then_inc(self.sem(f"w_loaded{c % self.ring}"), 16)
                    into = self.rows_in[:, c % self.ring, :, :]
                    sp.dma_start(into[:, 0, :], I["b_ada"][bass.ds(l, 1), cols].to_broadcast([2, self.CHUNK])).then_inc(self.sem(f"rows_loaded{c % self.ring}"), 16)
                    if self.is_gate(c):
                        if c - self.ring in self.gate_count:
                            sp.wait_ge(self.sem("gate_scaled"), self.gate_count[c - self.ring])
                        s = v // 3
                        sp.dma_start(into[:, 1, :], I["g_post"][bass.ds(l, 1), s, q * self.CHUNK:(q + 1) * self.CHUNK].to_broadcast([2, self.CHUNK])).then_inc(
                            self.sem(f"rows_loaded{c % self.ring}"), 16)

                def multiply(self, pe, c):
                    pe.wait_ge(self.sem(f"w_loaded{c % self.ring}"), 16 * (c // self.ring + 1))
                    if c >= 2:
                        pe.wait_ge(self.sem("row_copied"), c - 1)
                    for k in range(KD):
                        pe.matmul(self.row_out(c), condT[:, k, :], self.w[:, c % self.ring, k, :], start=(k == 0), stop=False)
                    pe.wait_ge(self.sem(f"rows_loaded{c % self.ring}"), 16 * self.rows_loads[c])
                    mm = pe.matmul(self.row_out(c), ones[0:1, 0:2], self.rows_in[0:1, c % self.ring, 0, :], start=False, stop=True)
                    mm.then_inc(self.sem("multiplied"), 1)

                def spread(self, pe, c):
                    if c >= 1:
                        pe.wait_ge(self.sem("chunk_done"), c)
                    if self.is_gate(c):
                        pe.wait_ge(self.sem("gate_scaled"), self.gate_count[c])
                        for cond in range(2):
                            mm = pe.matmul(ps[:, 5, cond * self.CHUNK:(cond + 1) * self.CHUNK], cond_select[:, cond, :], self.row[:, c % 2, :],
                                           start=True, stop=True)
                    else:
                        pe.wait_ge(self.sem("row_copied"), c + 1)
                        for m in range(self.HALVES):
                            mm = pe.transpose(ps[:, 5, 2 * m:2 * m + 2], self.row[:, c % 2, m * P:(m + 1) * P], ident[0:2, 0:2])
                    mm.then_inc(self.sem("spread"), 1)

                def take_row(self, act, c):
                    act.wait_ge(self.sem("multiplied"), c + 1)
                    if c >= 2:
                        act.wait_ge(self.sem("spread"), c - 1)
                    act.copy(self.row[:, c % 2, :], self.row_out(c)).then_inc(self.sem("row_copied"), 1)

                def take_spread(self, act, c):
                    v, q = self.chunks[c]
                    act.wait_ge(self.sem("spread"), c + 1)
                    if self.is_gate(c):
                        a = act.copy(gate[:, v // 3, :, q * self.CHUNK:(q + 1) * self.CHUNK], ps[:, 5, :].rearrange("p (c n) -> p c n", c=2))
                    elif v % 3 == 0:
                        a = act.copy(modT[:, 2 * (v // 3), q * self.HALVES:(q + 1) * self.HALVES, :],
                                     ps[:, 5, 0:2 * self.HALVES].rearrange("p (k c) -> p k c", c=2))
                    else:
                        act.wait_ge(self.sem("gain_loaded"), 16)
                        for m in range(self.HALVES):
                            k = q * self.HALVES + m
                            g = self.gpre[:, v // 3, k:k + 1]
                            a = act.activation(modT[:, 2 * (v // 3) + 1, k, :], ps[:, 5, 2 * m:2 * m + 2], ACT.Identity, bias=g, scale=g)
                    a.then_inc(self.sem("chunk_done"), 1)

                def tensor_step(self, pe, c):
                    if c == 0:
                        self.multiply(pe, 0)
                    if c + 1 < self.n:
                        self.multiply(pe, c + 1)
                    self.spread(pe, c)

                def scalar_step(self, act, c):
                    if c < self.n:
                        self.take_row(act, c)
                    if c >= 1:
                        self.take_spread(act, c - 1)

                def scale_gate_rows(self, pool):
                    for c, n in self.gate_count.items():
                        pool.wait_ge(self.sem("row_copied"), c + 1)
                        pool.wait_ge(self.sem(f"rows_loaded{c % self.ring}"), 16 * self.rows_loads[c])
                        pool.tensor_tensor(self.row[:, c % 2, :], self.row[:, c % 2, :], self.rows_in[:, c % self.ring, 1, :],
                                           ALU.mult).then_inc(self.sem("gate_scaled"), 1)

            def input_norm():
                AHEAD = 4
                with ExitStack() as own:
                    mods = Modulation("mix_mods", (0, 1), sb("w_ada_ring", [P, 4, KD, Modulation.CHUNK], own), own)
                    x = sb("in_x", [P, NT, D], own)
                    junk = sb("in_junk", [P, D], own)
                    ssq, rstd = small[:, 0:NT], small[:, NT:2 * NT]

                    def turned_to(t, k):
                        at = t % 2 * 1024 + k * P
                        return psf[:, at:at + P]

                    with nc.Block() as block:
                        @block.sync
                        def _(sp):
                            mods.load_gain(sp)
                            for t in range(NT):
                                if t == AHEAD:
                                    for c in range(mods.n):
                                        mods.load(sp, c)
                                sp.dma_start(x[:, t, :], x_dram[t * P:(t + 1) * P, :]).then_inc(sem(f"in_x_loaded{t}"), 16)
                            load_cuts(sp, A_CUTS[:1])

                        @block.tensor
                        def _(pe):
                            for c in range(mods.n):
                                mods.tensor_step(pe, c)
                            for t in range(NT):
                                pe.wait_ge(sem("in_normed"), t + 1)
                                if t >= 2:
                                    pe.wait_ge(sem("in_modulated_dve"), t - 1)
                                    pe.wait_ge(sem("in_modulated_act"), t - 1)
                                for k in range(KD):
                                    mm = pe.transpose(turned_to(t, k), x[:, t, k * P:(k + 1) * P], ident[:, :])
                                mm.then_inc(sem("in_turned"), 1)

                        @block.scalar
                        def _(act):
                            def squares(t):
                                act.wait_ge(sem(f"in_x_loaded{t}"), 16)
                                act_step(act.activation(junk[:, :], x[:, t, :], ACT.Square, accum_out=ssq[:, t:t + 1]))
                                act.sem_inc(sem("in_squared"), 1)

                            for t in range(AHEAD):
                                squares(t)
                            for c in range(mods.n + 1):
                                mods.scalar_step(act, c)
                            act.wait_ge(mods.sem("chunk_done"), mods.n)
                            for t in range(NT):
                                if t + AHEAD < NT:
                                    squares(t + AHEAD)
                                c = 1 if t == PROMPT else 0
                                act.wait_ge(sem("in_turned"), t + 1)
                                for k in range(4, KD):
                                    a = act.activation(hT[:, k, t * P:(t + 1) * P], turned_to(t, k), ACT.Identity,
                                                       bias=modT[:, 0, k, c:c + 1], scale=modT[:, 1, k, c:c + 1])
                                a.then_inc(sem("in_modulated_act"), 1)

                        @block.gpsimd
                        def _(pool):
                            for t in range(NT):
                                pool.wait_ge(sem("in_squared"), t + 1)
                                pool_step(pool.tensor_scalar(rstd[:, t:t + 1], ssq[:, t:t + 1], 1.0 / D, EPS, ALU.mult, ALU.add))
                                pool.tensor_tensor(rstd[:, t:t + 1], rstd[:, t:t + 1], minus_half[:, 0:1], ALU.pow).then_inc(sem("in_rstd"), 1)

                        @block.vector
                        def _(dve):
                            def normalise(t):
                                dve.wait_ge(sem("in_rstd"), t + 1)
                                dve.tensor_scalar(x[:, t, :], x[:, t, :], rstd[:, t:t + 1], None, ALU.mult).then_inc(sem("in_normed"), 1)

                            for t in range(AHEAD):
                                normalise(t)
                            dve.wait_ge(mods.sem("chunk_done"), mods.n)
                            for t in range(NT):
                                c = 1 if t == PROMPT else 0
                                dve.wait_ge(sem("in_turned"), t + 1)
                                for k in range(4):
                                    a = dve.tensor_scalar(hT[:, k, t * P:(t + 1) * P], turned_to(t, k), modT[:, 1, k, c:c + 1], modT[:, 0, k, c:c + 1],
                                                          ALU.mult, ALU.add)
                                a.then_inc(sem("in_modulated_dve"), 1)
                                if t + AHEAD < NT:
                                    normalise(t + AHEAD)

            def residual_norm(tag, sub, norm):
                with ExitStack() as own:
                    x = sb(f"{tag}_x", [P, NT, D], own)
                    junk = sb(f"{tag}_junk", [P, D], own)
                    xn = sb(f"{tag}_x_normed", [P, 2, D], own) if norm else None
                    FULL = 3
                    full = sb(f"{tag}_h_full", [P, FULL, KD, P], own) if norm else None
                    ssq, rstd = small[:, 0:NT], small[:, NT:2 * NT]
                    ssq2, rstd2 = small[:, 2 * NT:3 * NT], small[:, 3 * NT:4 * NT]
                    y_sq, y_rstd, x_new = sem(f"{tag}_y_squares"), sem(f"{tag}_y_rstd"), sem(f"{tag}_x_new")
                    if norm:
                        x_sq, x_rstd = sem(f"{tag}_x_squares"), sem(f"{tag}_x_rstd")
                        normed, turned = sem(f"{tag}_normed"), sem(f"{tag}_turned")
                        mod_d, mod_a = sem(f"{tag}_modulated_dve"), sem(f"{tag}_modulated_act")
                        hi_done, lo_done = sem(f"{tag}_hi_done"), sem(f"{tag}_lo_done")
                    ON_DVE = 3
                    ADD, SQUARES, NORM, MODULATE, HIGH, LOW = 1, 2, 3, 4, 5, 6
                    STEPS = NT + (LOW if norm else ADD)

                    def turned_to(t, k):
                        at = t % 2 * 1536 + (k * P if k < ON_DVE else 512 + (k - ON_DVE) * P)
                        return psf[:, at:at + P]

                    with nc.Block() as block:
                        @block.sync
                        def _(sp):
                            for t in range(NT):
                                sp.dma_start(x[:, t, :], x_dram[t * P:(t + 1) * P, :]).then_inc(sem(f"{tag}_x_loaded{t}"), 16)
                            for t in range(NT):
                                sp.wait_ge(x_new, t + 1)
                                sp.dma_start(x_dram[t * P:(t + 1) * P, :], x[:, t, :]).then_inc(sem(f"{tag}_x_stored"), 16)
                            sp.wait_ge(sem(f"{tag}_x_stored"), 16 * NT)

                        @block.scalar
                        def _(act):
                            def squares_y(t):
                                act_step(act.activation(junk[:, :], mix[:, t, :], ACT.Square, accum_out=ssq[:, t:t + 1]))
                                act.sem_inc(y_sq, 1)

                            def squares_x(t):
                                act.wait_ge(x_new, t + 1)
                                act_step(act.activation(junk[:, :], x[:, t, :], ACT.Square, accum_out=ssq2[:, t:t + 1]))
                                act.sem_inc(x_sq, 1)

                            def modulate(t):
                                c = 1 if t == PROMPT else 0
                                act.wait_ge(turned, t + 1)
                                if t >= FULL:
                                    act.wait_ge(lo_done, t - FULL + 1)
                                for k in range(ON_DVE, KD):
                                    a = act.activation(full[:, t % FULL, k, :], turned_to(t, k), ACT.Identity,
                                                       bias=modT[:, 2, k, c:c + 1], scale=modT[:, 3, k, c:c + 1])
                                a.then_inc(mod_a, 1)

                            def high_part(t):
                                act.wait_ge(mod_a, t + 1)
                                act.wait_ge(mod_d, t + 1)
                                act.copy(hi[:, :, t * P:(t + 1) * P], full[:, t % FULL, :, :]).then_inc(hi_done, 1)

                            for n in range(STEPS):
                                if n < NT:
                                    squares_y(n)
                                if norm and 0 <= n - HIGH < NT:
                                    high_part(n - HIGH)
                                if norm and 0 <= n - SQUARES < NT:
                                    squares_x(n - SQUARES)
                                if norm and 0 <= n - MODULATE < NT:
                                    modulate(n - MODULATE)

                        @block.gpsimd
                        def _(pool):
                            def inverse_root(s, r, t, ready, done):
                                pool.wait_ge(ready, t + 1)
                                pool_step(pool.tensor_scalar(r[:, t:t + 1], s[:, t:t + 1], 1.0 / D, EPS, ALU.mult, ALU.add))
                                pool.tensor_tensor(r[:, t:t + 1], r[:, t:t + 1], minus_half[:, 0:1], ALU.pow).then_inc(done, 1)

                            for n in range(NT + SQUARES):
                                if n < NT:
                                    inverse_root(ssq, rstd, n, y_sq, y_rstd)
                                if norm and n >= SQUARES:
                                    inverse_root(ssq2, rstd2, n - SQUARES, x_sq, x_rstd)

                        @block.vector
                        def _(dve):
                            def add_residual(t):
                                dve.wait_ge(y_rstd, t + 1)
                                dve_step(dve.scalar_tensor_tensor(mix[:, t, :], mix[:, t, :], rstd[:, t:t + 1],
                                                                  gate[:, sub, 1 if t == PROMPT else 0, :], ALU.mult, ALU.mult))
                                dve.wait_ge(sem(f"{tag}_x_loaded{t}"), 16)
                                dve.tensor_tensor(x[:, t, :], x[:, t, :], mix[:, t, :], ALU.add).then_inc(x_new, 1)

                            def normalise(t):
                                dve.wait_ge(x_rstd, t + 1)
                                dve.wait_ge(x_new, t + 1)
                                if t >= 2:
                                    dve.wait_ge(turned, t - 1)
                                dve.tensor_scalar(xn[:, t % 2, :], x[:, t, :], rstd2[:, t:t + 1], None, ALU.mult).then_inc(normed, 1)

                            def modulate(t):
                                c = 1 if t == PROMPT else 0
                                dve.wait_ge(turned, t + 1)
                                if t >= FULL:
                                    dve.wait_ge(lo_done, t - FULL + 1)
                                for k in range(ON_DVE):
                                    a = dve.tensor_scalar(full[:, t % FULL, k, :], turned_to(t, k), modT[:, 3, k, c:c + 1],
                                                          modT[:, 2, k, c:c + 1], ALU.mult, ALU.add)
                                a.then_inc(mod_d, 1)

                            def low_part(t):
                                dve.wait_ge(hi_done, t + 1)
                                tt = slice(t * P, (t + 1) * P)
                                dve.tensor_tensor(lo[:, :, tt], full[:, t % FULL, :, :], hi[:, :, tt].bitcast(F32), ALU.subtract).then_inc(lo_done, 1)

                            for n in range(ADD, STEPS):
                                if n - ADD < NT:
                                    add_residual(n - ADD)
                                if norm and 0 <= n - LOW < NT:
                                    low_part(n - LOW)
                                if norm and 0 <= n - NORM < NT:
                                    normalise(n - NORM)
                                if norm and 0 <= n - MODULATE < NT:
                                    modulate(n - MODULATE)

                        @block.tensor
                        def _(pe):
                            for t in range(NT if norm else 0):
                                pe.wait_ge(normed, t + 1)
                                if t >= 2:
                                    pe.wait_ge(mod_d, t - 1)
                                    pe.wait_ge(mod_a, t - 1)
                                for k in range(KD):
                                    mm = pe.transpose(turned_to(t, k), xn[:, t % 2, k * P:(k + 1) * P], ident[:, :])
                                mm.then_inc(turned, 1)

            def attention(tag, units, own, n_bias_cols):
                nu = len(units)
                P_sb = sb(f"{tag}_probs", [P, 2, NT * P], own)
                PT = sb(f"{tag}_probsT", [P, 2, NT * P], own)
                Ssb = sb(f"{tag}_scores", [P, 2, n_bias_cols], own) if n_bias_cols else None
                biased = sb(f"{tag}_bias_tiles", [P, 2, n_bias_cols], own) if n_bias_cols else None
                nmax = small[:, 64:68]
                den = small[:, 68:72]
                rden = small[:, 72:76]
                groups, count = [], [0, 0]
                for i, u in enumerate(units):
                    g0 = []
                    for g in range((u["n"] // P + 2) // 3):
                        e = len(groups) % 2
                        count[e] += 1
                        g0.append((len(groups), e, count[e], 3 * g, min(3 * g + 3, u["n"] // P)))
                        groups.append(g0[-1])
                    u["groups"] = g0
                copied = [sem(f"{tag}_probsT_copied_act"), sem(f"{tag}_probsT_copied_dve")]
                S_ready, max_ready, exp_done = sem(f"{tag}_scores_ready"), sem(f"{tag}_max_ready"), sem(f"{tag}_exp_done")
                turned, pv_done, out_done = sem(f"{tag}_probs_turned"), sem(f"{tag}_pv_done"), sem(f"{tag}_out_done")
                bias_ready = sem(f"{tag}_bias_ready")
                bias_count = [0]
                for u in units:
                    if u["bias"] is not None:
                        bias_count[0] += 1
                        u["bias_n"] = bias_count[0]

                def S(i, a, b):
                    return psf[:, i % 2 * 1536 + a:i % 2 * 1536 + b]

                def PTp(i, k, z):
                    at = (i % 2 * 3 + k // 3) * 512 + k % 3 * P
                    return psf[:, at:at + (z - k) * P]

                def out_p(i):
                    return ps[:, 6 + i % 2, 0:P]

                def tensor(pe):
                    def scores(i):
                        if i >= 2:
                            for gi, e, n, a, b in units[i - 2]["groups"]:
                                pe.wait_ge(copied[e], n)
                        for kT, c0 in units[i]["keys"]:
                            mm = pe.matmul(S(i, c0, c0 + kT.shape[1]), units[i]["q"], kT, start=True, stop=True)
                        mm.then_inc(S_ready, 1)

                    def turn(i):
                        pe.wait_ge(exp_done, i + 1)
                        for gi, e, n, a, b in units[i]["groups"]:
                            for k in range(a, b):
                                mm = pe.transpose(PTp(i, k, k + 1), P_sb[:, i % 2, k * P:(k + 1) * P], ident[:, :])
                            mm.then_inc(turned, 1)

                    def apply(i):
                        u = units[i]
                        if i >= 2:
                            pe.wait_ge(out_done, i - 1)
                        for gi, e, n, a, b in u["groups"]:
                            pe.wait_ge(copied[e], n)
                            for k in range(a, b):
                                mm = pe.matmul(out_p(i), PT[:, i % 2, k * P:(k + 1) * P], u["v"][k],
                                               start=(k == 0), stop=(k == u["n"] // P - 1))
                        mm.then_inc(pv_done, 1)

                    scores(0)
                    scores(1)
                    for i in range(nu):
                        turn(i)
                        if i >= 1:
                            apply(i - 1)
                        if i + 2 < nu:
                            scores(i + 2)
                    apply(nu - 1)

                def copy_groups(eng, e, i):
                    for gi, ge, n, a, b in units[i]["groups"]:
                        if ge != e:
                            continue
                        eng.wait_ge(turned, gi + 1)
                        src, dst = PTp(i, a, b), PT[:, i % 2, a * P:b * P]
                        ins = eng.copy(dst, src) if e == 0 else eng.tensor_copy(dst, src)
                        ins.then_inc(copied[e], 1)

                def scalar(act):
                    def exp(i):
                        n = units[i]["n"]
                        act.wait_ge(max_ready, i + 1)
                        if i >= 2:
                            act.wait_ge(turned, units[i - 2]["groups"][-1][0] + 1)
                        src = S(i, 0, n) if units[i]["bias"] is None else Ssb[:, i % 2, 0:n]
                        act.activation(P_sb[:, i % 2, 0:n], src, ACT.Exp, bias=nmax[:, i % 4:i % 4 + 1],
                                       accum_out=den[:, i % 4:i % 4 + 1]).then_inc(exp_done, 1)
                    exp(0)
                    for i in range(nu):
                        copy_groups(act, 0, i)
                        if i + 1 < nu:
                            exp(i + 1)

                def vector(dve):
                    def maximum(i):
                        u = units[i]
                        dve.wait_ge(S_ready, i + 1)
                        if u["bias"] is None:
                            dve.tensor_reduce(nmax[:, i % 4:i % 4 + 1], S(i, 0, u["n"]), AX.X, ALU.max, negate=True).then_inc(max_ready, 1)
                        else:
                            dve.wait_ge(bias_ready, u["bias_n"])
                            if i >= 2:
                                dve.wait_ge(exp_done, i - 1)
                            dve_step(dve.tensor_tensor_reduce(Ssb[:, i % 2, :], S(i, 0, u["n"]), biased[:, u["bias_n"] % 2, :], 1.0, LOWEST,
                                                              ALU.add, ALU.max, nmax[:, i % 4:i % 4 + 1]))
                            dve.tensor_scalar(nmax[:, i % 4:i % 4 + 1], nmax[:, i % 4:i % 4 + 1], -1.0, None, ALU.mult).then_inc(max_ready, 1)

                    def output(i):
                        dve.wait_ge(exp_done, i + 1)
                        dve_step(dve.reciprocal(rden[:, i % 4:i % 4 + 1], den[:, i % 4:i % 4 + 1]))
                        dve.wait_ge(pv_done, i + 1)
                        dve.tensor_scalar(units[i]["out"], out_p(i)[:, units[i]["cols"]], rden[:, i % 4:i % 4 + 1], None,
                                          ALU.mult).then_inc(out_done, 1)
                    maximum(0)
                    maximum(1)
                    for i in range(nu):
                        copy_groups(dve, 1, i)
                        if i >= 1:
                            output(i - 1)
                        if i + 2 < nu:
                            maximum(i + 2)
                    output(nu - 1)

                return tensor, scalar, vector, biased, bias_ready, max_ready

            def mixer_a():
                with ExitStack() as own:
                    Z = sb("a_z", [P, NT, 512], own)
                    QK = sb("a_qkT", [P, 4, NSLOT * P], own)
                    V = sb("a_v", [P, NSLOT, P], own)
                    g = sb("a_g", [P, 8, HD], own)
                    ctx_k = sb("a_ctx_k", [P, P], own)
                    with ExitStack() as inner:
                        sq = sb("a_sq", [P, 2, 512], inner)
                        r1 = sb("a_r1", [P, 2, 512], inner)
                        r2 = sb("a_r2", [P, 512], inner)
                        zr = sb("a_zr", [P, 2, 512], inner)
                        cos = sb("cos_sb", [P, LAT, HD], inner)
                        sin = sb("sin_sb", [P, LAT, HD], inner)
                        ss = small[:, 96:96 + NT * 8].rearrange("p (t h) -> p t h", h=8)
                        rs = small[:, 168:168 + NT * 8].rearrange("p (t h) -> p t h", h=8)
                        cuts = A_CUTS
                        with nc.Block() as block:
                            @block.sync
                            def _(sp):
                                o, n = cuts[1]
                                sp.dma_start(ring[:, 1, :, 0:n], w_in[:, :, o:o + n]).then_inc(sem("a_w_loaded1"), 16)
                                sp.dma_start(ctx_k[:, :], I["cache_k_attn"][l]).then_inc(sem("a_ctx_k_loaded"), 16)
                                sp.dma_start(V[:, CTX_SLOT, :], I["cache_v_attn"][l]).then_inc(sem("a_ctx_v_loaded"), 16)
                                sp.dma_start(cos[:, :, :], I["cos"]).then_inc(sem("a_rotary_loaded"), 16)
                                sp.dma_start(sin[:, :, :], I["sin"]).then_inc(sem("a_rotary_loaded"), 16)
                                for h in range(8):
                                    src = I["q_norm"] if h < 6 else I["k_norm"]
                                    sp.dma_start(g[:, h, :], src[bass.ds(l, 1), :].to_broadcast([P, HD])).then_inc(sem("a_g_loaded"), 16)
                                sp.wait_ge(sem("a_normed"), NT)
                                sp.dma_start(O["new_k_attn"][l], Z[:, PROMPT, 384:512]).then_inc(sem("a_cache_stored"), 16)
                                sp.wait_ge(sem("a_v_copied"), NT)
                                sp.dma_start(O["new_v_attn"][l], V[:, PROMPT_SLOT, :]).then_inc(sem("a_cache_stored"), 16)

                            @block.tensor
                            def _(pe):
                                def turn(t):
                                    pe.wait_ge(sem("a_rotated"), t + 1)
                                    if t >= 2:
                                        pe.wait_ge(sem("a_qk_copied"), t - 1)
                                    for m in range(4):
                                        mm = pe.transpose(ps[:, 4 + t % 2, m * P:(m + 1) * P], zr[:, t % 2, m * P:(m + 1) * P], ident[:, :])
                                    mm.then_inc(sem("a_qk_turned"), 1)

                                LAG = 3
                                for c, (o, n) in enumerate(cuts):
                                    if c == 1:
                                        pe.wait_ge(sem("a_w_loaded1"), 16)
                                    for t in range(NT):
                                        j = c * NT + t
                                        if j >= 4:
                                            pe.wait_ge(sem("a_projected_copied"), j - 3)
                                        for k in range(KD):
                                            mm = pe.matmul(ps[:, j % 4, 0:n], hT[:, k, t * P:(t + 1) * P], ring[:, c, k, 0:n],
                                                           start=(k == 0), stop=(k == KD - 1))
                                        mm.then_inc(sem("a_projected"), 1)
                                        if c == 1 and t >= LAG:
                                            turn(t - LAG)
                                pe.wait_ge(sem("a_ctx_k_loaded"), 16)
                                pe.transpose(ps[:, 6, 0:P], ctx_k[:, :], ident[:, :]).then_inc(sem("a_ctx_turned"), 1)
                                for t in range(NT - LAG, NT):
                                    turn(t)

                            @block.scalar
                            def _(act):
                                def take_turned(t):
                                    act.wait_ge(sem("a_qk_turned"), t + 1)
                                    act.copy(QK[:, :, key_slot(t) * P:(key_slot(t) + 1) * P],
                                             ps[:, 4 + t % 2, :].rearrange("p (m n) -> p m n", m=4)).then_inc(sem("a_qk_copied"), 1)

                                for j in range(2 * NT):
                                    t = j % NT
                                    act.wait_ge(sem("a_projected"), j + 1)
                                    if j < NT:
                                        act.copy(V[:, key_slot(t), :], ps[:, j % 4, P:2 * P]).then_inc(sem("a_v_copied"), 1)
                                        act.copy(Z[:, t, 384:512], ps[:, j % 4, 0:P]).then_inc(sem("a_projected_copied"), 1)
                                    else:
                                        act.copy(Z[:, t, 0:384], ps[:, j % 4, 0:384]).then_inc(sem("a_projected_copied"), 1)
                                        if t >= 4:
                                            take_turned(t - 4)
                                act.wait_ge(sem("a_ctx_turned"), 1)
                                act.copy(QK[:, 3, CTX_SLOT * P:(CTX_SLOT + 1) * P], ps[:, 6, 0:P])
                                for t in range(NT - 4, NT):
                                    take_turned(t)

                            @block.gpsimd
                            def _(pool):
                                for t in range(NT + 1):
                                    if t < NT:
                                        pool.wait_ge(sem("a_projected_copied"), NT + t + 1)
                                        if t >= 2:
                                            pool.wait_ge(sem("a_squares_summed"), t - 1)
                                        pool.tensor_tensor(sq[:, t % 2, :], Z[:, t, :], Z[:, t, :], ALU.mult).then_inc(sem("a_squared"), 1)
                                    if t >= 1:
                                        u = t - 1
                                        pool.wait_ge(sem("a_squares_summed"), t)
                                        pool_step(pool.tensor_scalar(rs[:, u, :], ss[:, u, :], 1.0 / HD, EPS, ALU.mult, ALU.add))
                                        pool.tensor_tensor(rs[:, u, :], rs[:, u, :], minus_half[:, 0:8], ALU.pow).then_inc(sem("a_rstd"), 1)

                            @block.vector
                            def _(dve):
                                dve.wait_ge(sem("a_g_loaded"), 8 * 16)
                                dve.wait_ge(sem("a_rotary_loaded"), 32)
                                dve_step(dve.tensor_scalar(g[:, 0:6, :], g[:, 0:6, :], SCALE, None, ALU.mult))

                                def norm_and_rotate(t):
                                    z = Z[:, t, :].rearrange("p (h d) -> p h d", d=HD)
                                    dve.wait_ge(sem("a_rstd"), t + 1)
                                    dve_step(dve.tensor_tensor(z, z, rs[:, t, :].unsqueeze(2).to_broadcast([P, 8, HD]), ALU.mult))
                                    dve.tensor_tensor(z, z, g[:, :, :], ALU.mult).then_inc(sem("a_normed"), 1)
                                    dve.wait_ge(sem("a_normed"), t + 1)
                                    if t >= 2:
                                        dve.wait_ge(sem("a_qk_turned"), t - 1)
                                    outq = zr[:, t % 2, 0:384].rearrange("p (g n d) -> p n g d", n=2, d=HD)
                                    outk = zr[:, t % 2, 384:512]
                                    if t == PROMPT:
                                        dve_step(dve.tensor_copy(outq, Z[:, t, 0:384].rearrange("p (n g d) -> p n g d", n=2, d=HD)))
                                        dve.tensor_copy(outk, Z[:, t, 384:512]).then_inc(sem("a_rotated"), 1)
                                        return
                                    a = r1[:, t % 2, :].rearrange("p (h d) -> p h d", d=HD)
                                    dve_step(dve.tensor_tensor(a, z, cos[:, t:t + 1, :].to_broadcast([P, 8, HD]), ALU.mult))
                                    q16 = HD // 4
                                    for part in range(2):
                                        src = Z[:, t, :].rearrange("p (h f s d) -> p h f s d", f=2, s=2, d=q16)[:, :, :, 1 - part, :]
                                        dst = r2[:, :].rearrange("p (h f s d) -> p h f s d", f=2, s=2, d=q16)[:, :, :, part, :]
                                        tab = sin[:, t:t + 1, :].rearrange("p a (f s d) -> p a f s d", f=2, s=2)[:, :, :, part, :]
                                        dve_step(dve.tensor_tensor(dst, src, tab.to_broadcast([P, 8, 2, q16]), ALU.mult))
                                    dve_step(dve.tensor_tensor(outq, r1[:, t % 2, 0:384].rearrange("p (n g d) -> p n g d", n=2, d=HD),
                                                               r2[:, 0:384].rearrange("p (n g d) -> p n g d", n=2, d=HD), ALU.add))
                                    dve.tensor_tensor(outk, r1[:, t % 2, 384:512], r2[:, 384:512], ALU.add).then_inc(sem("a_rotated"), 1)

                                for t in range(NT + 1):
                                    if t < NT:
                                        dve.wait_ge(sem("a_squared"), t + 1)
                                        dve.tensor_reduce(ss[:, t, :], sq[:, t % 2, :].rearrange("p (h d) -> p h d", d=HD),
                                                          AX.X, ALU.add).then_inc(sem("a_squares_summed"), 1)
                                    if t >= 1:
                                        norm_and_rotate(t - 1)

                    units = []
                    for t in [PROMPT] + list(range(LAT)):
                        s = key_slot(t)
                        for h in range(6):
                            n = h // 3
                            rows = slice(n * HD, (n + 1) * HD)
                            if t == PROMPT:
                                keys, vs, nk = [(QK[rows, 3, s * P:(s + 1) * P], 0)], [s], P
                            else:
                                keys = [(QK[rows, 3, 0:512], 0), (QK[rows, 3, 512:1024], 512), (QK[rows, 3, 1024:1152], 1024)]
                                vs, nk = list(range(9)), 9 * P
                            units.append({"q": QK[rows, h % 3, s * P:(s + 1) * P], "keys": keys, "n": nk,
                                          "v": [V[:, x, :] for x in vs], "cols": rows, "bias": None,
                                          "out": mix[:, t, h * HD:(h + 1) * HD]})
                    tensor, scalar, vector, _, _, _ = attention("attn_a", units, own, 0)
                    with nc.Block() as block:
                        block.tensor(tensor)
                        block.scalar(scalar)
                        block.vector(vector)

                        @block.sync
                        def _(sp):
                            load_c_weights(sp, 0)
                            sp.wait_ge(sem("a_cache_stored"), 32)

            def mixer_c(pair):
                tag = f"c{pair}"
                with ExitStack() as own:
                    QK = sb(f"{tag}_qkT", [P, 2, NSLOT * P], own)
                    V = sb(f"{tag}_v", [P, NSLOT, P], own)
                    ctx_k = sb(f"{tag}_ctx_k", [P, P], own)
                    k_nat = sb(f"{tag}_k_prompt", [P, P], own)
                    T = sb(f"{tag}_bias", [P, 2, BIAS_U * GRID_W], own)
                    window = sb(f"{tag}_window", [P, WIN_TYPES, WIN], own)
                    slot = pair % 2
                    with nc.Block() as block:
                        @block.sync
                        def _(sp):
                            sp.dma_start(ctx_k[:, :], I["cache_k_nbhd"][l, :, pair * P:(pair + 1) * P]).then_inc(sem(f"{tag}_ctx_k_loaded"), 16)
                            sp.dma_start(V[:, CTX_SLOT, :], I["cache_v_nbhd"][l, :, pair * P:(pair + 1) * P]).then_inc(sem(f"{tag}_tables_loaded"), 16)
                            sp.dma_start(window[:, :, :], I["window"].rearrange("p (w n) -> p w n", w=WIN_TYPES)).then_inc(sem(f"{tag}_tables_loaded"), 16)
                            sp.wait_ge(bias_copied, 6 * DEPTH * 16)
                            for j in range(2):
                                by_column = bias_dram[l, 2 * pair + j, GRID_W - 1:GRID_W - 1 + GRID_W * (bias_pitch - 1)].rearrange("(c j) -> c j", c=GRID_W)
                                for r in range(2):
                                    rows = by_column[:, (1 - r) * BIAS_W:(1 - r + BIAS_U) * BIAS_W].rearrange("c (u k) -> c u k", k=BIAS_W)
                                    sp.dma_start(T[r * HD:(r + 1) * HD, j, :].rearrange("p (u k) -> p u k", k=GRID_W),
                                                 rows[:, :, 0:GRID_W]).then_inc(sem(f"{tag}_tables_loaded"), 16)
                            sp.wait_ge(sem(f"{tag}_v_copied"), NT)
                            sp.dma_start(O["new_v_nbhd"][l, :, pair * P:(pair + 1) * P], V[:, PROMPT_SLOT, :]).then_inc(sem(f"{tag}_cache_stored"), 16)
                            sp.wait_ge(sem(f"{tag}_k_prompt_copied"), 1)
                            sp.dma_start(O["new_k_nbhd"][l, :, pair * P:(pair + 1) * P], k_nat[:, :]).then_inc(sem(f"{tag}_cache_stored"), 16)
                            sp.wait_ge(sem(f"{tag}_tables_loaded"), 6 * 16)

                        @block.tensor
                        def _(pe):
                            for j in range(6):
                                m, n = j // 3, j % 3
                                if j >= 3:
                                    pe.wait_ge(sem(f"{tag}_qk_copied"), j - 2)
                                for k in range(KD):
                                    mm = pe.matmul(ps[:, j % 3, 0:384], ring[:, slot, k, m * P:(m + 1) * P], hT[:, k, n * 384:(n + 1) * 384],
                                                   start=(k == 0), stop=(k == KD - 1))
                                mm.then_inc(sem(f"{tag}_qk_projected"), 1)
                            for t in range(NT):
                                if t >= 3:
                                    pe.wait_ge(sem(f"{tag}_v_copied"), t - 2)
                                for k in range(KD):
                                    mm = pe.matmul(ps[:, 3 + t % 3, 0:P], hT[:, k, t * P:(t + 1) * P], ring[:, slot, k, 2 * P:3 * P],
                                                   start=(k == 0), stop=(k == KD - 1))
                                mm.then_inc(sem(f"{tag}_v_projected"), 1)
                            pe.wait_ge(sem(f"{tag}_ctx_k_loaded"), 16)
                            pe.transpose(ps[:, 6, 0:P], ctx_k[:, :], ident[:, :]).then_inc(sem(f"{tag}_ctx_turned"), 1)
                            pe.wait_ge(sem(f"{tag}_qk_copied"), 6)
                            pe.transpose(ps[:, 7, 0:P], QK[:, 1, PROMPT_SLOT * P:NSLOT * P], ident[:, :]).then_inc(sem(f"{tag}_k_prompt_turned"), 1)

                        @block.scalar
                        def _(act):
                            for j in range(6):
                                m, n = j // 3, j % 3
                                act.wait_ge(sem(f"{tag}_qk_projected"), j + 1)
                                s = SCALE if m == 0 else 1.0
                                if n < 2:
                                    act.mul(QK[:, m, n * 384:(n + 1) * 384], ps[:, j % 3, 0:384], s).then_inc(sem(f"{tag}_qk_copied"), 1)
                                else:
                                    act_step(act.mul(QK[:, m, 768:1024], ps[:, j % 3, 0:256], s))
                                    act.mul(QK[:, m, PROMPT_SLOT * P:NSLOT * P], ps[:, j % 3, 256:384], s).then_inc(sem(f"{tag}_qk_copied"), 1)
                            act.wait_ge(sem(f"{tag}_ctx_turned"), 1)
                            act.copy(QK[:, 1, CTX_SLOT * P:(CTX_SLOT + 1) * P], ps[:, 6, 0:P])
                            act.wait_ge(sem(f"{tag}_k_prompt_turned"), 1)
                            act.copy(k_nat[:, :], ps[:, 7, 0:P]).then_inc(sem(f"{tag}_k_prompt_copied"), 1)

                        @block.vector
                        def _(dve):
                            for t in range(NT):
                                dve.wait_ge(sem(f"{tag}_v_projected"), t + 1)
                                dve.tensor_copy(V[:, key_slot(t), :], ps[:, 3 + t % 3, 0:P]).then_inc(sem(f"{tag}_v_copied"), 1)

                    units = []
                    for t in [PROMPT] + list(range(LAT)):
                        s = key_slot(t)
                        for j in range(2):
                            rows = slice(j * HD, (j + 1) * HD)
                            w0 = window_start_row(t) * GRID_W if t != PROMPT else 0
                            if t == PROMPT:
                                keys, vs, nk = [(QK[rows, 1, s * P:(s + 1) * P], 0)], [s], P
                            else:
                                keys = [(QK[rows, 1, w0:w0 + 512], 0), (QK[rows, 1, w0 + 512:w0 + WIN], 512),
                                        (QK[rows, 1, CTX_SLOT * P:(CTX_SLOT + 1) * P], WIN)]
                                vs, nk = [w0 // P + x for x in range(WIN // P)] + [CTX_SLOT], WIN + P
                            units.append({"q": QK[rows, 0, s * P:(s + 1) * P], "keys": keys, "n": nk,
                                          "v": [V[:, x, :] for x in vs], "cols": rows,
                                          "bias": None if t == PROMPT else (t, j),
                                          "out": mix[:, t, 640 + (2 * pair + j) * HD:640 + (2 * pair + j + 1) * HD]})
                    tensor, scalar, vector, biased, bias_ready, max_ready = attention(f"attn_{tag}", units, own, WIN + P)
                    with nc.Block() as block:
                        block.tensor(tensor)
                        block.scalar(scalar)
                        block.vector(vector)

                        @block.sync
                        def _(sp):
                            if pair < 2:
                                load_c_weights(sp, pair + 1)
                            else:
                                load_cuts(sp, B_CUTS[:2])
                            sp.wait_ge(sem(f"{tag}_cache_stored"), 32)

                        @block.gpsimd
                        def _(pool):
                            pool_step(pool.memset(biased[:, :, WIN:WIN + P], 0.0))
                            for i, u in enumerate(units):
                                if u["bias"] is None:
                                    continue
                                t, j = u["bias"]
                                if u["bias_n"] > 2:
                                    pool.wait_ge(max_ready, i - 1)
                                u0 = window_start_row(t) - 2 * t + NA_ROWS
                                pool.tensor_tensor(biased[:, u["bias_n"] % 2, 0:WIN], T[:, j, u0 * GRID_W:u0 * GRID_W + WIN],
                                                   window[:, window_type(t), :], ALU.add).then_inc(bias_ready, 1)

            def mixer_b():
                with ExitStack() as own:
                    qT = sb("b_qT", [P, 2, TOK], own)
                    kT = sb("b_kT", [P, 2, 2, TOK], own)
                    K = sb("b_k", [P, NT, 256], own)
                    OG = sb("b_og", [P, NT, 272], own)
                    V = sb("b_v", [P, NT, 4, VA], own)
                    HB = sb("b_h_backward", [P, NT, 256], own)
                    cols = sb("b_columns", [P, 4, 2, NT, 4], own)
                    decay = sb("b_decay", [P, 2, 2, NT], own)
                    state = sb("b_state", [P, 2, 2, 2 * VA], own)
                    state_p = sb("b_state_prompt", [P, 2, 2, 2 * VA], own)
                    gn = sb("b_out_norm", [P, 256], own)
                    cuts = B_CUTS
                    gbias = small[:, 96:112]

                    with nc.Block() as block:
                        @block.sync
                        def _(sp):
                            sp.dma_start(gbias, I["gate_bias"][bass.ds(l, 1), :].to_broadcast([P, 16])).then_inc(sem("b_rows_loaded"), 16)
                            sp.dma_start(gn[:, :], I["out_norm"][bass.ds(l, 1), :].to_broadcast([P, 256])).then_inc(sem("b_rows_loaded"), 16)
                            for c in (2, 3):
                                o, n = cuts[c]
                                sp.wait_ge(sem("b_w_used"), c - 1)
                                sp.dma_start(ring[:, c % 2, :, 0:n], w_in[:, :, o:o + n]).then_inc(sem(f"b_w_loaded{c}"), 16)
                            sp.wait_ge(sem("b_state_cleared"), 1)
                            for d in range(2):
                                for h in range(4):
                                    pr, j = h // 2, h % 2
                                    rows = slice(j * HD, (j + 1) * HD)
                                    sp.dma_start(state[rows, d, pr, j * VA:j * VA + HD], I["state_C"][l, d, h]).then_inc(sem("b_state_loaded"), 16)
                                    sp.dma_start(state[rows, d, pr, j * VA + HD:(j + 1) * VA], I["state_n"][l, d, h]).then_inc(sem("b_state_loaded"), 16)
                            sp.wait_ge(sem("b_rows_loaded"), 32)
                            sp.wait_ge(sem("b_state_loaded"), 16 * 16)

                        @block.gpsimd
                        def _(pool):
                            pool_step(pool.memset(state[:, :, :, :], 0.0))
                            pool.sem_inc(sem("b_state_cleared"), 1)
                            pool_step(pool.memset(state_p[:, :, :, :], 0.0))
                            pool_step(pool.memset(kT[HD:P, :, 0, :], 0.0))
                            pool_step(pool.memset(kT[0:HD, :, 1, :], 0.0))
                            pool_step(pool.memset(V[:, :, :, HD:VA], 1.0))

                        @block.tensor
                        def _(pe):
                            for j in range(6):
                                m, n = j // 3, j % 3
                                if j >= 4:
                                    pe.wait_ge(sem("b_copied"), j - 3)
                                for k in range(KD):
                                    mm = pe.matmul(ps[:, j % 4, 0:384], ring[:, 0, k, m * P:(m + 1) * P], hT[:, k, n * 384:(n + 1) * 384],
                                                   start=(k == 0), stop=(k == KD - 1))
                                mm.then_inc(sem("b_projected"), 1)
                            pe.wait_ge(sem("b_projected"), 6)
                            pe.sem_inc(sem("b_w_used"), 1)
                            for c in range(1, 4):
                                if c >= 2:
                                    pe.wait_ge(sem(f"b_w_loaded{c}"), 16)
                                n = cuts[c][1]
                                for t in range(NT):
                                    j = 6 + (c - 1) * NT + t
                                    pe.wait_ge(sem("b_copied"), j - 3)
                                    for k in range(KD):
                                        mm = pe.matmul(ps[:, j % 4, 0:n], hT[:, k, t * P:(t + 1) * P], ring[:, c % 2, k, 0:n],
                                                       start=(k == 0), stop=(k == KD - 1))
                                    mm.then_inc(sem("b_projected"), 1)
                                    if c == 3:
                                        pe.wait_ge(sem("b_copied"), 6 + NT + t + 1)
                                        if t >= 2:
                                            pe.wait_ge(sem("b_kT_copied"), t - 1)
                                        for m in range(2):
                                            mm = pe.transpose(ps[:, 4 + t % 2, m * P:(m + 1) * P], K[:, t, m * P:(m + 1) * P], ident[:, :])
                                        mm.then_inc(sem("b_k_turned"), 1)
                                pe.wait_ge(sem("b_projected"), 6 + c * NT)
                                pe.sem_inc(sem("b_w_used"), 1)

                        @block.scalar
                        def _(act):
                            for j in range(6 + 3 * NT):
                                act.wait_ge(sem("b_projected"), j + 1)
                                if j < 6:
                                    m, n = j // 3, j % 3
                                    a = act.copy(qT[:, m, n * 384:(n + 1) * 384], ps[:, j % 4, 0:384])
                                else:
                                    c, t = (j - 6) // NT + 1, (j - 6) % NT
                                    if c == 1:
                                        a = act.copy(OG[:, t, :], ps[:, j % 4, 0:272])
                                    elif c == 2:
                                        a = act.mul(K[:, t, :], ps[:, j % 4, 0:256], SCALE)
                                    else:
                                        a = act.copy(V[:, t, :, 0:HD], ps[:, j % 4, 0:256].rearrange("p (h d) -> p h d", d=HD))
                                a.then_inc(sem("b_copied"), 1)
                                if 6 + NT <= j < 6 + 2 * NT:
                                    act.wait_ge(sem("b_copied"), 6 + t + 1)
                                    act.activation(OG[:, t, 0:256], OG[:, t, 0:256], ACT.Exp, scale=-1.0).then_inc(sem("b_sigmoid_exp"), 1)

                        @block.vector
                        def _(dve):
                            o = OG[:, :, 0:256]
                            dve.wait_ge(sem("b_rows_loaded"), 32)
                            dve.wait_ge(sem("b_sigmoid_exp"), NT)
                            dve_step(dve.tensor_scalar(o, o, 1.0, None, ALU.add))
                            dve_step(dve.reciprocal(o, o))
                            dve_step(dve.tensor_tensor(o, o, gn[:, :].unsqueeze(1).to_broadcast([P, NT, 256]), ALU.mult))
                            for t in range(NT):
                                dve.wait_ge(sem("b_k_turned"), t + 1)
                                for j in range(2):
                                    rows = slice(j * HD, (j + 1) * HD)
                                    a = dve.tensor_copy(kT[rows, :, j, t * P:(t + 1) * P], ps[rows, 4 + t % 2, 0:256].rearrange("p (m n) -> p m n", m=2))
                                a.then_inc(sem("b_kT_copied"), 1)

                    hflat = hT[:, :, :].rearrange("p k t -> p (k t)")

                    def rows_of(i):
                        return hflat[0:36, i * TOK:(i + 1) * TOK]
                    B_, A_, M_, WI, AE, FA, FM = (rows_of(i) for i in range(7))
                    LF = B_
                    small_rows = hflat[0:36, 7 * TOK:7 * TOK + 64]
                    m_in = small_rows[:, 0:NT]
                    m_out = small_rows[:, 16:16 + NT]
                    dec = small_rows[:, 32:32 + NT]
                    a_max = small_rows[:, 48:48 + NT]
                    b_last = hflat[0:36, 7 * TOK + 104:7 * TOK + 104 + NT]
                    dec_diag = hflat[0:36, 7 * TOK + 64:7 * TOK + 64 + 4 * NT]
                    gI = hflat[:, 7 * TOK + 128:7 * TOK + 128 + 9 * 36].rearrange("p (t c) -> p t c", c=36)
                    gF = hflat[:, 7 * TOK + 128 + 9 * 36:7 * TOK + 128 + 18 * 36].rearrange("p (t c) -> p t c", c=36)
                    with ExitStack() as inner:
                        raw = sb("b_gates", [P, NT, 16], inner)
                        e1 = sb("b_gate_e", [P, NT, 8], inner)
                        more = HB[:, :, :].rearrange("p t n -> p (t n)")
                        FW, carry_limit = more[0:36, 0:TOK], more[0:36, TOK:2 * TOK]
                        mods = Modulation("mlp_mods", (3, 4, 2, 5),
                                          ring[:, :, :, :].rearrange("p a k n -> p (a k n)").rearrange("p (r k n) -> p r k n", k=KD, n=Modulation.CHUNK), inner)
                        with nc.Block() as block:
                            @block.sync
                            def _(sp):
                                mods.load_gain(sp)
                                for c in range(mods.ring):
                                    mods.load(sp, c)
                                sp.wait_ge(sem("b_m_cleared"), 1)
                                for d in range(2):
                                    sp.dma_start(m_in[32 * d:32 * d + 4, 0:1], I["state_m"][l, d]).then_inc(sem("b_m0_loaded"), 16)
                                for c in range(mods.ring, mods.n):
                                    mods.load(sp, c)
                                sp.wait_ge(sem("b_m0_loaded"), 32)
                                sp.wait_ge(sem("b_stabiliser_done"), 1)
                                for d in range(2):
                                    sp.dma_start(O["new_m"][l, d], m_out[32 * d:32 * d + 4, PROMPT:NT]).then_inc(sem("b_m_stored"), 16)
                                sp.wait_ge(sem("b_m_stored"), 32)

                            @block.gpsimd
                            def _(pool):
                                pool_step(pool.memset(hflat[:, 7 * TOK:8 * TOK], 0.0))
                                pool.sem_inc(sem("b_m_cleared"), 1)
                                for i in (2, 0, 1, 3, 4):
                                    pool_step(pool.memset(rows_of(i), 0.0))
                                pool_step(pool.memset(FW, 0.0))
                                pool_step(pool.memset(hflat[:, 6 * TOK:7 * TOK], 0.0))
                                pool.sem_inc(sem("b_rows_cleared"), 1)
                                pool_step(pool.memset(FA, 1.0))
                                pool_step(pool.memset(FA.rearrange("p (t n) -> p t n", n=P)[:, :, 0:1], 0.0))
                                pool_step(pool.tensor_scalar(carry_limit, FA, 2e38, -1e38, ALU.mult, ALU.add))
                                pool.sem_inc(sem("b_carry_ready"), 1)
                                mods.scale_gate_rows(pool)

                            @block.scalar
                            def _(act):
                                act.wait_ge(sem("b_gate_abs"), 1)
                                act_step(act.activation(e1[:, :, :], e1[:, :, :], ACT.Exp, scale=-1.0))
                                act.activation(e1[:, :, :], e1[:, :, :], ACT.Ln, bias=1.0).then_inc(sem("b_gate_ln"), 1)
                                for c in range(6):
                                    mods.scalar_step(act, c)
                                act.wait_ge(sem("b_arguments"), 1)
                                act_step(act.activation(WI, WI, ACT.Exp))
                                act_step(act.activation(AE, AE, ACT.Exp))
                                act_step(act.activation(B_, B_, ACT.Exp))
                                act_step(act.activation(dec, dec, ACT.Exp))
                                act.sem_inc(sem("b_exponentials"), 1)
                                for c in range(6, mods.n + 1):
                                    mods.scalar_step(act, c)

                            @block.vector
                            def _(dve):
                                dve_step(dve.tensor_tensor(raw[:, :, :], OG[:, :, 256:272], gbias.unsqueeze(1).to_broadcast([P, NT, 16]), ALU.add))
                                r4 = raw[:, :, :].rearrange("p t (d g h) -> p t d g h", d=2, g=2)
                                e4 = e1[:, :, :].rearrange("p t (d h) -> p t d h", d=2)
                                dve_step(dve.scalar_tensor_tensor(e4, r4[:, :, :, 1, :], -1.0, r4[:, :, :, 1, :], ALU.mult, ALU.max))
                                dve.sem_inc(sem("b_gate_abs"), 1)
                                dve.wait_ge(sem("b_gate_ln"), 1)
                                dve.wait_ge(sem("b_m_cleared"), 1)
                                for d in range(2):
                                    dve_step(dve.tensor_copy(gI[:, :, 32 * d:32 * d + 4], r4[:, :, d, 0, :]))
                                    dve_step(dve.scalar_tensor_tensor(gF[:, :, 32 * d:32 * d + 4], r4[:, :, d, 1, :], 0.0, e4[:, :, d, :],
                                                                      ALU.min, ALU.subtract))
                                dve.sem_inc(sem("b_gates_ready"), 1)
                                dve.wait_ge(sem("b_gates_turned"), 1)
                                dve.wait_ge(sem("b_rows_cleared"), 1)
                                for i, dst in enumerate((A_, LF)):
                                    src = psf[0:36, i * TOK:(i + 1) * TOK]
                                    dve_step(dve.tensor_copy(dst[0:4, :], src[0:4, :]))
                                    for a, z in ((0, LAT * P), (LAT * P, TOK)):
                                        dve_step(dve.tensor_copy(dst[32:36, a:z], src[32:36, a:z][:, ::-1]))
                                dve.wait_ge(sem("b_m0_loaded"), 32)
                                dve.wait_ge(sem("b_carry_ready"), 1)
                                dve_step(dve.tensor_tensor_scan(B_, FA, LF, 0.0, ALU.mult, ALU.add))
                                dve_step(dve.tensor_tensor(A_, A_, B_, ALU.subtract))
                                in_chunks = [x.rearrange("p (t n) -> p t n", n=P) for x in (A_, B_, WI)]
                                dve_step(dve.tensor_reduce(a_max, in_chunks[0], AX.X, ALU.max))
                                dve_step(dve.tensor_copy(b_last, in_chunks[1][:, :, P - 1]))
                                dve_step(dve.tensor_tensor_scan(m_out[:, 0:LAT], a_max[:, 0:LAT], b_last[:, 0:LAT], m_in[:, 0:1], ALU.max, ALU.add))
                                dve_step(dve.tensor_tensor_scan(m_out[:, LAT:NT], a_max[:, LAT:NT], b_last[:, LAT:NT], 0.0, ALU.max, ALU.add))
                                dve_step(dve.tensor_copy(m_in[:, 1:LAT], m_out[:, 0:LAT - 1]))
                                dve_step(dve.tensor_copy(WI, A_))
                                dve_step(dve.tensor_tensor(in_chunks[2][:, :, 0], in_chunks[0][:, :, 0], m_in, ALU.max))
                                dve_step(dve.tensor_tensor_scan(M_, carry_limit, WI, 0.0, ALU.min, ALU.max))
                                dve.sem_inc(sem("b_stabiliser_done"), 1)
                                M3, A3, W3, E3 = (x.rearrange("p (t n) -> p t n", n=P) for x in (M_, A_, WI, AE))
                                mlast = M3[:, :, P - 1]
                                dve_step(dve.tensor_tensor(W3, m_in.unsqueeze(2).to_broadcast([36, NT, P]), M3, ALU.subtract))
                                dve_step(dve.tensor_tensor(E3, A3, mlast.unsqueeze(2).to_broadcast([36, NT, P]), ALU.subtract))
                                dve_step(dve.scalar_tensor_tensor(B_, B_, -1.0, M_, ALU.mult, ALU.subtract))
                                dve_step(dve.tensor_tensor(dec, m_in, mlast, ALU.subtract))
                                dve.sem_inc(sem("b_arguments"), 1)

                                def in_token_order(dst, src):
                                    dve_step(dve.tensor_copy(dst[0:4, :], src[0:4, :]))
                                    for a, z in ((0, LAT * P), (LAT * P, TOK)):
                                        dve_step(dve.tensor_copy(dst[32:36, a:z], src[32:36, a:z][:, ::-1]))
                                in_token_order(FA, A_)
                                in_token_order(FM, M_)
                                dve.wait_ge(sem("b_exponentials"), 1)
                                in_token_order(FW, WI)
                                in_token_order(A_, AE)
                                in_token_order(M_, B_)
                                dve_step(dve.tensor_tensor(dec_diag.rearrange("p (j c) -> p j c", j=4), diagonal[:, :, :],
                                                           dec.unsqueeze(1).to_broadcast([36, 4, NT]), ALU.mult))
                                dve.sem_inc(sem("b_rows_ready"), 1)
                                dve.wait_ge(sem("b_columns_turned"), 2)
                                for q in range(4):
                                    for d in range(2):
                                        dve.tensor_copy(cols[:, q, d, :, :],
                                                        ps[:, q, 0:36 * NT].rearrange("p (t h) -> p t h", t=NT)[:, :, 32 * d:32 * d + 4])
                                for d in range(2):
                                    src = ps[:, 4, d * 64:d * 64 + 4 * NT].rearrange("p (j c) -> p j c", j=4)
                                    for j in range(2):
                                        rows = slice(j * HD, (j + 1) * HD)
                                        dve.tensor_copy(decay[rows, d, :, :], src[rows, j:4:2, :])

                            @block.tensor
                            def _(pe):
                                pe.wait_ge(sem("b_gates_ready"), 1)
                                for i, g_ in enumerate((gI, gF)):
                                    for t in range(NT):
                                        mm = pe.transpose(psf[0:36, i * TOK + t * P:i * TOK + (t + 1) * P], g_[:, t, :], ident[:, :])
                                mm.then_inc(sem("b_gates_turned"), 1)
                                for c in range(11):
                                    mods.tensor_step(pe, c)
                                pe.wait_ge(sem("b_rows_ready"), 1)
                                for q, src in enumerate((FA, FW, M_, A_)):
                                    for t in range(NT):
                                        pe.transpose(ps[:, q, t * 36:(t + 1) * 36], src[:, t * P:(t + 1) * P], ident[0:36, 0:36])
                                for d in range(2):
                                    r = slice(32 * d, 32 * d + 4)
                                    if d == 1:
                                        pe.wait_ge(sem("b_columns_turned"), 1)
                                    pe.matmul(ps[:, 4, d * 64:d * 64 + 4 * NT], ones[r, :], dec_diag[r, :], start=True, stop=True).then_inc(sem("b_columns_turned"), 1)
                                for c in range(11, mods.n):
                                    mods.tensor_step(pe, c)

                    E4 = sb("b_e", [P, 2, 512], own)
                    W4 = sb("b_w", [P, 2, 512], own)
                    J4 = sb("b_inter", [P, 2, 4 * VA], own)
                    N4 = sb("b_num", [P, 2, 4 * VA], own)
                    KS = sb("b_ks", [P, 2, 256], own)
                    dn = small[:, 112:116]
                    rdn = small[:, 116:120]
                    work = []
                    for c in range(LAT):
                        work += [(0, c, c), (1, LAT - 1 - c, c)]
                    work += [(0, PROMPT, PROMPT), (1, PROMPT, PROMPT)]
                    nw = len(work)
                    qA, qWI, qEM, qAE = range(4)
                    m_rows = hflat[:, 6 * TOK:7 * TOK]
                    with nc.Block() as block:
                        @block.tensor
                        def _(pe):
                            def scores(i):
                                d, t, c = work[i]
                                tt = slice(t * P, (t + 1) * P)
                                if i >= 2:
                                    pe.wait_ge(sem("b_weighted"), i - 1)
                                for h in range(4):
                                    mm = pe.matmul(ps[:, i % 2, h * P:(h + 1) * P], kT[:, h // 2, h % 2, tt], qT[:, h // 2, tt], start=True, stop=True)
                                mm.then_inc(sem("b_scores"), 1)
                                if i >= 1:
                                    pe.wait_ge(sem("b_masked"), i)
                                for h in range(4):
                                    mm = pe.matmul(ps[:, 2, h * P:(h + 1) * P], neg_select[:, d, h, :], m_rows[:, tt], start=True, stop=True)
                                mm.then_inc(sem("b_stabiliser_spread"), 1)

                            def apply(i):
                                d, t, c = work[i]
                                st = state_p if t == PROMPT else state
                                tt = slice(t * P, (t + 1) * P)
                                if i >= 2:
                                    pe.wait_ge(sem("b_combined"), i - 1)
                                    pe.wait_ge(sem("b_state_new"), i - 1)
                                for pr in range(2):
                                    mm = pe.matmul(ps[:, 3 + i % 2, pr * 2 * VA:(pr + 1) * 2 * VA], qT[:, pr, tt], st[:, d, pr, :], start=True, stop=True)
                                mm.then_inc(sem("b_inter_done"), 1)
                                pe.wait_ge(sem("b_weighted"), i + 1)
                                for h in range(4):
                                    mm = pe.matmul(ps[:, 5 + i % 2, h * VA:(h + 1) * VA], W4[:, i % 2, h * P:(h + 1) * P], V[:, t, h, :], start=True, stop=True)
                                mm.then_inc(sem("b_applied"), 1)
                                pe.wait_ge(sem("b_keys_scaled"), i + 1)
                                if i >= 1:
                                    pe.wait_ge(sem("b_state_new"), i)
                                for pr in range(2):
                                    mm = pe.matmul(ps[:, 7, pr * 2 * VA:(pr + 1) * 2 * VA], KS[:, i % 2, pr * P:(pr + 1) * P],
                                                   V[:, t, 2 * pr:2 * pr + 2, :].rearrange("p h d -> p (h d)"), start=True, stop=True)
                                mm.then_inc(sem("b_updated"), 1)
                            scores(0)
                            for i in range(nw):
                                if i + 1 < nw:
                                    scores(i + 1)
                                apply(i)

                        @block.scalar
                        def _(act):
                            for i, (d, t, c) in enumerate(work):
                                act.wait_ge(sem("b_masked"), i + 1)
                                for h in range(4):
                                    a = act.activation(E4[:, i % 2, h * P:(h + 1) * P], E4[:, i % 2, h * P:(h + 1) * P], ACT.Exp,
                                                       bias=cols[:, qA, d, t, h:h + 1])
                                a.then_inc(sem("b_exp"), 1)
                                act.wait_ge(sem("b_inter_done"), i + 1)
                                if i >= 2:
                                    act.wait_ge(sem("b_combined"), i - 1)
                                for h in range(4):
                                    a = act.mul(J4[:, i % 2, h * VA:(h + 1) * VA], ps[:, 3 + i % 2, h * VA:(h + 1) * VA], cols[:, qWI, d, t, h:h + 1])
                                a.then_inc(sem("b_inter_scaled"), 1)

                        @block.gpsimd
                        def _(pool):
                            for i, (d, t, c) in enumerate(work):
                                if i >= 2:
                                    pool.wait_ge(sem("b_updated"), i - 1)
                                pool.tensor_tensor(KS[:, i % 2, :].rearrange("p (h d) -> p h d", d=HD), K[:, t, :].rearrange("p (h d) -> p h d", d=HD),
                                                   cols[:, qAE, d, t, :].unsqueeze(2).to_broadcast([P, 4, HD]), ALU.mult).then_inc(sem("b_keys_scaled"), 1)

                        @block.vector
                        def _(dve):
                            def mask(i):
                                d, t, c = work[i]
                                dve.wait_ge(sem("b_stabiliser_spread"), i + 1)
                                if i >= 2:
                                    dve.wait_ge(sem("b_weighted"), i - 1)
                                dve.tensor_tensor(E4[:, i % 2, :].rearrange("p (h t) -> p h t", h=4), ps[:, 2, :].rearrange("p (h t) -> p h t", h=4),
                                                  causal[:, d:d + 1, :].to_broadcast([P, 4, P]), ALU.add).then_inc(sem("b_masked"), 1)

                            def weight(i):
                                dve.wait_ge(sem("b_exp"), i + 1)
                                if i >= 2:
                                    dve.wait_ge(sem("b_applied"), i - 1)
                                dve.tensor_tensor(W4[:, i % 2, :], ps[:, i % 2, :], E4[:, i % 2, :], ALU.mult).then_inc(sem("b_weighted"), 1)

                            def finish(i):
                                d, t, c = work[i]
                                N3 = N4[:, i % 2, :].rearrange("p (h d) -> p h d", d=VA)
                                dve.wait_ge(sem("b_inter_scaled"), i + 1)
                                dve.wait_ge(sem("b_applied"), i + 1)
                                dve.tensor_tensor(N4[:, i % 2, :], ps[:, 5 + i % 2, 0:4 * VA], J4[:, i % 2, :], ALU.add).then_inc(sem("b_combined"), 1)
                                dve.wait_ge(sem("b_updated"), i + 1)
                                st = state_p if t == PROMPT else state
                                for pr in range(2):
                                    for j in range(2):
                                        rows, cc = slice(j * HD, (j + 1) * HD), slice(j * VA, (j + 1) * VA)
                                        o = pr * 2 * VA
                                        a = dve.scalar_tensor_tensor(st[rows, d, pr, cc], st[rows, d, pr, cc], decay[rows, d, pr, c:c + 1],
                                                                     ps[rows, 7, o + j * VA:o + (j + 1) * VA], ALU.mult, ALU.add)
                                a.then_inc(sem("b_state_new"), 1)
                                dve.wait_ge(sem("b_combined"), i + 1)
                                dve_step(dve.scalar_tensor_tensor(dn, N3[:, :, HD], -1.0, N3[:, :, HD], ALU.mult, ALU.max))
                                dve_step(dve.tensor_tensor(dn, dn, cols[:, qEM, d, t, :], ALU.max))
                                dve_step(dve.reciprocal(rdn, dn))
                                dst = (HB[:, t, :] if d else mix[:, t, 384:640]).rearrange("p (h d) -> p h d", d=HD)
                                dve_step(dve.tensor_tensor(dst, N3[:, :, 0:HD], rdn.unsqueeze(2).to_broadcast([P, 4, HD]), ALU.mult))

                            mask(0)
                            for i in range(nw):
                                if i + 1 < nw:
                                    mask(i + 1)
                                weight(i)
                                if i >= 1:
                                    finish(i - 1)
                            finish(nw - 1)

                    with nc.Block() as block:
                        h = mix[:, :, 384:640]
                        h4 = h.rearrange("p t (h d) -> p t h d", d=HD)
                        ss = small[:, 120:120 + 4 * NT].rearrange("p (t h) -> p t h", h=4)
                        rs = small[:, 160:160 + 4 * NT].rearrange("p (t h) -> p t h", h=4)
                        @block.sync
                        def _(sp):
                            for d in range(2):
                                for h in range(4):
                                    pr, j = h // 2, h % 2
                                    rows = slice(j * HD, (j + 1) * HD)
                                    sp.dma_start(O["new_C"][l, d, h], state_p[rows, d, pr, j * VA:j * VA + HD]).then_inc(sem("b_state_stored"), 16)
                                    sp.dma_start(O["new_n"][l, d, h], state_p[rows, d, pr, j * VA + HD:(j + 1) * VA]).then_inc(sem("b_state_stored"), 16)
                            sp.wait_ge(sem("b_state_stored"), 16 * 16)

                        squares = hflat[:, 0:NT * 256].rearrange("p (t d) -> p t d", d=256)

                        @block.scalar
                        def _(act):
                            act.wait_ge(sem("b_directions_added"), 1)
                            act.activation(squares, h, ACT.Square).then_inc(sem("b_out_squared"), 1)

                        @block.gpsimd
                        def _(pool):
                            pool.wait_ge(sem("b_out_summed"), 1)
                            pool_step(pool.tensor_scalar(rs, ss, 1.0 / HD, EPS, ALU.mult, ALU.add))
                            pool_step(pool.tensor_tensor(rs, rs, minus_half[:, 0:4 * NT].rearrange("p (t h) -> p t h", h=4), ALU.pow))
                            pool.sem_inc(sem("b_out_rstd"), 1)

                        @block.vector
                        def _(dve):
                            dve.tensor_tensor(h, h, HB[:, :, :], ALU.add).then_inc(sem("b_directions_added"), 1)
                            dve.wait_ge(sem("b_out_squared"), 1)
                            dve.tensor_reduce(ss, squares.rearrange("p t (h d) -> p t h d", d=HD), AX.X, ALU.add).then_inc(sem("b_out_summed"), 1)
                            dve_step(dve.tensor_tensor(h, h, OG[:, :, 0:256], ALU.mult))
                            dve.wait_ge(sem("b_out_rstd"), 1)
                            for t in range(NT):
                                dve.tensor_tensor(h4[:, t, :, :], h4[:, t, :, :], rs[:, t, :].unsqueeze(2).to_broadcast([P, 4, HD]), ALU.mult)

            def out_projection():
                CUT = 256
                NCUT = D // CUT
                w_out = I["w_out"][l].rearrange("(k p) n -> p k n", p=P)
                with ExitStack() as own:
                    raw = sb("w_out_raw", [P, 2, KD, CUT], own)
                    w_hi = sb("w_out_hi", [P, 2, KD, CUT], own, F32R)
                    w_lo = sb("w_out_lo", [P, 2, KD, CUT], own, F32R)
                    with nc.Block() as block:
                        @block.sync
                        def _(sp):
                            for c in range(NCUT):
                                if c >= 2:
                                    sp.wait_ge(sem("o_w_lo"), c - 1)
                                sp.dma_start(raw[:, c % 2, :, :], w_out[:, :, c * CUT:(c + 1) * CUT]).then_inc(sem(f"o_w_loaded{c % 2}"), 16)

                        @block.tensor
                        def _(pe):
                            for t in range(NT):
                                if t >= 2:
                                    pe.wait_ge(sem("o_mix_lo"), t - 1)
                                for k in range(KD):
                                    mm = pe.transpose(psf[:, t % 2 * 1024 + k * P:t % 2 * 1024 + (k + 1) * P], mix[:, t, k * P:(k + 1) * P], ident[:, :])
                                mm.then_inc(sem("o_mix_turned"), 1)
                            for c in range(NCUT):
                                pe.wait_ge(sem("o_w_lo"), c + 1)
                                for t in range(NT):
                                    j = c * NT + t
                                    if c == 0:
                                        pe.wait_ge(sem("o_mix_lo"), t + 1)
                                    if j >= 4:
                                        pe.wait_ge(sem("o_copied"), j - 3)
                                    tt = slice(t * P, (t + 1) * P)
                                    for k in range(KD):
                                        for a, b in ((hi, w_hi), (hi, w_lo), (lo, w_hi)):
                                            mm = pe.matmul(ps[:, 4 + j % 4, 0:CUT], a[:, k, tt], b[:, c % 2, k, :],
                                                           start=(k == 0 and a is hi and b is w_hi), stop=(k == KD - 1 and a is lo))
                                    mm.then_inc(sem("o_projected"), 1)

                        @block.vector
                        def _(dve):
                            def weights(c):
                                dve.wait_ge(sem("o_w_hi"), c + 1)
                                dve.tensor_tensor(w_lo[:, c % 2, :, :], raw[:, c % 2, :, :], w_hi[:, c % 2, :, :].bitcast(F32),
                                                  ALU.subtract).then_inc(sem("o_w_lo"), 1)
                            weights(0)
                            for t in range(NT):
                                tt = slice(t * P, (t + 1) * P)
                                dve.wait_ge(sem("o_mix_hi"), t + 1)
                                dve.tensor_tensor(lo[:, :, tt], psf[:, t % 2 * 1024:t % 2 * 1024 + 1024].rearrange("p (k n) -> p k n", n=P),
                                                  hi[:, :, tt].bitcast(F32), ALU.subtract).then_inc(sem("o_mix_lo"), 1)
                            for c in range(1, NCUT):
                                weights(c)

                        @block.scalar
                        def _(act):
                            def weights(c):
                                act.wait_ge(sem(f"o_w_loaded{c % 2}"), 16 * (c // 2 + 1))
                                if c >= 2:
                                    act.wait_ge(sem("o_projected"), (c - 1) * NT)
                                act.copy(w_hi[:, c % 2, :, :], raw[:, c % 2, :, :]).then_inc(sem("o_w_hi"), 1)
                            weights(0)
                            for t in range(NT):
                                act.wait_ge(sem("o_mix_turned"), t + 1)
                                act.copy(hi[:, :, t * P:(t + 1) * P],
                                         psf[:, t % 2 * 1024:t % 2 * 1024 + 1024].rearrange("p (k n) -> p k n", n=P)).then_inc(sem("o_mix_hi"), 1)
                            weights(1)
                            for j in range(NCUT * NT):
                                c, t = j // NT, j % NT
                                act.wait_ge(sem("o_projected"), j + 1)
                                act.copy(mix[:, t, c * CUT:(c + 1) * CUT], ps[:, 4 + j % 4, 0:CUT]).then_inc(sem("o_copied"), 1)
                                if t == NT - 1 and 1 <= c + 1 and c + 2 < NCUT:
                                    weights(c + 2)

            def mlp():
                NG = D_FF // HID
                KH = HID // P
                UP = 3 * KH
                DOWN = 2 * NT
                w_up = I["w_ffn_up"][l].rearrange("(k p) n -> p k n", p=P)
                w_down = I["w_ffn_down"][l].rearrange("(g k p) n -> g p k n", p=P, k=KH)
                with ExitStack() as own:
                    raw_up = sb("w_up_raw", [P, KD, HID], own)
                    raw_down = sb("w_down_raw", [P, KH, D], own)
                    up_hi, up_lo = (sb(f"w_up_{x}", [P, KD, HID], own, F32R) for x in ("hi", "lo"))
                    down_hi, down_lo = (sb(f"w_down_{x}", [P, KH, D], own, F32R) for x in ("hi", "lo"))
                    u_hi, u_lo = (sb(f"u_{x}", [P, KH, TOK], own, F32R) for x in ("hi", "lo"))
                    relu = sb("relu", [P, 2, 384], own)
                    square = sb("square", [P, 2, 384], own)
                    with nc.Block() as block:
                        @block.sync
                        def _(sp):
                            for g in range(NG):
                                if g >= 1:
                                    sp.wait_ge(sem("m_up_lo"), g)
                                sp.dma_start(raw_up[:, :, :], w_up[:, :, g * HID:(g + 1) * HID]).then_inc(sem("m_up_loaded"), 16)
                                if g >= 1:
                                    sp.wait_ge(sem("m_down_lo"), g)
                                sp.dma_start(raw_down[:, :, :], w_down[g]).then_inc(sem("m_down_loaded"), 16)

                        @block.gpsimd
                        def _(pool):
                            pool.memset(mix[:, :, :], 0.0).then_inc(sem("m_out_cleared"), 1)
                            with pool.Fori(0, NG) as g:
                                pool.wait_ge(sem("m_up_hi"), g + 1)
                                pool.tensor_tensor(up_lo[:, :, :], raw_up[:, :, :], up_hi[:, :, :].bitcast(F32), ALU.subtract).then_inc(sem("m_up_lo"), 1)
                                pool.wait_ge(sem("m_down_hi"), g + 1)
                                pool.tensor_tensor(down_lo[:, :, :], raw_down[:, :, :], down_hi[:, :, :].bitcast(F32), ALU.subtract).then_inc(sem("m_down_lo"), 1)

                        @block.tensor
                        def _(pe):
                            with pe.Fori(0, NG) as g:
                                pe.wait_ge(sem("m_up_lo"), g + 1)
                                for j in range(UP):
                                    n, m = j // KH, j % KH
                                    if j >= 3:
                                        pe.wait_ge(sem("m_relu"), g * UP + j - 2)
                                    for k in range(KD):
                                        for a, b in ((up_hi, hi), (up_hi, lo), (up_lo, hi)):
                                            mm = pe.matmul(ps[:, j % 3, 0:384], a[:, k, m * P:(m + 1) * P], b[:, k, n * 384:(n + 1) * 384],
                                                           start=(k == 0 and a is up_hi and b is hi), stop=(k == KD - 1 and a is up_lo))
                                    mm.then_inc(sem("m_up_done"), 1)
                                pe.wait_ge(sem("m_down_lo"), g + 1)
                                pe.wait_ge(sem("m_added"), g * DOWN)
                                for j in range(DOWN):
                                    t, n = j // 2, j % 2
                                    if j % 6 == 0:
                                        pe.wait_ge(sem("m_u_lo"), g * UP + KH * (t // 3 + 1))
                                    if j >= 5:
                                        pe.wait_ge(sem("m_added"), g * DOWN + j - 4)
                                    for k in range(KH):
                                        for a, b in ((u_hi, down_hi), (u_hi, down_lo), (u_lo, down_hi)):
                                            mm = pe.matmul(ps[:, 3 + j % 5, :], a[:, k, t * P:(t + 1) * P], b[:, k, n * 512:(n + 1) * 512],
                                                           start=(k == 0 and a is u_hi and b is down_hi), stop=(k == KH - 1 and a is u_lo))
                                    mm.then_inc(sem("m_down_done"), 1)

                        @block.scalar
                        def _(act):
                            with act.Fori(0, NG) as g:
                                act.wait_ge(sem("m_up_loaded"), 16 * g + 16)
                                act.wait_ge(sem("m_up_done"), g * UP)
                                act.copy(up_hi[:, :, :], raw_up[:, :, :]).then_inc(sem("m_up_hi"), 1)
                                act.wait_ge(sem("m_down_loaded"), 16 * g + 16)
                                act.wait_ge(sem("m_down_done"), g * DOWN)
                                act.copy(down_hi[:, :, :], raw_down[:, :, :]).then_inc(sem("m_down_hi"), 1)
                                for j in range(UP):
                                    n, m = j // KH, j % KH
                                    act.wait_ge(sem("m_up_done"), g * UP + j + 1)
                                    if j >= 2:
                                        act.wait_ge(sem("m_u_lo"), g * UP + j - 1)
                                    act.activation(relu[:, j % 2, :], ps[:, j % 3, 0:384], ACT.Relu).then_inc(sem("m_relu"), 1)
                                    act.wait_ge(sem("m_relu"), g * UP + j + 1)
                                    act.activation(square[:, j % 2, :], relu[:, j % 2, :], ACT.Square).then_inc(sem("m_square"), 1)
                                    act.wait_ge(sem("m_square"), g * UP + j + 1)
                                    act.copy(u_hi[:, m, n * 384:(n + 1) * 384], square[:, j % 2, :]).then_inc(sem("m_u_hi"), 1)

                        @block.vector
                        def _(dve):
                            dve.wait_ge(sem("m_out_cleared"), 1)
                            with dve.Fori(0, NG) as g:
                                for j in range(UP):
                                    n, m = j // KH, j % KH
                                    dve.wait_ge(sem("m_u_hi"), g * UP + j + 1)
                                    dve.tensor_tensor(u_lo[:, m, n * 384:(n + 1) * 384], square[:, j % 2, :],
                                                      u_hi[:, m, n * 384:(n + 1) * 384].bitcast(F32), ALU.subtract).then_inc(sem("m_u_lo"), 1)
                                for j in range(DOWN):
                                    t, n = j // 2, j % 2
                                    y = mix[:, t, n * 512:(n + 1) * 512]
                                    dve.wait_ge(sem("m_down_done"), g * DOWN + j + 1)
                                    dve.tensor_tensor(y, y, ps[:, 3 + j % 5, :], ALU.add).then_inc(sem("m_added"), 1)

            open_section()
            mixer_memory = ExitStack()
            hT = sb("hT", [P, KD, TOK], mixer_memory)
            ring = sb("ring", [P, 2, KD, W_C], mixer_memory)
            input_norm()
            mixer_a()
            close_section()
            for pair in range(3):
                open_section()
                mixer_c(pair)
                close_section()
            open_section()
            mixer_b()
            close_section()
            mixer_memory.close()
            mlp_memory = ExitStack()
            hi = sb("h_hi", [P, KD, TOK], mlp_memory, F32R)
            lo = sb("h_lo", [P, KD, TOK], mlp_memory, F32R)
            open_section()
            out_projection()
            residual_norm("mix", 0, True)
            mlp()
            mlp_memory.close()
            residual_norm("mlp", 1, False)
            close_section()

        with nc.Block() as block:
            @block.sync
            def _(sp):
                sp.dma_start(O["y_sample"], x_dram[0:LAT * P, :]).then_inc(sem("outputs_stored"), 16)
                sp.dma_start(O["y_prompt"], x_dram[LAT * P:TOK, :]).then_inc(sem("outputs_stored"), 16)
                sp.wait_ge(sem("outputs_stored"), 32)
        sem_stack.close()


OUTS = (
    ("y_prompt", (P, D), (1, P, D)),
    ("y_sample", (LAT * P, D), (1, LAT * P, D)),
    ("new_k_attn", (DEPTH, P, 2 * HD), (1, DEPTH, P, 2, HD)),
    ("new_v_attn", (DEPTH, P, 2 * HD), (1, DEPTH, P, 2, HD)),
    ("new_k_nbhd", (DEPTH, P, 6 * HD), (1, DEPTH, P, 6, HD)),
    ("new_v_nbhd", (DEPTH, P, 6 * HD), (1, DEPTH, P, 6, HD)),
    ("new_C", (DEPTH, 2, 4, HD, HD), (1, DEPTH, 2, 4, HD, HD)),
    ("new_n", (DEPTH, 2, 4, HD, 1), (1, DEPTH, 2, 4, HD)),
    ("new_m", (DEPTH, 2, 4, 1), (1, DEPTH, 2, 4)),
)


def kernel(**inputs):
    import concourse.bacc as bacc
    from concourse.bass_utils import run_bass_kernel_spmd

    a = {k: np.asarray(v) for k, v in inputs.items()}
    bias_rows = np.zeros((DEPTH, 6, BIAS_DR, BIAS_W), np.float32)
    bias_rows[:, :, 2:17, GRID_W - NA_COLS:GRID_W + NA_COLS - 1] = a["nbhd_rel_bias"]

    def transposed(v):
        v = v.reshape(v.shape[:-1] + (KD, P))
        return np.moveaxis(v, -1, 0)

    laid = {
        "x_sample": a["x_sample"].reshape(LAT * P, D),
        "x_prompt": a["x_prompt"].reshape(P, D),
        "condT": transposed(np.stack([a["c"].reshape(D), a["c_ctx"]])).transpose(0, 2, 1),
        "w_ada": a["w_ada"], "b_ada": a["b_ada"],
        "g_preT": transposed(np.stack([a["g_pre_mix"], a["g_pre_ffn"]], 1)).transpose(1, 0, 2, 3),
        "g_post": np.stack([a["g_post_mix"], a["g_post_ffn"]], 1),
        "w_in": a["w_in"], "w_out": a["w_out"], "w_ffn_up": a["w_ffn_up"], "w_ffn_down": a["w_ffn_down"],
        "q_norm": a["q_norm_attn"], "k_norm": a["k_norm_attn"],
        "gate_bias": a["mlstm_gate_bias"], "out_norm": a["mlstm_out_norm"].reshape(DEPTH, 256),
        "bias_rows": bias_rows.reshape(DEPTH, 6, BIAS_DR * BIAS_W),
        "cache_k_attn": a["cache_k_attn"].reshape(DEPTH, P, 2 * HD),
        "cache_v_attn": a["cache_v_attn"].reshape(DEPTH, P, 2 * HD),
        "cache_k_nbhd": a["cache_k_nbhd"].reshape(DEPTH, P, 6 * HD),
        "cache_v_nbhd": a["cache_v_nbhd"].reshape(DEPTH, P, 6 * HD),
        "state_C": a["state_mlstm_C"].reshape(DEPTH, 2, 4, HD, HD),
        "state_n": a["state_mlstm_n"].reshape(DEPTH, 2, 4, HD, 1),
        "state_m": a["state_mlstm_m"].reshape(DEPTH, 2, 4, 1),
        **shape_constants(),
    }
    laid = {k: np.ascontiguousarray(v) for k, v in laid.items()}
    nc = bacc.Bacc("TRN2", target_bir_lowering=False, num_devices=1)
    ins = {k: nc.dram_tensor(f"in_{k}", v.shape, F32, kind="ExternalInput").ap() for k, v in laid.items()}
    outs = {k: nc.dram_tensor(f"out_{k}", s, F32, kind="ExternalOutput").ap() for k, s, _ in OUTS}
    with nc.allow_non_contiguous_dma(reason="single columns of the mLSTM state"):
        build(nc, ins, outs)
    r = run_bass_kernel_spmd(nc, [{f"in_{k}": v for k, v in laid.items()}], core_ids=[0])
    return tuple(np.asarray(r.results[0][f"out_{k}"]).reshape(full) for k, _, full in OUTS)
```

```python
from contextlib import ExitStack

import concourse.bass as bass
import concourse.mybir as mybir
import numpy as np

ALU = mybir.AluOpType
ACT = mybir.ActivationFunctionType
AX = mybir.AxisListType
F32 = mybir.dt.float32
F32R = mybir.dt.float32r

P = 128
D = 1024
KD = D // P
DEPTH = 2
LAT = 8
NT = LAT + 1
PROMPT = LAT
TOK = NT * P
PROMPT_SLOT = 8
CTX_SLOT = 9
NSLOT = 10
HD = 64
GRID_W = 64
ROWS = 16
NA_ROWS = 8
NA_COLS = 16
EPS = 1e-6
SCALE = HD ** -0.5
NEG = -1e30
LOWEST = -3e38
OFF_A, OFF_B, OFF_C = 0, 640, 1680
W_C = 384
D_FF = 4096
HID = 256
VA = HD + 1
WIN_ROWS = 10
WIN = WIN_ROWS * GRID_W
WIN_TYPES = 5
BIAS_U = 18
BIAS_DR = 20
BIAS_W = 2 * GRID_W - 1


def window_start_row(t):
    return min(max(2 * t - 4, 0), ROWS - WIN_ROWS)


def window_type(t):
    return {0: 0, 1: 1, 6: 3, 7: 4}.get(t, 2)


def shape_constants():
    f = np.float32
    ident = np.eye(P, dtype=f)
    quarter = HD // 4
    inv = (10000.0 ** (-np.arange(quarter, dtype=f) / quarter)).astype(f)
    pos = np.arange(LAT * P)
    cos = np.zeros((LAT * P, 2, 2, quarter), f)
    sin = np.zeros((LAT * P, 2, 2, quarter), f)
    for half, x in enumerate((pos // GRID_W, pos % GRID_W)):
        ang = x.astype(f)[:, None] * inv[None, :]
        cos[:, half, 0] = cos[:, half, 1] = np.cos(ang)
        sin[:, half, 0] = -np.sin(ang)
        sin[:, half, 1] = np.sin(ang)
    cos = cos.reshape(LAT, P, HD).transpose(1, 0, 2)
    sin = sin.reshape(LAT, P, HD).transpose(1, 0, 2)
    s = np.arange(P)
    causal = np.zeros((P, 2, P), f)
    causal[:, 0] = np.where(s[:, None] <= s[None, :], 0, NEG)
    causal[:, 1] = np.where(s[:, None] >= s[None, :], 0, NEG)
    window = np.full((P, WIN_TYPES, WIN_ROWS, GRID_W), NEG, f)
    for t in (0, 1, 2, 6, 7):
        for p in range(P):
            r, c = 2 * t + p // GRID_W, p % GRID_W
            rs = min(max(r - NA_ROWS // 2, 0), ROWS - NA_ROWS) - window_start_row(t)
            cs = min(max(c - NA_COLS // 2, 0), GRID_W - NA_COLS)
            window[p, window_type(t), rs:rs + NA_ROWS, cs:cs + NA_COLS] = 0
    neg_select = np.zeros((P, 2, 4, P), f)
    diagonal = np.zeros((36, 4, NT), f)
    for j in range(4):
        for d in range(2):
            neg_select[32 * d + j, d, j] = -1
            diagonal[32 * d + j, j] = 1
    cond_select = np.zeros((2, 2, P), f)
    cond_select[0, 0] = cond_select[1, 1] = 1
    return {
        "ident": ident, "cos": cos.copy(), "sin": sin.copy(), "causal": causal,
        "window": window.reshape(P, WIN_TYPES * WIN), "neg_select": neg_select,
        "diagonal": diagonal, "cond_select": cond_select,
    }


class Steps:

    def __init__(self, eng, sem):
        self.eng, self.sem, self.n = eng, sem, 0

    def __call__(self, ins):
        self.n += 1
        ins.then_inc(self.sem, 1)
        self.eng.wait_ge(self.sem, self.n)


def build(nc, I, O):
    sems = {}
    with ExitStack() as ctx:
        sem_stack = ExitStack()
        dve_step = act_step = pool_step = None

        def sem(name):
            if name not in sems:
                sems[name] = sem_stack.enter_context(nc.semaphore(name))
            return sems[name]

        def open_section():
            nonlocal dve_step, act_step, pool_step
            dve_step = Steps(nc.vector, sem("dve_steps"))
            act_step = Steps(nc.scalar, sem("act_steps"))
            pool_step = Steps(nc.gpsimd, sem("pool_steps"))

        def close_section():
            numbers = sorted(s.num for s in sems.values())
            first = 0
            for i, n in enumerate(numbers):
                if i + 1 == len(numbers) or numbers[i + 1] != n + 1:
                    nc.all_engine_barrier(sems_to_clear=range(numbers[first], n + 1))
                    first = i + 1
            sem_stack.close()
            sems.clear()

        def sb(name, shape, stack=ctx, dtype=F32):
            return stack.enter_context(nc.sbuf_tensor(name, shape, dtype))

        def dram(name, shape):
            return nc.dram_tensor(name, shape, F32, kind="Internal").ap()

        ps = ctx.enter_context(nc.psum_tensor("ps", [P, 8, 512], F32))
        psf = ps[:, :, :].rearrange("p b n -> p (b n)")

        def x_tile(t):
            return O["y_prompt"] if t == PROMPT else O["y_sample"][t * P:(t + 1) * P, :]
        residual_copied = ctx.enter_context(nc.semaphore("residual_copied"))
        bias_pitch = BIAS_DR * BIAS_W
        bias_dram = dram("bias_by_column", (6, GRID_W * bias_pitch))

        ident = sb("ident_sb", [P, P])
        causal = sb("causal_sb", [P, 2, P])
        neg_select = sb("neg_select_sb", [P, 2, 4, P])
        diagonal = sb("diagonal_sb", [36, 4, NT])
        cond_select = sb("cond_select_sb", [2, 2, P])
        ones = sb("ones", [36, P])
        minus_half = sb("minus_half", [P, NT * 4])
        condT = sb("condT", [P, KD, 2])
        cond_e = sb("cond_e", [P, KD, 2])
        modT = sb("modT", [P, 4, KD, 2])
        gate = sb("gate", [P, 2, 2, D])
        mix = sb("mix", [P, NT, D])
        small = sb("small", [P, 256])

        with nc.Block() as block:
            @block.sync
            def _(sp):
                for k, t in (("ident", ident[:, :]), ("causal", causal[:, :, :]), ("neg_select", neg_select[:, :, :, :]),
                             ("diagonal", diagonal[:, :, :]),
                             ("cond_select", cond_select[:, :, :])):
                    sp.dma_start(t, I[k]).then_inc(sem("constants_loaded"), 16)
                sp.dma_start(O["y_sample"], I["x_sample"]).then_inc(residual_copied, 16)
                sp.dma_start(O["y_prompt"], I["x_prompt"]).then_inc(residual_copied, 16)
                sp.wait_ge(sem("constants_loaded"), 5 * 16)

            @block.gpsimd
            def _(pool):
                pool.memset(ones[:, :], 1.0)
                pool.memset(small[:, :], 0.0)
                pool.memset(minus_half[:, :], -0.5)

            @block.scalar
            def _(act):
                act.dma_start(condT[:, :, :], I["condT"]).then_inc(sem("cond_loaded"), 16)
                act.wait_ge(sem("cond_loaded"), 16)
                act.activation(cond_e[:, :, :], condT[:, :, :], ACT.Exp, scale=-1.0).then_inc(sem("cond_exp"), 1)

            @block.vector
            def _(dve):
                step = Steps(dve, sem("silu_steps"))
                dve.wait_ge(sem("cond_exp"), 1)
                step(dve.tensor_scalar(cond_e[:, :, :], cond_e[:, :, :], 1.0, None, ALU.add))
                step(dve.reciprocal(cond_e[:, :, :], cond_e[:, :, :]))
                step(dve.tensor_tensor(condT[:, :, :], condT[:, :, :], cond_e[:, :, :], ALU.mult))

        close_section()
        with nc.Fori(0, DEPTH) as l:

            w_in = I["w_in"][l].rearrange("(k p) n -> p k n", p=P)

            A_CUTS = ((OFF_A + 384, 256), (OFF_A, 384))
            B_CUTS = ((OFF_B, 256), (OFF_B + 768, 272), (OFF_B + 256, 256), (OFF_B + 512, 256))

            def load_cuts(sp, cuts):
                for c, (o, n) in enumerate(cuts):
                    sp.dma_start(ring[:, c, :, 0:n], w_in[:, :, o:o + n]).then_inc(sem("next_w_loaded"), 16)
                sp.wait_ge(sem("next_w_loaded"), 16 * len(cuts))

            def load_c_weights(sp, pair):
                for m in range(3):
                    o = OFF_C + m * 384 + pair * P
                    sp.dma_start(ring[:, pair % 2, :, m * P:(m + 1) * P], w_in[:, :, o:o + P]).then_inc(sem("next_c_w_loaded"), 16)
                sp.wait_ge(sem("next_c_w_loaded"), 48)

            class Modulation:
                CHUNK = 256
                HALVES = CHUNK // P

                def __init__(self, tag, vectors, w, own):
                    self.tag, self.w, self.ring = tag, w, w.shape[1]
                    self.chunks = [(v, q) for v in vectors for q in range(D // self.CHUNK)]
                    self.n = len(self.chunks)
                    self.w_dram = I["w_ada"][l].rearrange("(k p) n -> p k n", p=P)
                    self.gpre = sb(f"{tag}_g_preT", [P, 2, KD], own)
                    gates = [c for c in range(self.n) if self.is_gate(c)]
                    self.gate_count = {c: i + 1 for i, c in enumerate(gates)}
                    self.rows_in = sb(f"{tag}_rows_in", [2, self.ring, 2, self.CHUNK], own)
                    self.row = sb(f"{tag}_row", [2, 2, self.CHUNK], own)
                    self.rows_loads, loads = [], [0] * self.ring
                    for c in range(self.n):
                        loads[c % self.ring] += 2 if self.is_gate(c) else 1
                        self.rows_loads.append(loads[c % self.ring])

                def sem(self, name):
                    return sem(f"{self.tag}_{name}")

                def is_gate(self, c):
                    return self.chunks[c][0] in (2, 5)

                def row_out(self, c):
                    return ps[0:2, 6 + c % 2, 0:self.CHUNK]

                def load_gain(self, sp):
                    sp.dma_start(self.gpre[:, :, :], I["g_preT"][l]).then_inc(self.sem("gain_loaded"), 16)

                def load(self, sp, c):
                    v, q = self.chunks[c]
                    cols = slice(v * D + q * self.CHUNK, v * D + (q + 1) * self.CHUNK)
                    if c >= self.ring:
                        sp.wait_ge(self.sem("multiplied"), c - self.ring + 1)
                    sp.dma_start(self.w[:, c % self.ring, :, :], self.w_dram[:, :, cols]).then_inc(self.sem(f"w_loaded{c % self.ring}"), 16)
                    into = self.rows_in[:, c % self.ring, :, :]
                    sp.dma_start(into[:, 0, :], I["b_ada"][bass.ds(l, 1), cols].to_broadcast([2, self.CHUNK])).then_inc(self.sem(f"rows_loaded{c % self.ring}"), 16)
                    if self.is_gate(c):
                        if c - self.ring in self.gate_count:
                            sp.wait_ge(self.sem("gate_scaled"), self.gate_count[c - self.ring])
                        s = v // 3
                        sp.dma_start(into[:, 1, :], I["g_post"][bass.ds(l, 1), s, q * self.CHUNK:(q + 1) * self.CHUNK].to_broadcast([2, self.CHUNK])).then_inc(
                            self.sem(f"rows_loaded{c % self.ring}"), 16)

                def multiply(self, pe, c):
                    pe.wait_ge(self.sem(f"w_loaded{c % self.ring}"), 16 * (c // self.ring + 1))
                    if c >= 2:
                        pe.wait_ge(self.sem("row_copied"), c - 1)
                    for k in range(KD):
                        pe.matmul(self.row_out(c), condT[:, k, :], self.w[:, c % self.ring, k, :], start=(k == 0), stop=False)
                    pe.wait_ge(self.sem(f"rows_loaded{c % self.ring}"), 16 * self.rows_loads[c])
                    mm = pe.matmul(self.row_out(c), ones[0:1, 0:2], self.rows_in[0:1, c % self.ring, 0, :], start=False, stop=True)
                    mm.then_inc(self.sem("multiplied"), 1)

                def spread(self, pe, c):
                    if c >= 1:
                        pe.wait_ge(self.sem("chunk_done"), c)
                    if self.is_gate(c):
                        pe.wait_ge(self.sem("gate_scaled"), self.gate_count[c])
                        for cond in range(2):
                            mm = pe.matmul(ps[:, 5, cond * self.CHUNK:(cond + 1) * self.CHUNK], cond_select[:, cond, :], self.row[:, c % 2, :],
                                           start=True, stop=True)
                    else:
                        pe.wait_ge(self.sem("row_copied"), c + 1)
                        for m in range(self.HALVES):
                            mm = pe.transpose(ps[:, 5, 2 * m:2 * m + 2], self.row[:, c % 2, m * P:(m + 1) * P], ident[0:2, 0:2])
                    mm.then_inc(self.sem("spread"), 1)

                def take_row(self, act, c):
                    act.wait_ge(self.sem("multiplied"), c + 1)
                    if c >= 2:
                        act.wait_ge(self.sem("spread"), c - 1)
                    act.copy(self.row[:, c % 2, :], self.row_out(c)).then_inc(self.sem("row_copied"), 1)

                def take_spread(self, act, c):
                    v, q = self.chunks[c]
                    act.wait_ge(self.sem("spread"), c + 1)
                    if self.is_gate(c):
                        a = act.copy(gate[:, v // 3, :, q * self.CHUNK:(q + 1) * self.CHUNK], ps[:, 5, :].rearrange("p (c n) -> p c n", c=2))
                    elif v % 3 == 0:
                        a = act.copy(modT[:, 2 * (v // 3), q * self.HALVES:(q + 1) * self.HALVES, :],
                                     ps[:, 5, 0:2 * self.HALVES].rearrange("p (k c) -> p k c", c=2))
                    else:
                        act.wait_ge(self.sem("gain_loaded"), 16)
                        for m in range(self.HALVES):
                            k = q * self.HALVES + m
                            g = self.gpre[:, v // 3, k:k + 1]
                            a = act.activation(modT[:, 2 * (v // 3) + 1, k, :], ps[:, 5, 2 * m:2 * m + 2], ACT.Identity, bias=g, scale=g)
                    a.then_inc(self.sem("chunk_done"), 1)

                def tensor_step(self, pe, c):
                    if c == 0:
                        self.multiply(pe, 0)
                    if c + 1 < self.n:
                        self.multiply(pe, c + 1)
                    self.spread(pe, c)

                def scalar_step(self, act, c):
                    if c < self.n:
                        self.take_row(act, c)
                    if c >= 1:
                        self.take_spread(act, c - 1)

                def scale_gate_rows(self, pool):
                    for c, n in self.gate_count.items():
                        pool.wait_ge(self.sem("row_copied"), c + 1)
                        pool.wait_ge(self.sem(f"rows_loaded{c % self.ring}"), 16 * self.rows_loads[c])
                        pool.tensor_tensor(self.row[:, c % 2, :], self.row[:, c % 2, :], self.rows_in[:, c % self.ring, 1, :],
                                           ALU.mult).then_inc(self.sem("gate_scaled"), 1)

            def input_norm():
                AHEAD = 5
                with ExitStack() as own:
                    mods = Modulation("mix_mods", (0, 1), sb("w_ada_ring", [P, 4, KD, Modulation.CHUNK], own), own)
                    x = sb("in_x", [P, NT, D], own)
                    junk = sb("in_junk", [P, D], own)
                    ssq, rstd = small[:, 0:NT], small[:, NT:2 * NT]

                    def turned_to(t, k):
                        at = t % 2 * 1024 + k * P
                        return psf[:, at:at + P]

                    with nc.Block() as block:
                        @block.sync
                        def _(sp):
                            mods.load_gain(sp)
                            for c in range(mods.ring):
                                mods.load(sp, c)
                            sp.wait_ge(residual_copied, 32)
                            for t in range(NT):
                                if t == AHEAD:
                                    for c in range(mods.ring, mods.n):
                                        mods.load(sp, c)
                                sp.dma_start(x[:, t, :], x_tile(t)).then_inc(sem(f"in_x_loaded{t}"), 16)
                            load_cuts(sp, A_CUTS[:1])

                        @block.tensor
                        def _(pe):
                            for c in range(mods.n):
                                mods.tensor_step(pe, c)
                            for t in range(NT):
                                pe.wait_ge(sem("in_normed"), t + 1)
                                if t >= 2:
                                    pe.wait_ge(sem("in_modulated_dve"), t - 1)
                                    pe.wait_ge(sem("in_modulated_act"), t - 1)
                                for k in range(KD):
                                    mm = pe.transpose(turned_to(t, k), x[:, t, k * P:(k + 1) * P], ident[:, :])
                                mm.then_inc(sem("in_turned"), 1)

                        @block.scalar
                        def _(act):
                            def squares(t):
                                act.wait_ge(sem(f"in_x_loaded{t}"), 16)
                                act_step(act.activation(junk[:, :], x[:, t, :], ACT.Square, accum_out=ssq[:, t:t + 1]))
                                act.sem_inc(sem("in_squared"), 1)

                            for c in range(mods.n + 1):
                                mods.scalar_step(act, c)
                                if c >= mods.ring and c - mods.ring < AHEAD:
                                    squares(c - mods.ring)
                            act.wait_ge(mods.sem("chunk_done"), mods.n)
                            for t in range(NT):
                                if t + AHEAD < NT:
                                    squares(t + AHEAD)
                                c = 1 if t == PROMPT else 0
                                act.wait_ge(sem("in_turned"), t + 1)
                                for k in range(4, KD):
                                    a = act.activation(hT[:, k, t * P:(t + 1) * P], turned_to(t, k), ACT.Identity,
                                                       bias=modT[:, 0, k, c:c + 1], scale=modT[:, 1, k, c:c + 1])
                                a.then_inc(sem("in_modulated_act"), 1)

                        @block.gpsimd
                        def _(pool):
                            for t in range(NT):
                                pool.wait_ge(sem("in_squared"), t + 1)
                                pool_step(pool.tensor_scalar(rstd[:, t:t + 1], ssq[:, t:t + 1], 1.0 / D, EPS, ALU.mult, ALU.add))
                                pool.tensor_tensor(rstd[:, t:t + 1], rstd[:, t:t + 1], minus_half[:, 0:1], ALU.pow).then_inc(sem("in_rstd"), 1)

                        @block.vector
                        def _(dve):
                            def normalise(t):
                                dve.wait_ge(sem("in_rstd"), t + 1)
                                dve.tensor_scalar(x[:, t, :], x[:, t, :], rstd[:, t:t + 1], None, ALU.mult).then_inc(sem("in_normed"), 1)

                            for t in range(AHEAD):
                                normalise(t)
                            dve.wait_ge(mods.sem("chunk_done"), mods.n)
                            for t in range(NT):
                                c = 1 if t == PROMPT else 0
                                dve.wait_ge(sem("in_turned"), t + 1)
                                for k in range(4):
                                    a = dve.tensor_scalar(hT[:, k, t * P:(t + 1) * P], turned_to(t, k), modT[:, 1, k, c:c + 1], modT[:, 0, k, c:c + 1],
                                                          ALU.mult, ALU.add)
                                a.then_inc(sem("in_modulated_dve"), 1)
                                if t + AHEAD < NT:
                                    normalise(t + AHEAD)

            def residual_norm(tag, sub, norm):
                with ExitStack() as own:
                    SLOTS = 6 if norm else NT
                    x = sb(f"{tag}_x", [P, SLOTS, D], own)
                    junk = sb(f"{tag}_junk", [P, D], own)
                    xn = sb(f"{tag}_x_normed", [P, 2, D], own) if norm else None
                    FULL = 3
                    full = sb(f"{tag}_h_full", [P, FULL, KD, P], own) if norm else None
                    ssq, rstd = small[:, 0:NT], small[:, NT:2 * NT]
                    ssq2, rstd2 = small[:, 2 * NT:3 * NT], small[:, 3 * NT:4 * NT]
                    y_sq, y_rstd, x_new = sem(f"{tag}_y_squares"), sem(f"{tag}_y_rstd"), sem(f"{tag}_x_new")
                    if norm:
                        x_sq, x_rstd = sem(f"{tag}_x_squares"), sem(f"{tag}_x_rstd")
                        normed, turned = sem(f"{tag}_normed"), sem(f"{tag}_turned")
                        mod_d, mod_a = sem(f"{tag}_modulated_dve"), sem(f"{tag}_modulated_act")
                        hi_done, lo_done = sem(f"{tag}_hi_done"), sem(f"{tag}_lo_done")
                    ON_DVE = 4
                    ADD, SQUARES, NORM, MODULATE, HIGH, LOW = 1, 2, 3, 4, 5, 6
                    STEPS = NT + (LOW if norm else ADD)

                    def turned_to(t, k):
                        at = t % 2 * 1536 + (k * P if k < ON_DVE else 512 + (k - ON_DVE) * P)
                        return psf[:, at:at + P]

                    with nc.Block() as block:
                        @block.sync
                        def _(sp):
                            for t in range(SLOTS):
                                sp.dma_start(x[:, t % SLOTS, :], x_tile(t)).then_inc(sem(f"{tag}_x_loaded{t}"), 16)
                            for t in range(NT):
                                sp.wait_ge(x_new, t + 1)
                                sp.dma_start(x_tile(t), x[:, t % SLOTS, :]).then_inc(sem(f"{tag}_x_stored{t}"), 16)
                                if t >= 3 and t - 3 + SLOTS < NT:
                                    u = t - 3 + SLOTS
                                    sp.wait_ge(sem(f"{tag}_x_stored{t - 3}"), 16)
                                    sp.wait_ge(normed, t - 2)
                                    sp.dma_start(x[:, u % SLOTS, :], x_tile(u)).then_inc(sem(f"{tag}_x_loaded{u}"), 16)
                            for t in range(NT):
                                sp.wait_ge(sem(f"{tag}_x_stored{t}"), 16)

                        @block.scalar
                        def _(act):
                            def squares_y(t):
                                act_step(act.activation(junk[:, :], mix[:, t, :], ACT.Square, accum_out=ssq[:, t:t + 1]))
                                act.sem_inc(y_sq, 1)

                            def squares_x(t):
                                act.wait_ge(x_new, t + 1)
                                act_step(act.activation(junk[:, :], x[:, t % SLOTS, :], ACT.Square, accum_out=ssq2[:, t:t + 1]))
                                act.sem_inc(x_sq, 1)

                            def modulate(t):
                                c = 1 if t == PROMPT else 0
                                act.wait_ge(turned, t + 1)
                                if t >= FULL:
                                    act.wait_ge(lo_done, t - FULL + 1)
                                for k in range(ON_DVE, KD):
                                    a = act.activation(full[:, t % FULL, k, :], turned_to(t, k), ACT.Identity,
                                                       bias=modT[:, 2, k, c:c + 1], scale=modT[:, 3, k, c:c + 1])
                                a.then_inc(mod_a, 1)

                            def high_part(t):
                                act.wait_ge(mod_a, t + 1)
                                act.wait_ge(mod_d, t + 1)
                                act.copy(hi[:, :, t * P:(t + 1) * P], full[:, t % FULL, :, :]).then_inc(hi_done, 1)

                            for n in range(STEPS):
                                if n < NT:
                                    squares_y(n)
                                if norm and 0 <= n - HIGH < NT:
                                    high_part(n - HIGH)
                                if norm and 0 <= n - SQUARES < NT:
                                    squares_x(n - SQUARES)
                                if norm and 0 <= n - MODULATE < NT:
                                    modulate(n - MODULATE)

                        @block.gpsimd
                        def _(pool):
                            def inverse_root(s, r, t, ready, done):
                                pool.wait_ge(ready, t + 1)
                                pool_step(pool.tensor_scalar(r[:, t:t + 1], s[:, t:t + 1], 1.0 / D, EPS, ALU.mult, ALU.add))
                                pool.tensor_tensor(r[:, t:t + 1], r[:, t:t + 1], minus_half[:, 0:1], ALU.pow).then_inc(done, 1)

                            for n in range(NT + SQUARES):
                                if n < NT:
                                    inverse_root(ssq, rstd, n, y_sq, y_rstd)
                                if norm and n >= SQUARES:
                                    inverse_root(ssq2, rstd2, n - SQUARES, x_sq, x_rstd)

                        @block.vector
                        def _(dve):
                            def add_residual(t):
                                dve.wait_ge(y_rstd, t + 1)
                                dve_step(dve.scalar_tensor_tensor(mix[:, t, :], mix[:, t, :], rstd[:, t:t + 1],
                                                                  gate[:, sub, 1 if t == PROMPT else 0, :], ALU.mult, ALU.mult))
                                dve.wait_ge(sem(f"{tag}_x_loaded{t}"), 16)
                                dve.tensor_tensor(x[:, t % SLOTS, :], x[:, t % SLOTS, :], mix[:, t, :], ALU.add).then_inc(x_new, 1)

                            def normalise(t):
                                dve.wait_ge(x_rstd, t + 1)
                                dve.wait_ge(x_new, t + 1)
                                if t >= 2:
                                    dve.wait_ge(turned, t - 1)
                                dve.tensor_scalar(xn[:, t % 2, :], x[:, t % SLOTS, :], rstd2[:, t:t + 1], None, ALU.mult).then_inc(normed, 1)

                            def modulate(t):
                                c = 1 if t == PROMPT else 0
                                dve.wait_ge(turned, t + 1)
                                if t >= FULL:
                                    dve.wait_ge(lo_done, t - FULL + 1)
                                for k in range(ON_DVE):
                                    a = dve.tensor_scalar(full[:, t % FULL, k, :], turned_to(t, k), modT[:, 3, k, c:c + 1],
                                                          modT[:, 2, k, c:c + 1], ALU.mult, ALU.add)
                                a.then_inc(mod_d, 1)

                            def low_part(t):
                                dve.wait_ge(hi_done, t + 1)
                                tt = slice(t * P, (t + 1) * P)
                                dve.tensor_tensor(lo[:, :, tt], full[:, t % FULL, :, :], hi[:, :, tt].bitcast(F32), ALU.subtract).then_inc(lo_done, 1)

                            for n in range(ADD, STEPS):
                                if n - ADD < NT:
                                    add_residual(n - ADD)
                                if norm and 0 <= n - LOW < NT:
                                    low_part(n - LOW)
                                if norm and 0 <= n - NORM < NT:
                                    normalise(n - NORM)
                                if norm and 0 <= n - MODULATE < NT:
                                    modulate(n - MODULATE)

                        @block.tensor
                        def _(pe):
                            for t in range(NT if norm else 0):
                                pe.wait_ge(normed, t + 1)
                                if t >= 2:
                                    pe.wait_ge(mod_d, t - 1)
                                    pe.wait_ge(mod_a, t - 1)
                                for k in range(KD):
                                    mm = pe.transpose(turned_to(t, k), xn[:, t % 2, k * P:(k + 1) * P], ident[:, :])
                                mm.then_inc(turned, 1)

            def half(j):
                return slice(j * HD, (j + 1) * HD)

            def high_parts(act, src, q=None, k=None, scale=1.0):
                for j in range(2):
                    if q is not None:
                        a = act.mul(q[half(j), j], src[half(j)], scale)
                    else:
                        act.copy(k[half(j), j], src[half(j)])
                        a = act.copy(k[half(1 - j), j], src[half(j)])
                return a

            def low_parts(dve, src, q=None, k=None, k_low=None, scale=1.0):
                for j in range(2):
                    if q is not None:
                        a = dve.scalar_tensor_tensor(q[half(1 - j), j], src[half(j)], scale, q[half(j), j].bitcast(F32), ALU.mult, ALU.subtract)
                    else:
                        a = dve.tensor_tensor(k_low[half(j)], src[half(j)], k[half(j), j].bitcast(F32), ALU.subtract)
                return a

            def unit_operands(q, k, k_low, j, segments):
                return ((q[:, j], q[half(j), j]), [(k[:, j, a:z], k_low[half(j), a:z], c) for a, z, c in segments])

            def attention(tag, units, own, n_bias_cols):
                nu = len(units)
                P_sb = sb(f"{tag}_probs", [P, 2, NT * P], own)
                PT = sb(f"{tag}_probsT", [P, 2, NT * P], own)
                Ssb = sb(f"{tag}_scores", [P, 2, n_bias_cols], own) if n_bias_cols else None
                biased = sb(f"{tag}_bias_tiles", [P, 2, n_bias_cols], own) if n_bias_cols else None
                nmax = small[:, 64:68]
                den = small[:, 68:72]
                rden = small[:, 72:76]
                groups, count = [], [0, 0]
                for i, u in enumerate(units):
                    g0 = []
                    for g in range((u["n"] // P + 2) // 3):
                        e = len(groups) % 2
                        count[e] += 1
                        g0.append((len(groups), e, count[e], 3 * g, min(3 * g + 3, u["n"] // P)))
                        groups.append(g0[-1])
                    u["groups"] = g0
                copied = [sem(f"{tag}_probsT_copied_act"), sem(f"{tag}_probsT_copied_dve")]
                S_ready, max_ready, exp_done = sem(f"{tag}_scores_ready"), sem(f"{tag}_max_ready"), sem(f"{tag}_exp_done")
                turned, pv_done, out_done = sem(f"{tag}_probs_turned"), sem(f"{tag}_pv_done"), sem(f"{tag}_out_done")
                bias_ready = sem(f"{tag}_bias_ready")
                bias_count = [0]
                for u in units:
                    if u["bias"] is not None:
                        bias_count[0] += 1
                        u["bias_n"] = bias_count[0]

                def S(i, a, b):
                    return psf[:, i % 2 * 1536 + a:i % 2 * 1536 + b]

                def PTp(i, k, z):
                    at = (i % 2 * 3 + k // 3) * 512 + k % 3 * P
                    return psf[:, at:at + (z - k) * P]

                def out_p(i):
                    return ps[:, 6 + i % 2, 0:P]

                def tensor(pe):
                    def scores(i):
                        if i >= 2:
                            for gi, e, n, a, b in units[i - 2]["groups"]:
                                pe.wait_ge(copied[e], n)
                        stacked, high = units[i]["q"]
                        for k_hi, k_lo, c0 in units[i]["keys"]:
                            at = S(i, c0, c0 + k_hi.shape[1])
                            pe.matmul(at, stacked, k_hi, start=True, stop=False)
                            mm = pe.matmul(at, high, k_lo, start=False, stop=True)
                        mm.then_inc(S_ready, 1)

                    def turn(i):
                        pe.wait_ge(exp_done, i + 1)
                        for gi, e, n, a, b in units[i]["groups"]:
                            for k in range(a, b):
                                mm = pe.transpose(PTp(i, k, k + 1), P_sb[:, i % 2, k * P:(k + 1) * P], ident[:, :])
                            mm.then_inc(turned, 1)

                    def apply(i):
                        u = units[i]
                        if i >= 2:
                            pe.wait_ge(out_done, i - 1)
                        for gi, e, n, a, b in u["groups"]:
                            pe.wait_ge(copied[e], n)
                            for k in range(a, b):
                                mm = pe.matmul(out_p(i), PT[:, i % 2, k * P:(k + 1) * P], u["v"][k],
                                               start=(k == 0), stop=(k == u["n"] // P - 1))
                        mm.then_inc(pv_done, 1)

                    scores(0)
                    scores(1)
                    for i in range(nu):
                        turn(i)
                        if i >= 1:
                            apply(i - 1)
                        if i + 2 < nu:
                            scores(i + 2)
                    apply(nu - 1)

                def copy_groups(eng, e, i):
                    for gi, ge, n, a, b in units[i]["groups"]:
                        if ge != e:
                            continue
                        eng.wait_ge(turned, gi + 1)
                        src, dst = PTp(i, a, b), PT[:, i % 2, a * P:b * P]
                        ins = eng.copy(dst, src) if e == 0 else eng.tensor_copy(dst, src)
                        ins.then_inc(copied[e], 1)

                def scalar(act):
                    def exp(i):
                        n = units[i]["n"]
                        act.wait_ge(max_ready, i + 1)
                        if i >= 2:
                            act.wait_ge(turned, units[i - 2]["groups"][-1][0] + 1)
                        src = S(i, 0, n) if units[i]["bias"] is None else Ssb[:, i % 2, 0:n]
                        act.activation(P_sb[:, i % 2, 0:n], src, ACT.Exp, bias=nmax[:, i % 4:i % 4 + 1],
                                       accum_out=den[:, i % 4:i % 4 + 1]).then_inc(exp_done, 1)
                    exp(0)
                    for i in range(nu):
                        copy_groups(act, 0, i)
                        if i + 1 < nu:
                            exp(i + 1)

                def vector(dve):
                    def maximum(i):
                        u = units[i]
                        dve.wait_ge(S_ready, i + 1)
                        if u["bias"] is None:
                            dve.tensor_reduce(nmax[:, i % 4:i % 4 + 1], S(i, 0, u["n"]), AX.X, ALU.max, negate=True).then_inc(max_ready, 1)
                        else:
                            dve.wait_ge(bias_ready, u["bias_n"])
                            if i >= 2:
                                dve.wait_ge(exp_done, i - 1)
                            dve_step(dve.tensor_tensor_reduce(Ssb[:, i % 2, :], S(i, 0, u["n"]), biased[:, u["bias_n"] % 2, :], 1.0, LOWEST,
                                                              ALU.add, ALU.max, nmax[:, i % 4:i % 4 + 1]))
                            dve.tensor_scalar(nmax[:, i % 4:i % 4 + 1], nmax[:, i % 4:i % 4 + 1], -1.0, None, ALU.mult).then_inc(max_ready, 1)

                    def output(i):
                        dve.wait_ge(exp_done, i + 1)
                        dve_step(dve.reciprocal(rden[:, i % 4:i % 4 + 1], den[:, i % 4:i % 4 + 1]))
                        dve.wait_ge(pv_done, i + 1)
                        dve.tensor_scalar(units[i]["out"], out_p(i)[:, units[i]["cols"]], rden[:, i % 4:i % 4 + 1], None,
                                          ALU.mult).then_inc(out_done, 1)
                    maximum(0)
                    maximum(1)
                    for i in range(nu):
                        copy_groups(dve, 1, i)
                        if i >= 1:
                            output(i - 1)
                        if i + 2 < nu:
                            maximum(i + 2)
                    output(nu - 1)

                return tensor, scalar, vector, biased, bias_ready, max_ready

            def mixer_a():
                with ExitStack() as own:
                    Z = mix[:, :, 0:512]
                    Q = sb("a_qT", [P, 2, 3, TOK], own, F32R)
                    KH = sb("a_kT_high", [P, 2, NSLOT * P], own, F32R)
                    KL = sb("a_kT_low", [P, NSLOT * P], own, F32R)
                    V = sb("a_v", [P, NSLOT, P], own)
                    g = sb("a_g", [P, 8, HD], own)
                    ctx_k = sb("a_ctx_k", [P, P], own)
                    with ExitStack() as inner:
                        sq = sb("a_sq", [P, 2, 512], inner)
                        r1 = sb("a_r1", [P, 2, 512], inner)
                        r2 = sb("a_r2", [P, 512], inner)
                        zr = sb("a_zr", [P, 2, 512], inner)
                        cos = sb("cos_sb", [P, LAT, HD], inner)
                        sin = sb("sin_sb", [P, LAT, HD], inner)
                        ss = small[:, 96:96 + NT * 8].rearrange("p (t h) -> p t h", h=8)
                        rs = small[:, 168:168 + NT * 8].rearrange("p (t h) -> p t h", h=8)
                        cuts = A_CUTS
                        with nc.Block() as block:
                            @block.sync
                            def _(sp):
                                o, n = cuts[1]
                                sp.dma_start(ring[:, 1, :, 0:n], w_in[:, :, o:o + n]).then_inc(sem("a_w_loaded1"), 16)
                                sp.dma_start(ctx_k[:, :], I["cache_k_attn"][l]).then_inc(sem("a_ctx_k_loaded"), 16)
                                sp.dma_start(V[:, CTX_SLOT, :], I["cache_v_attn"][l]).then_inc(sem("a_ctx_v_loaded"), 16)
                                sp.dma_start(cos[:, :, :], I["cos"]).then_inc(sem("a_rotary_loaded"), 16)
                                sp.dma_start(sin[:, :, :], I["sin"]).then_inc(sem("a_rotary_loaded"), 16)
                                for h in range(8):
                                    src = I["q_norm"] if h < 6 else I["k_norm"]
                                    sp.dma_start(g[:, h, :], src[bass.ds(l, 1), :].to_broadcast([P, HD])).then_inc(sem("a_g_loaded"), 16)
                                sp.wait_ge(sem("a_normed"), NT)
                                sp.dma_start(O["new_k_attn"][l], Z[:, PROMPT, 384:512]).then_inc(sem("a_k_stored"), 16)
                                sp.wait_ge(sem("a_v_copied"), NT)
                                sp.dma_start(O["new_v_attn"][l], V[:, PROMPT_SLOT, :]).then_inc(sem("a_v_stored"), 16)
                                sp.wait_ge(sem("a_k_stored"), 16)

                            @block.tensor
                            def _(pe):
                                def turn(t):
                                    pe.wait_ge(sem("a_rotated"), t + 1)
                                    if t >= 3:
                                        pe.wait_ge(sem("a_qk_copied"), t - 2)
                                    for m in range(4):
                                        mm = pe.transpose(ps[:, 4 + t % 3, m * P:(m + 1) * P], zr[:, t % 2, m * P:(m + 1) * P], ident[:, :])
                                    mm.then_inc(sem("a_qk_turned"), 1)

                                LAG = 3
                                for c, (o, n) in enumerate(cuts):
                                    if c == 1:
                                        pe.wait_ge(sem("a_w_loaded1"), 16)
                                    for t in range(NT):
                                        j = c * NT + t
                                        if j >= 4:
                                            pe.wait_ge(sem("a_projected_copied"), j - 3)
                                        for k in range(KD):
                                            mm = pe.matmul(ps[:, j % 4, 0:n], hT[:, k, t * P:(t + 1) * P], ring[:, c, k, 0:n],
                                                           start=(k == 0), stop=(k == KD - 1))
                                        mm.then_inc(sem("a_projected"), 1)
                                        if c == 1 and t >= LAG:
                                            turn(t - LAG)
                                pe.wait_ge(sem("a_ctx_k_loaded"), 16)
                                pe.transpose(ps[:, 7, 0:P], ctx_k[:, :], ident[:, :]).then_inc(sem("a_ctx_turned"), 1)
                                for t in range(NT - LAG, NT):
                                    turn(t)

                            @block.scalar
                            def _(act):
                                def take_turned(t):
                                    tt = slice(t * P, (t + 1) * P)
                                    act.wait_ge(sem("a_qk_turned"), t + 1)
                                    high_parts(act, ps[:, 4 + t % 3, 0:384].rearrange("p (m n) -> p m n", m=3), q=Q[:, :, :, tt])
                                    high_parts(act, ps[:, 4 + t % 3, 384:512], k=KH[:, :, tt]).then_inc(sem("a_qk_high"), 1)

                                for j in range(2 * NT):
                                    t = j % NT
                                    act.wait_ge(sem("a_projected"), j + 1)
                                    if j < NT:
                                        act.copy(V[:, t, :], ps[:, j % 4, P:2 * P]).then_inc(sem("a_v_copied"), 1)
                                        act.copy(Z[:, t, 384:512], ps[:, j % 4, 0:P]).then_inc(sem("a_projected_copied"), 1)
                                    else:
                                        act.copy(Z[:, t, 0:384], ps[:, j % 4, 0:384]).then_inc(sem("a_projected_copied"), 1)
                                        if t >= 4:
                                            take_turned(t - 4)
                                act.wait_ge(sem("a_ctx_turned"), 1)
                                high_parts(act, ps[:, 7, 0:P], k=KH[:, :, CTX_SLOT * P:(CTX_SLOT + 1) * P]).then_inc(sem("a_ctx_high"), 1)
                                for t in range(NT - 4, NT):
                                    take_turned(t)

                            @block.gpsimd
                            def _(pool):
                                pool.wait_ge(sem("a_rotary_loaded"), 32)
                                for t in range(NT + 2):
                                    if 2 <= t < LAT + 2:
                                        u = t - 2
                                        if u >= 2:
                                            pool.wait_ge(sem("a_rotated"), u - 1)
                                        pool.wait_ge(sem("a_normed"), u + 1)
                                        pool.tensor_tensor(r1[:, u % 2, :].rearrange("p (h d) -> p h d", d=HD), Z[:, u, :].rearrange("p (h d) -> p h d", d=HD),
                                                           cos[:, u:u + 1, :].to_broadcast([P, 8, HD]), ALU.mult).then_inc(sem("a_cosines_applied"), 1)
                                    if t < NT:
                                        pool.wait_ge(sem("a_projected_copied"), NT + t + 1)
                                        if t >= 2:
                                            pool.wait_ge(sem("a_squares_summed"), t - 1)
                                        pool.tensor_tensor(sq[:, t % 2, :], Z[:, t, :], Z[:, t, :], ALU.mult).then_inc(sem("a_squared"), 1)
                                    if 1 <= t <= NT:
                                        u = t - 1
                                        pool.wait_ge(sem("a_squares_summed"), t)
                                        pool_step(pool.tensor_scalar(rs[:, u, :], ss[:, u, :], 1.0 / HD, EPS, ALU.mult, ALU.add))
                                        pool.tensor_tensor(rs[:, u, :], rs[:, u, :], minus_half[:, 0:8], ALU.pow).then_inc(sem("a_rstd"), 1)

                            @block.vector
                            def _(dve):
                                dve.wait_ge(sem("a_g_loaded"), 8 * 16)
                                dve.wait_ge(sem("a_rotary_loaded"), 32)
                                dve_step(dve.tensor_scalar(g[:, 0:6, :], g[:, 0:6, :], SCALE, None, ALU.mult))

                                def norm_and_rotate(t):
                                    z = Z[:, t, :].rearrange("p (h d) -> p h d", d=HD)
                                    dve.wait_ge(sem("a_rstd"), t + 1)
                                    dve_step(dve.tensor_tensor(z, z, rs[:, t, :].unsqueeze(2).to_broadcast([P, 8, HD]), ALU.mult))
                                    dve.tensor_tensor(z, z, g[:, :, :], ALU.mult).then_inc(sem("a_normed"), 1)
                                    dve.wait_ge(sem("a_normed"), t + 1)
                                    if t >= 2:
                                        dve.wait_ge(sem("a_qk_turned"), t - 1)
                                    outq = zr[:, t % 2, 0:384].rearrange("p (g n d) -> p n g d", n=2, d=HD)
                                    outk = zr[:, t % 2, 384:512]
                                    if t == PROMPT:
                                        dve_step(dve.tensor_copy(outq, Z[:, t, 0:384].rearrange("p (n g d) -> p n g d", n=2, d=HD)))
                                        dve.tensor_copy(outk, Z[:, t, 384:512]).then_inc(sem("a_rotated"), 1)
                                        return
                                    q16 = HD // 4
                                    for part in range(2):
                                        src = Z[:, t, :].rearrange("p (h f s d) -> p h f s d", f=2, s=2, d=q16)[:, :, :, 1 - part, :]
                                        dst = r2[:, :].rearrange("p (h f s d) -> p h f s d", f=2, s=2, d=q16)[:, :, :, part, :]
                                        tab = sin[:, t:t + 1, :].rearrange("p a (f s d) -> p a f s d", f=2, s=2)[:, :, :, part, :]
                                        dve_step(dve.tensor_tensor(dst, src, tab.to_broadcast([P, 8, 2, q16]), ALU.mult))
                                    dve.wait_ge(sem("a_cosines_applied"), t + 1)
                                    dve_step(dve.tensor_tensor(outq, r1[:, t % 2, 0:384].rearrange("p (n g d) -> p n g d", n=2, d=HD),
                                                               r2[:, 0:384].rearrange("p (n g d) -> p n g d", n=2, d=HD), ALU.add))
                                    dve.tensor_tensor(outk, r1[:, t % 2, 384:512], r2[:, 384:512], ALU.add).then_inc(sem("a_rotated"), 1)

                                def take_turned(t):
                                    tt = slice(t * P, (t + 1) * P)
                                    dve.wait_ge(sem("a_qk_high"), t + 1)
                                    low_parts(dve, ps[:, 4 + t % 3, 0:384].rearrange("p (m n) -> p m n", m=3), q=Q[:, :, :, tt])
                                    low_parts(dve, ps[:, 4 + t % 3, 384:512], k=KH[:, :, tt], k_low=KL[:, tt]).then_inc(sem("a_qk_copied"), 1)

                                for t in range(NT + 5):
                                    if t >= 5:
                                        take_turned(t - 5)
                                    if t < NT:
                                        dve.wait_ge(sem("a_squared"), t + 1)
                                        dve.tensor_reduce(ss[:, t, :], sq[:, t % 2, :].rearrange("p (h d) -> p h d", d=HD),
                                                          AX.X, ALU.add).then_inc(sem("a_squares_summed"), 1)
                                    if 1 <= t <= NT:
                                        norm_and_rotate(t - 1)
                                dve.wait_ge(sem("a_ctx_high"), 1)
                                ctx = slice(CTX_SLOT * P, (CTX_SLOT + 1) * P)
                                low_parts(dve, ps[:, 7, 0:P], k=KH[:, :, ctx], k_low=KL[:, ctx])

                    units = []
                    for t in [PROMPT] + list(range(LAT)):
                        for h in range(6):
                            n = h // 3
                            rows = slice(n * HD, (n + 1) * HD)
                            if t == PROMPT:
                                segments, vs, nk = [(t * P, (t + 1) * P, 0)], [t], P
                            else:
                                segments = [(0, 512, 0), (512, 1024, 512), (CTX_SLOT * P, (CTX_SLOT + 1) * P, 1024)]
                                vs, nk = list(range(LAT)) + [CTX_SLOT], 9 * P
                            q, keys = unit_operands(Q[:, :, h % 3, t * P:(t + 1) * P], KH, KL, n, segments)
                            units.append({"q": q, "keys": keys, "n": nk,
                                          "v": [V[:, x, :] for x in vs], "cols": rows, "bias": None,
                                          "out": mix[:, t, h * HD:(h + 1) * HD]})
                    tensor, scalar, vector, _, _, _ = attention("attn_a", units, own, 0)
                    with nc.Block() as block:
                        block.tensor(tensor)
                        block.scalar(scalar)
                        block.vector(vector)

                        @block.sync
                        def _(sp):
                            load_c_weights(sp, 0)
                            for h in range(6):
                                sp.dma_start(bias_dram[h].rearrange("(c j) -> c j", c=GRID_W),
                                             I["bias_rows"][l, h:h + 1, :].to_broadcast([GRID_W, bias_pitch])).then_inc(sem("bias_copied"), 16)
                            sp.wait_ge(sem("bias_copied"), 6 * 16)
                            sp.wait_ge(sem("a_v_stored"), 16)

            def mixer_c(pair):
                tag = f"c{pair}"
                with ExitStack() as own:
                    Q = sb(f"{tag}_qT", [P, 2, TOK], own, F32R)
                    KH = sb(f"{tag}_kT_high", [P, 2, NSLOT * P], own, F32R)
                    KL = sb(f"{tag}_kT_low", [P, NSLOT * P], own, F32R)
                    kT_prompt = sb(f"{tag}_kT_prompt", [P, P], own)
                    V = sb(f"{tag}_v", [P, NSLOT, P], own)
                    ctx_k = sb(f"{tag}_ctx_k", [P, P], own)
                    k_nat = sb(f"{tag}_k_prompt", [P, P], own)
                    T = sb(f"{tag}_bias", [P, 2, BIAS_U * GRID_W], own)
                    window = sb(f"{tag}_window", [P, WIN_TYPES, WIN], own)
                    slot = pair % 2
                    with nc.Block() as block:
                        @block.sync
                        def _(sp):
                            sp.dma_start(ctx_k[:, :], I["cache_k_nbhd"][l, :, pair * P:(pair + 1) * P]).then_inc(sem(f"{tag}_ctx_k_loaded"), 16)
                            sp.dma_start(V[:, CTX_SLOT, :], I["cache_v_nbhd"][l, :, pair * P:(pair + 1) * P]).then_inc(sem(f"{tag}_tables_loaded"), 16)
                            sp.dma_start(window[:, :, :], I["window"].rearrange("p (w n) -> p w n", w=WIN_TYPES)).then_inc(sem(f"{tag}_tables_loaded"), 16)
                            for j in range(2):
                                by_column = bias_dram[2 * pair + j, GRID_W - 1:GRID_W - 1 + GRID_W * (bias_pitch - 1)].rearrange("(c j) -> c j", c=GRID_W)
                                for r in range(2):
                                    rows = by_column[:, (1 - r) * BIAS_W:(1 - r + BIAS_U) * BIAS_W].rearrange("c (u k) -> c u k", k=BIAS_W)
                                    sp.dma_start(T[r * HD:(r + 1) * HD, j, :].rearrange("p (u k) -> p u k", k=GRID_W),
                                                 rows[:, :, 0:GRID_W]).then_inc(sem(f"{tag}_tables_loaded"), 16)
                            sp.wait_ge(sem(f"{tag}_v_copied"), NT)
                            sp.dma_start(O["new_v_nbhd"][l, :, pair * P:(pair + 1) * P], V[:, PROMPT_SLOT, :]).then_inc(sem(f"{tag}_cache_stored"), 16)
                            sp.wait_ge(sem(f"{tag}_k_prompt_copied"), 1)
                            sp.dma_start(O["new_k_nbhd"][l, :, pair * P:(pair + 1) * P], k_nat[:, :]).then_inc(sem(f"{tag}_cache_stored"), 16)
                            sp.wait_ge(sem(f"{tag}_tables_loaded"), 6 * 16)

                        @block.tensor
                        def _(pe):
                            for j in range(6):
                                m, n = j // 3, j % 3
                                if j >= 3:
                                    pe.wait_ge(sem(f"{tag}_qk_copied"), j - 2)
                                for k in range(KD):
                                    mm = pe.matmul(ps[:, j % 3, 0:384], ring[:, slot, k, m * P:(m + 1) * P], hT[:, k, n * 384:(n + 1) * 384],
                                                   start=(k == 0), stop=(k == KD - 1))
                                mm.then_inc(sem(f"{tag}_qk_projected"), 1)
                            for t in range(NT):
                                if t >= 3:
                                    pe.wait_ge(sem(f"{tag}_v_copied"), t - 2)
                                for k in range(KD):
                                    mm = pe.matmul(ps[:, 3 + t % 3, 0:P], hT[:, k, t * P:(t + 1) * P], ring[:, slot, k, 2 * P:3 * P],
                                                   start=(k == 0), stop=(k == KD - 1))
                                mm.then_inc(sem(f"{tag}_v_projected"), 1)
                            pe.wait_ge(sem(f"{tag}_ctx_k_loaded"), 16)
                            pe.transpose(ps[:, 6, 0:P], ctx_k[:, :], ident[:, :]).then_inc(sem(f"{tag}_ctx_turned"), 1)
                            pe.wait_ge(sem(f"{tag}_k_prompt_kept"), 1)
                            pe.transpose(ps[:, 7, 0:P], kT_prompt[:, :], ident[:, :]).then_inc(sem(f"{tag}_k_prompt_turned"), 1)

                        @block.scalar
                        def _(act):
                            for j in range(6):
                                m, n = j // 3, j % 3
                                act.wait_ge(sem(f"{tag}_qk_projected"), j + 1)
                                nn = slice(n * 384, (n + 1) * 384)
                                if m == 0:
                                    high_parts(act, ps[:, j % 3, 0:384], q=Q[:, :, nn], scale=SCALE).then_inc(sem(f"{tag}_qk_high"), 1)
                                else:
                                    if n == 2:
                                        act.copy(kT_prompt[:, :], ps[:, j % 3, 256:384]).then_inc(sem(f"{tag}_k_prompt_kept"), 1)
                                    high_parts(act, ps[:, j % 3, 0:384], k=KH[:, :, nn]).then_inc(sem(f"{tag}_qk_high"), 1)
                            act.wait_ge(sem(f"{tag}_ctx_turned"), 1)
                            high_parts(act, ps[:, 6, 0:P], k=KH[:, :, CTX_SLOT * P:(CTX_SLOT + 1) * P]).then_inc(sem(f"{tag}_qk_high"), 1)
                            act.wait_ge(sem(f"{tag}_k_prompt_turned"), 1)
                            act.copy(k_nat[:, :], ps[:, 7, 0:P]).then_inc(sem(f"{tag}_k_prompt_copied"), 1)

                        @block.vector
                        def _(dve):
                            for j in range(6):
                                m, n = j // 3, j % 3
                                nn = slice(n * 384, (n + 1) * 384)
                                dve.wait_ge(sem(f"{tag}_qk_high"), j + 1)
                                if m == 0:
                                    a = low_parts(dve, ps[:, j % 3, 0:384], q=Q[:, :, nn], scale=SCALE)
                                else:
                                    a = low_parts(dve, ps[:, j % 3, 0:384], k=KH[:, :, nn], k_low=KL[:, nn])
                                a.then_inc(sem(f"{tag}_qk_copied"), 1)
                            for t in range(NT):
                                dve.wait_ge(sem(f"{tag}_v_projected"), t + 1)
                                dve.tensor_copy(V[:, t, :], ps[:, 3 + t % 3, 0:P]).then_inc(sem(f"{tag}_v_copied"), 1)
                            ctx = slice(CTX_SLOT * P, (CTX_SLOT + 1) * P)
                            dve.wait_ge(sem(f"{tag}_qk_high"), 7)
                            low_parts(dve, ps[:, 6, 0:P], k=KH[:, :, ctx], k_low=KL[:, ctx])

                    units = []
                    for t in [PROMPT] + list(range(LAT)):
                        for j in range(2):
                            rows = slice(j * HD, (j + 1) * HD)
                            w0 = window_start_row(t) * GRID_W if t != PROMPT else 0
                            if t == PROMPT:
                                segments, vs, nk = [(t * P, (t + 1) * P, 0)], [t], P
                            else:
                                segments = [(w0, w0 + 512, 0), (w0 + 512, w0 + WIN, 512), (CTX_SLOT * P, (CTX_SLOT + 1) * P, WIN)]
                                vs, nk = [w0 // P + x for x in range(WIN // P)] + [CTX_SLOT], WIN + P
                            q, keys = unit_operands(Q[:, :, t * P:(t + 1) * P], KH, KL, j, segments)
                            units.append({"q": q, "keys": keys, "n": nk,
                                          "v": [V[:, x, :] for x in vs], "cols": rows,
                                          "bias": None if t == PROMPT else (t, j),
                                          "out": mix[:, t, 640 + (2 * pair + j) * HD:640 + (2 * pair + j + 1) * HD]})
                    tensor, scalar, vector, biased, bias_ready, max_ready = attention(f"attn_{tag}", units, own, WIN + P)
                    with nc.Block() as block:
                        block.tensor(tensor)
                        block.scalar(scalar)
                        block.vector(vector)

                        @block.sync
                        def _(sp):
                            if pair < 2:
                                load_c_weights(sp, pair + 1)
                            else:
                                load_cuts(sp, B_CUTS[:2])
                            sp.wait_ge(sem(f"{tag}_cache_stored"), 32)

                        @block.gpsimd
                        def _(pool):
                            pool_step(pool.memset(biased[:, :, WIN:WIN + P], 0.0))
                            for i, u in enumerate(units):
                                if u["bias"] is None:
                                    continue
                                t, j = u["bias"]
                                if u["bias_n"] > 2:
                                    pool.wait_ge(max_ready, i - 1)
                                u0 = window_start_row(t) - 2 * t + NA_ROWS
                                pool.tensor_tensor(biased[:, u["bias_n"] % 2, 0:WIN], T[:, j, u0 * GRID_W:u0 * GRID_W + WIN],
                                                   window[:, window_type(t), :], ALU.add).then_inc(bias_ready, 1)

            def mixer_b():
                with ExitStack() as own:
                    qT = sb("b_qT", [P, 2, TOK], own)
                    kT = sb("b_kT", [P, 2, 2, TOK], own)
                    K = sb("b_k", [P, NT, 256], own)
                    OG = sb("b_og", [P, NT, 272], own)
                    V = sb("b_v", [P, NT, 4, VA], own)
                    HB = sb("b_h_backward", [P, NT, 256], own)
                    cols = sb("b_columns", [P, 4, 2, NT, 4], own)
                    decay = sb("b_decay", [P, 2, 2, NT], own)
                    state = sb("b_state", [P, 2, 2, 2 * VA], own)
                    state_p = sb("b_state_prompt", [P, 2, 2, 2 * VA], own)
                    gn = sb("b_out_norm", [P, 256], own)
                    cuts = B_CUTS
                    gbias = small[:, 96:112]

                    with nc.Block() as block:
                        @block.sync
                        def _(sp):
                            sp.dma_start(gbias, I["gate_bias"][bass.ds(l, 1), :].to_broadcast([P, 16])).then_inc(sem("b_rows_loaded"), 16)
                            sp.dma_start(gn[:, :], I["out_norm"][bass.ds(l, 1), :].to_broadcast([P, 256])).then_inc(sem("b_rows_loaded"), 16)
                            for c in (2, 3):
                                o, n = cuts[c]
                                sp.wait_ge(sem("b_w_used"), c - 1)
                                sp.dma_start(ring[:, c % 2, :, 0:n], w_in[:, :, o:o + n]).then_inc(sem(f"b_w_loaded{c}"), 16)
                            sp.wait_ge(sem("b_state_cleared"), 1)
                            for d in range(2):
                                for h in range(4):
                                    pr, j = h // 2, h % 2
                                    rows = slice(j * HD, (j + 1) * HD)
                                    sp.dma_start(state[rows, d, pr, j * VA:j * VA + HD], I["state_C"][l, d, h]).then_inc(sem("b_state_loaded"), 16)
                                    sp.dma_start(state[rows, d, pr, j * VA + HD:(j + 1) * VA], I["state_n"][l, d, h]).then_inc(sem("b_state_loaded"), 16)
                            sp.wait_ge(sem("b_rows_loaded"), 32)
                            sp.wait_ge(sem("b_state_loaded"), 16 * 16)

                        @block.gpsimd
                        def _(pool):
                            pool_step(pool.memset(state[:, :, :, :], 0.0))
                            pool.sem_inc(sem("b_state_cleared"), 1)
                            pool_step(pool.memset(state_p[:, :, :, :], 0.0))
                            pool_step(pool.memset(kT[HD:P, :, 0, :], 0.0))
                            pool_step(pool.memset(kT[0:HD, :, 1, :], 0.0))
                            pool_step(pool.memset(V[:, :, :, HD:VA], 1.0))

                        @block.tensor
                        def _(pe):
                            for j in range(6):
                                m, n = j // 3, j % 3
                                if j >= 4:
                                    pe.wait_ge(sem("b_copied"), j - 3)
                                for k in range(KD):
                                    mm = pe.matmul(ps[:, j % 4, 0:384], ring[:, 0, k, m * P:(m + 1) * P], hT[:, k, n * 384:(n + 1) * 384],
                                                   start=(k == 0), stop=(k == KD - 1))
                                mm.then_inc(sem("b_projected"), 1)
                            pe.wait_ge(sem("b_projected"), 6)
                            pe.sem_inc(sem("b_w_used"), 1)
                            for c in range(1, 4):
                                if c >= 2:
                                    pe.wait_ge(sem(f"b_w_loaded{c}"), 16)
                                n = cuts[c][1]
                                for t in range(NT):
                                    j = 6 + (c - 1) * NT + t
                                    pe.wait_ge(sem("b_copied"), j - 3)
                                    for k in range(KD):
                                        mm = pe.matmul(ps[:, j % 4, 0:n], hT[:, k, t * P:(t + 1) * P], ring[:, c % 2, k, 0:n],
                                                       start=(k == 0), stop=(k == KD - 1))
                                    mm.then_inc(sem("b_projected"), 1)
                                    if c == 3:
                                        pe.wait_ge(sem("b_copied"), 6 + NT + t + 1)
                                        if t >= 2:
                                            pe.wait_ge(sem("b_kT_copied"), t - 1)
                                        for m in range(2):
                                            mm = pe.transpose(ps[:, 4 + t % 2, m * P:(m + 1) * P], K[:, t, m * P:(m + 1) * P], ident[:, :])
                                        mm.then_inc(sem("b_k_turned"), 1)
                                pe.wait_ge(sem("b_projected"), 6 + c * NT)
                                pe.sem_inc(sem("b_w_used"), 1)

                        @block.scalar
                        def _(act):
                            for j in range(6 + 3 * NT):
                                act.wait_ge(sem("b_projected"), j + 1)
                                if j < 6:
                                    m, n = j // 3, j % 3
                                    a = act.copy(qT[:, m, n * 384:(n + 1) * 384], ps[:, j % 4, 0:384])
                                else:
                                    c, t = (j - 6) // NT + 1, (j - 6) % NT
                                    if c == 1:
                                        a = act.copy(OG[:, t, :], ps[:, j % 4, 0:272])
                                    elif c == 2:
                                        a = act.mul(K[:, t, :], ps[:, j % 4, 0:256], SCALE)
                                    else:
                                        a = act.copy(V[:, t, :, 0:HD], ps[:, j % 4, 0:256].rearrange("p (h d) -> p h d", d=HD))
                                a.then_inc(sem("b_copied"), 1)
                                if 6 + NT <= j < 6 + 2 * NT:
                                    act.wait_ge(sem("b_copied"), 6 + t + 1)
                                    act.activation(OG[:, t, 0:256], OG[:, t, 0:256], ACT.Exp, scale=-1.0).then_inc(sem("b_sigmoid_exp"), 1)

                        @block.vector
                        def _(dve):
                            o = OG[:, :, 0:256]
                            dve.wait_ge(sem("b_rows_loaded"), 32)
                            dve.wait_ge(sem("b_sigmoid_exp"), NT)
                            dve_step(dve.tensor_scalar(o, o, 1.0, None, ALU.add))
                            dve_step(dve.reciprocal(o, o))
                            dve_step(dve.tensor_tensor(o, o, gn[:, :].unsqueeze(1).to_broadcast([P, NT, 256]), ALU.mult))
                            for t in range(NT):
                                dve.wait_ge(sem("b_k_turned"), t + 1)
                                for j in range(2):
                                    rows = slice(j * HD, (j + 1) * HD)
                                    a = dve.tensor_copy(kT[rows, :, j, t * P:(t + 1) * P], ps[rows, 4 + t % 2, 0:256].rearrange("p (m n) -> p m n", m=2))
                                a.then_inc(sem("b_kT_copied"), 1)

                    hflat = hT[:, :, :].rearrange("p k t -> p (k t)")

                    def rows_of(i):
                        return hflat[0:36, i * TOK:(i + 1) * TOK]
                    B_, A_, M_, WI, AE, FA, FM = (rows_of(i) for i in range(7))
                    LF = B_
                    small_rows = hflat[0:36, 7 * TOK:7 * TOK + 64]
                    m_in = small_rows[:, 0:NT]
                    m_out = small_rows[:, 16:16 + NT]
                    dec = small_rows[:, 32:32 + NT]
                    a_max = small_rows[:, 48:48 + NT]
                    b_last = hflat[0:36, 7 * TOK + 104:7 * TOK + 104 + NT]
                    dec_diag = hflat[0:36, 7 * TOK + 64:7 * TOK + 64 + 4 * NT]
                    gI = hflat[:, 7 * TOK + 128:7 * TOK + 128 + 9 * 36].rearrange("p (t c) -> p t c", c=36)
                    gF = hflat[:, 7 * TOK + 128 + 9 * 36:7 * TOK + 128 + 18 * 36].rearrange("p (t c) -> p t c", c=36)
                    with ExitStack() as inner:
                        raw = sb("b_gates", [P, NT, 16], inner)
                        e1 = sb("b_gate_e", [P, NT, 8], inner)
                        more = HB[:, :, :].rearrange("p t n -> p (t n)")
                        FW, carry_limit = more[0:36, 0:TOK], more[0:36, TOK:2 * TOK]
                        mods = Modulation("mlp_mods", (3, 4, 2, 5),
                                          ring[:, :, :, :].rearrange("p a k n -> p (a k n)").rearrange("p (r k n) -> p r k n", k=KD, n=Modulation.CHUNK), inner)
                        with nc.Block() as block:
                            @block.sync
                            def _(sp):
                                mods.load_gain(sp)
                                for c in range(mods.ring):
                                    mods.load(sp, c)
                                sp.wait_ge(sem("b_m_cleared"), 1)
                                for d in range(2):
                                    sp.dma_start(m_in[32 * d:32 * d + 4, 0:1], I["state_m"][l, d]).then_inc(sem("b_m0_loaded"), 16)
                                for c in range(mods.ring, mods.n):
                                    mods.load(sp, c)
                                sp.wait_ge(sem("b_m0_loaded"), 32)
                                sp.wait_ge(sem("b_stabiliser_done"), 1)
                                for d in range(2):
                                    sp.dma_start(O["new_m"][l, d], m_out[32 * d:32 * d + 4, PROMPT:NT]).then_inc(sem("b_m_stored"), 16)
                                sp.wait_ge(sem("b_m_stored"), 32)

                            @block.gpsimd
                            def _(pool):
                                pool_step(pool.memset(hflat[:, 7 * TOK:8 * TOK], 0.0))
                                pool.sem_inc(sem("b_m_cleared"), 1)
                                for i in (2, 0, 1, 3, 4):
                                    pool_step(pool.memset(rows_of(i), 0.0))
                                pool_step(pool.memset(FW, 0.0))
                                pool_step(pool.memset(hflat[:, 6 * TOK:7 * TOK], 0.0))
                                pool.sem_inc(sem("b_rows_cleared"), 1)
                                pool_step(pool.memset(FA, 1.0))
                                pool_step(pool.memset(FA.rearrange("p (t n) -> p t n", n=P)[:, :, 0:1], 0.0))
                                pool_step(pool.tensor_scalar(carry_limit, FA, 2e38, -1e38, ALU.mult, ALU.add))
                                pool.sem_inc(sem("b_carry_ready"), 1)
                                mods.scale_gate_rows(pool)

                            @block.scalar
                            def _(act):
                                act.wait_ge(sem("b_gate_abs"), 1)
                                act_step(act.activation(e1[:, :, :], e1[:, :, :], ACT.Exp, scale=-1.0))
                                act.activation(e1[:, :, :], e1[:, :, :], ACT.Ln, bias=1.0).then_inc(sem("b_gate_ln"), 1)
                                for c in range(6):
                                    mods.scalar_step(act, c)
                                act.wait_ge(sem("b_arguments"), 1)
                                act_step(act.activation(WI, WI, ACT.Exp))
                                act_step(act.activation(AE, AE, ACT.Exp))
                                act_step(act.activation(B_, B_, ACT.Exp))
                                act_step(act.activation(dec, dec, ACT.Exp))
                                act.sem_inc(sem("b_exponentials"), 1)
                                for c in range(6, mods.n + 1):
                                    mods.scalar_step(act, c)

                            @block.vector
                            def _(dve):
                                dve_step(dve.tensor_tensor(raw[:, :, :], OG[:, :, 256:272], gbias.unsqueeze(1).to_broadcast([P, NT, 16]), ALU.add))
                                r4 = raw[:, :, :].rearrange("p t (d g h) -> p t d g h", d=2, g=2)
                                e4 = e1[:, :, :].rearrange("p t (d h) -> p t d h", d=2)
                                dve_step(dve.scalar_tensor_tensor(e4, r4[:, :, :, 1, :], -1.0, r4[:, :, :, 1, :], ALU.mult, ALU.max))
                                dve.sem_inc(sem("b_gate_abs"), 1)
                                dve.wait_ge(sem("b_gate_ln"), 1)
                                dve.wait_ge(sem("b_m_cleared"), 1)
                                for d in range(2):
                                    dve_step(dve.tensor_copy(gI[:, :, 32 * d:32 * d + 4], r4[:, :, d, 0, :]))
                                    dve_step(dve.scalar_tensor_tensor(gF[:, :, 32 * d:32 * d + 4], r4[:, :, d, 1, :], 0.0, e4[:, :, d, :],
                                                                      ALU.min, ALU.subtract))
                                dve.sem_inc(sem("b_gates_ready"), 1)
                                dve.wait_ge(sem("b_gates_turned"), 1)
                                dve.wait_ge(sem("b_rows_cleared"), 1)
                                for i, dst in enumerate((A_, LF)):
                                    src = psf[0:36, i * TOK:(i + 1) * TOK]
                                    dve_step(dve.tensor_copy(dst[0:4, :], src[0:4, :]))
                                    for a, z in ((0, LAT * P), (LAT * P, TOK)):
                                        dve_step(dve.tensor_copy(dst[32:36, a:z], src[32:36, a:z][:, ::-1]))
                                dve.wait_ge(sem("b_m0_loaded"), 32)
                                dve.wait_ge(sem("b_carry_ready"), 1)
                                dve_step(dve.tensor_tensor_scan(B_, FA, LF, 0.0, ALU.mult, ALU.add))
                                dve_step(dve.tensor_tensor(A_, A_, B_, ALU.subtract))
                                in_chunks = [x.rearrange("p (t n) -> p t n", n=P) for x in (A_, B_, WI)]
                                dve_step(dve.tensor_reduce(a_max, in_chunks[0], AX.X, ALU.max))
                                dve_step(dve.tensor_copy(b_last, in_chunks[1][:, :, P - 1]))
                                dve_step(dve.tensor_tensor_scan(m_out[:, 0:LAT], a_max[:, 0:LAT], b_last[:, 0:LAT], m_in[:, 0:1], ALU.max, ALU.add))
                                dve_step(dve.tensor_tensor_scan(m_out[:, LAT:NT], a_max[:, LAT:NT], b_last[:, LAT:NT], 0.0, ALU.max, ALU.add))
                                dve_step(dve.tensor_copy(m_in[:, 1:LAT], m_out[:, 0:LAT - 1]))
                                dve_step(dve.tensor_copy(WI, A_))
                                dve_step(dve.tensor_tensor(in_chunks[2][:, :, 0], in_chunks[0][:, :, 0], m_in, ALU.max))
                                dve_step(dve.tensor_tensor_scan(M_, carry_limit, WI, 0.0, ALU.min, ALU.max))
                                dve.sem_inc(sem("b_stabiliser_done"), 1)
                                M3, A3, W3, E3 = (x.rearrange("p (t n) -> p t n", n=P) for x in (M_, A_, WI, AE))
                                mlast = M3[:, :, P - 1]
                                dve_step(dve.tensor_tensor(W3, m_in.unsqueeze(2).to_broadcast([36, NT, P]), M3, ALU.subtract))
                                dve_step(dve.tensor_tensor(E3, A3, mlast.unsqueeze(2).to_broadcast([36, NT, P]), ALU.subtract))
                                dve_step(dve.scalar_tensor_tensor(B_, B_, -1.0, M_, ALU.mult, ALU.subtract))
                                dve_step(dve.tensor_tensor(dec, m_in, mlast, ALU.subtract))
                                dve.sem_inc(sem("b_arguments"), 1)

                                def in_token_order(dst, src):
                                    dve_step(dve.tensor_copy(dst[0:4, :], src[0:4, :]))
                                    for a, z in ((0, LAT * P), (LAT * P, TOK)):
                                        dve_step(dve.tensor_copy(dst[32:36, a:z], src[32:36, a:z][:, ::-1]))
                                in_token_order(FA, A_)
                                in_token_order(FM, M_)
                                dve.wait_ge(sem("b_exponentials"), 1)
                                in_token_order(FW, WI)
                                in_token_order(A_, AE)
                                in_token_order(M_, B_)
                                dve_step(dve.tensor_tensor(dec_diag.rearrange("p (j c) -> p j c", j=4), diagonal[:, :, :],
                                                           dec.unsqueeze(1).to_broadcast([36, 4, NT]), ALU.mult))
                                dve.sem_inc(sem("b_rows_ready"), 1)
                                dve.wait_ge(sem("b_columns_turned"), 2)
                                for q in range(4):
                                    for d in range(2):
                                        dve.tensor_copy(cols[:, q, d, :, :],
                                                        ps[:, q, 0:36 * NT].rearrange("p (t h) -> p t h", t=NT)[:, :, 32 * d:32 * d + 4])
                                for d in range(2):
                                    src = ps[:, 4, d * 64:d * 64 + 4 * NT].rearrange("p (j c) -> p j c", j=4)
                                    for j in range(2):
                                        rows = slice(j * HD, (j + 1) * HD)
                                        dve.tensor_copy(decay[rows, d, :, :], src[rows, j:4:2, :])

                            @block.tensor
                            def _(pe):
                                pe.wait_ge(sem("b_gates_ready"), 1)
                                for i, g_ in enumerate((gI, gF)):
                                    for t in range(NT):
                                        mm = pe.transpose(psf[0:36, i * TOK + t * P:i * TOK + (t + 1) * P], g_[:, t, :], ident[:, :])
                                mm.then_inc(sem("b_gates_turned"), 1)
                                for c in range(11):
                                    mods.tensor_step(pe, c)
                                pe.wait_ge(sem("b_rows_ready"), 1)
                                for q, src in enumerate((FA, FW, M_, A_)):
                                    for t in range(NT):
                                        pe.transpose(ps[:, q, t * 36:(t + 1) * 36], src[:, t * P:(t + 1) * P], ident[0:36, 0:36])
                                for d in range(2):
                                    r = slice(32 * d, 32 * d + 4)
                                    if d == 1:
                                        pe.wait_ge(sem("b_columns_turned"), 1)
                                    pe.matmul(ps[:, 4, d * 64:d * 64 + 4 * NT], ones[r, :], dec_diag[r, :], start=True, stop=True).then_inc(sem("b_columns_turned"), 1)
                                for c in range(11, mods.n):
                                    mods.tensor_step(pe, c)

                    E4 = sb("b_e", [P, 2, 512], own)
                    W4 = sb("b_w", [P, 2, 512], own)
                    J4 = sb("b_inter", [P, 2, 4 * VA], own)
                    N4 = sb("b_num", [P, 2, 4 * VA], own)
                    KS = sb("b_ks", [P, 2, 256], own)
                    dn = small[:, 112:116]
                    rdn = small[:, 116:120]
                    work = [(0, PROMPT, PROMPT), (1, PROMPT, PROMPT)]
                    for c in range(LAT):
                        work += [(0, c, c), (1, LAT - 1 - c, c)]
                    completed = {i: t for i, (d, t, c) in enumerate(work) if t in [w[1] for w in work[:i]]}
                    order = list(completed.values())
                    ss = small[:, 120:120 + 4 * NT].rearrange("p (t h) -> p t h", h=4)
                    rs = small[:, 160:160 + 4 * NT].rearrange("p (t h) -> p t h", h=4)
                    squares = hflat[:, 0:512].rearrange("p (a n) -> p a n", a=2)
                    nw = len(work)
                    qA, qWI, qEM, qAE = range(4)
                    m_rows = hflat[:, 6 * TOK:7 * TOK]
                    with nc.Block() as block:
                        @block.tensor
                        def _(pe):
                            def scores(i):
                                d, t, c = work[i]
                                tt = slice(t * P, (t + 1) * P)
                                if i >= 2:
                                    pe.wait_ge(sem("b_weighted"), i - 1)
                                for h in range(4):
                                    mm = pe.matmul(ps[:, i % 2, h * P:(h + 1) * P], kT[:, h // 2, h % 2, tt], qT[:, h // 2, tt], start=True, stop=True)
                                mm.then_inc(sem("b_scores"), 1)
                                if i >= 1:
                                    pe.wait_ge(sem("b_masked"), i)
                                for h in range(4):
                                    mm = pe.matmul(ps[:, 2, h * P:(h + 1) * P], neg_select[:, d, h, :], m_rows[:, tt], start=True, stop=True)
                                mm.then_inc(sem("b_stabiliser_spread"), 1)

                            def apply(i):
                                d, t, c = work[i]
                                st = state_p if t == PROMPT else state
                                tt = slice(t * P, (t + 1) * P)
                                if i >= 2:
                                    pe.wait_ge(sem("b_combined"), i - 1)
                                    pe.wait_ge(sem("b_state_new"), i - 1)
                                for pr in range(2):
                                    mm = pe.matmul(ps[:, 3 + i % 2, pr * 2 * VA:(pr + 1) * 2 * VA], qT[:, pr, tt], st[:, d, pr, :], start=True, stop=True)
                                mm.then_inc(sem("b_inter_done"), 1)
                                pe.wait_ge(sem("b_weighted"), i + 1)
                                for h in range(4):
                                    mm = pe.matmul(ps[:, 5 + i % 2, h * VA:(h + 1) * VA], W4[:, i % 2, h * P:(h + 1) * P], V[:, t, h, :], start=True, stop=True)
                                mm.then_inc(sem("b_applied"), 1)
                                pe.wait_ge(sem("b_keys_scaled"), i + 1)
                                if i >= 1:
                                    pe.wait_ge(sem("b_state_new"), i)
                                for pr in range(2):
                                    mm = pe.matmul(ps[:, 7, pr * 2 * VA:(pr + 1) * 2 * VA], KS[:, i % 2, pr * P:(pr + 1) * P],
                                                   V[:, t, 2 * pr:2 * pr + 2, :].rearrange("p h d -> p (h d)"), start=True, stop=True)
                                mm.then_inc(sem("b_updated"), 1)
                            scores(0)
                            for i in range(nw):
                                if i + 1 < nw:
                                    scores(i + 1)
                                apply(i)

                        @block.scalar
                        def _(act):
                            for i, (d, t, c) in enumerate(work):
                                act.wait_ge(sem("b_masked"), i + 1)
                                for h in range(4):
                                    a = act.activation(E4[:, i % 2, h * P:(h + 1) * P], E4[:, i % 2, h * P:(h + 1) * P], ACT.Exp,
                                                       bias=cols[:, qA, d, t, h:h + 1])
                                a.then_inc(sem("b_exp"), 1)
                                act.wait_ge(sem("b_inter_done"), i + 1)
                                if i >= 2:
                                    act.wait_ge(sem("b_combined"), i - 1)
                                for h in range(4):
                                    a = act.mul(J4[:, i % 2, h * VA:(h + 1) * VA], ps[:, 3 + i % 2, h * VA:(h + 1) * VA], cols[:, qWI, d, t, h:h + 1])
                                a.then_inc(sem("b_inter_scaled"), 1)

                        @block.gpsimd
                        def _(pool):
                            def add_directions(i):
                                t = completed[i]
                                n = order.index(t)
                                h, sq = mix[:, t, 384:640], squares[:, n % 2, :]
                                pool.wait_ge(sem("b_item_finished"), i + 1)
                                pool_step(pool.tensor_tensor(h, h, HB[:, t, :], ALU.add))
                                if n >= 2:
                                    pool.wait_ge(sem("b_out_summed"), n - 1)
                                pool.tensor_tensor(sq, h, h, ALU.mult).then_inc(sem("b_out_squared"), 1)
                                pool.wait_ge(sem("b_out_squared"), n + 1)
                                pool_step(pool.tensor_tensor(h, h, OG[:, t, 0:256], ALU.mult))

                            def inverse_root(i):
                                t = completed[i]
                                pool.wait_ge(sem("b_out_summed"), order.index(t) + 1)
                                pool_step(pool.tensor_scalar(rs[:, t, :], ss[:, t, :], 1.0 / HD, EPS, ALU.mult, ALU.add))
                                pool_step(pool.tensor_tensor(rs[:, t, :], rs[:, t, :], minus_half[:, 0:4], ALU.pow))

                            def norm_output(i):
                                inverse_root(i)
                                t = completed[i]
                                h = mix[:, t, 384:640].rearrange("p (h d) -> p h d", d=HD)
                                pool_step(pool.tensor_tensor(h, h, rs[:, t, :].unsqueeze(2).to_broadcast([P, 4, HD]), ALU.mult))

                            for i, (d, t, c) in enumerate(work):
                                if i >= 2:
                                    pool.wait_ge(sem("b_updated"), i - 1)
                                pool.tensor_tensor(KS[:, i % 2, :].rearrange("p (h d) -> p h d", d=HD), K[:, t, :].rearrange("p (h d) -> p h d", d=HD),
                                                   cols[:, qAE, d, t, :].unsqueeze(2).to_broadcast([P, 4, HD]), ALU.mult).then_inc(sem("b_keys_scaled"), 1)
                                if i - 3 in completed:
                                    norm_output(i - 3)
                                if i - 2 in completed:
                                    add_directions(i - 2)
                            norm_output(nw - 3)
                            for i in (nw - 2, nw - 1):
                                inverse_root(i)
                                pool.sem_inc(sem("b_last_rstd"), 1)

                        @block.vector
                        def _(dve):
                            def mask(i):
                                d, t, c = work[i]
                                dve.wait_ge(sem("b_stabiliser_spread"), i + 1)
                                if i >= 2:
                                    dve.wait_ge(sem("b_weighted"), i - 1)
                                dve.tensor_tensor(E4[:, i % 2, :].rearrange("p (h t) -> p h t", h=4), ps[:, 2, :].rearrange("p (h t) -> p h t", h=4),
                                                  causal[:, d:d + 1, :].to_broadcast([P, 4, P]), ALU.add).then_inc(sem("b_masked"), 1)

                            def weight(i):
                                dve.wait_ge(sem("b_exp"), i + 1)
                                if i >= 2:
                                    dve.wait_ge(sem("b_applied"), i - 1)
                                dve.tensor_tensor(W4[:, i % 2, :], ps[:, i % 2, :], E4[:, i % 2, :], ALU.mult).then_inc(sem("b_weighted"), 1)

                            def finish(i):
                                d, t, c = work[i]
                                N3 = N4[:, i % 2, :].rearrange("p (h d) -> p h d", d=VA)
                                dve.wait_ge(sem("b_inter_scaled"), i + 1)
                                dve.wait_ge(sem("b_applied"), i + 1)
                                dve.tensor_tensor(N4[:, i % 2, :], ps[:, 5 + i % 2, 0:4 * VA], J4[:, i % 2, :], ALU.add).then_inc(sem("b_combined"), 1)
                                dve.wait_ge(sem("b_updated"), i + 1)
                                st = state_p if t == PROMPT else state
                                for pr in range(2):
                                    for j in range(2):
                                        rows, cc = slice(j * HD, (j + 1) * HD), slice(j * VA, (j + 1) * VA)
                                        o = pr * 2 * VA
                                        a = dve.scalar_tensor_tensor(st[rows, d, pr, cc], st[rows, d, pr, cc], decay[rows, d, pr, c:c + 1],
                                                                     ps[rows, 7, o + j * VA:o + (j + 1) * VA], ALU.mult, ALU.add)
                                a.then_inc(sem("b_state_new"), 1)
                                dve.wait_ge(sem("b_combined"), i + 1)
                                dve_step(dve.scalar_tensor_tensor(dn, N3[:, :, HD], -1.0, N3[:, :, HD], ALU.mult, ALU.max))
                                dve_step(dve.tensor_tensor(dn, dn, cols[:, qEM, d, t, :], ALU.max))
                                dve_step(dve.reciprocal(rdn, dn))
                                dst = (HB[:, t, :] if d else mix[:, t, 384:640]).rearrange("p (h d) -> p h d", d=HD)
                                dve_step(dve.tensor_tensor(dst, N3[:, :, 0:HD], rdn.unsqueeze(2).to_broadcast([P, 4, HD]), ALU.mult))
                                dve.sem_inc(sem("b_item_finished"), 1)

                            def sum_squares(t):
                                n = order.index(t)
                                dve.wait_ge(sem("b_out_squared"), n + 1)
                                dve.tensor_reduce(ss[:, t, :], squares[:, n % 2, :].rearrange("p (h d) -> p h d", d=HD), AX.X, ALU.add).then_inc(sem("b_out_summed"), 1)

                            mask(0)
                            for i in range(nw):
                                weight(i)
                                if i + 1 < nw:
                                    mask(i + 1)
                                if i >= 1:
                                    finish(i - 1)
                                if i - 2 in completed:
                                    sum_squares(completed[i - 2])
                            finish(nw - 1)
                            for i in (nw - 2, nw - 1):
                                t = completed[i]
                                h, sq = mix[:, t, 384:640], squares[:, order.index(t) % 2, :]
                                dve_step(dve.tensor_tensor(h, h, HB[:, t, :], ALU.add))
                                dve_step(dve.tensor_tensor(sq, h, h, ALU.mult))
                                dve.tensor_reduce(ss[:, t, :], sq.rearrange("p (h d) -> p h d", d=HD), AX.X, ALU.add).then_inc(sem("b_out_summed"), 1)
                                dve_step(dve.tensor_tensor(h, h, OG[:, t, 0:256], ALU.mult))
                            for i in (nw - 2, nw - 1):
                                t = completed[i]
                                h = mix[:, t, 384:640].rearrange("p (h d) -> p h d", d=HD)
                                dve.wait_ge(sem("b_last_rstd"), i - nw + 3)
                                dve_step(dve.tensor_tensor(h, h, rs[:, t, :].unsqueeze(2).to_broadcast([P, 4, HD]), ALU.mult))

                        @block.sync
                        def _(sp):
                            sp.wait_ge(sem("b_state_new"), 2)
                            for d in range(2):
                                for h in range(4):
                                    pr, j = h // 2, h % 2
                                    rows = slice(j * HD, (j + 1) * HD)
                                    sp.dma_start(O["new_C"][l, d, h], state_p[rows, d, pr, j * VA:j * VA + HD]).then_inc(sem("b_state_stored"), 16)
                                    sp.dma_start(O["new_n"][l, d, h], state_p[rows, d, pr, j * VA + HD:(j + 1) * VA]).then_inc(sem("b_state_stored"), 16)
                            sp.wait_ge(sem("b_state_stored"), 16 * 16)

            def out_projection():
                CUT = 256
                NCUT = D // CUT
                FIRST_TURNED = 4
                w_out = I["w_out"][l].rearrange("(k p) n -> p k n", p=P)
                with ExitStack() as own:
                    raw = sb("w_out_raw", [P, 2, KD, CUT], own)
                    w_hi = sb("w_out_hi", [P, 2, KD, CUT], own, F32R)
                    w_lo = sb("w_out_lo", [P, 2, KD, CUT], own, F32R)
                    with nc.Block() as block:
                        @block.sync
                        def _(sp):
                            for c in range(NCUT):
                                if c >= 2:
                                    sp.wait_ge(sem("o_w_lo"), c - 1)
                                sp.dma_start(raw[:, c % 2, :, :], w_out[:, :, c * CUT:(c + 1) * CUT]).then_inc(sem(f"o_w_loaded{c % 2}"), 16)
                            sp.dma_start(raw_up[:, :, :], w_up[:, :, 0:HID]).then_inc(sem("m_up_loaded"), 16)

                        @block.gpsimd
                        def _(pool):
                            pool.wait_ge(sem("m_up_hi"), 1)
                            pool.tensor_tensor(up_lo[:, :, :], raw_up[:, :, :], up_hi[:, :, :].bitcast(F32), ALU.subtract).then_inc(sem("m_up_lo"), 1)

                        @block.tensor
                        def _(pe):
                            for t in range(NT):
                                if t >= 2:
                                    pe.wait_ge(sem("o_mix_lo"), t - 1)
                                for k in range(KD):
                                    mm = pe.transpose(psf[:, t % 2 * 1024 + k * P:t % 2 * 1024 + (k + 1) * P], mix[:, t, k * P:(k + 1) * P], ident[:, :])
                                mm.then_inc(sem("o_mix_turned"), 1)
                            for c in range(NCUT):
                                pe.wait_ge(sem("o_w_lo"), c + 1)
                                for t in range(NT):
                                    j = c * NT + t
                                    if c == 0:
                                        pe.wait_ge(sem("o_mix_lo"), t + 1)
                                    if j >= 4:
                                        pe.wait_ge(sem("o_copied"), j - 3)
                                    tt = slice(t * P, (t + 1) * P)
                                    for k in range(KD):
                                        for a, b in ((hi, w_hi), (hi, w_lo), (lo, w_hi)):
                                            mm = pe.matmul(ps[:, 4 + j % 4, 0:CUT], a[:, k, tt], b[:, c % 2, k, :],
                                                           start=(k == 0 and a is hi and b is w_hi), stop=(k == KD - 1 and a is lo))
                                    mm.then_inc(sem("o_projected"), 1)

                        @block.vector
                        def _(dve):
                            def weights(c):
                                dve.wait_ge(sem("o_w_hi"), c + 1)
                                dve.tensor_tensor(w_lo[:, c % 2, :, :], raw[:, c % 2, :, :], w_hi[:, c % 2, :, :].bitcast(F32),
                                                  ALU.subtract).then_inc(sem("o_w_lo"), 1)
                            for t in range(NT):
                                if t == FIRST_TURNED:
                                    weights(0)
                                tt = slice(t * P, (t + 1) * P)
                                dve.wait_ge(sem("o_mix_hi"), t + 1)
                                dve.tensor_tensor(lo[:, :, tt], psf[:, t % 2 * 1024:t % 2 * 1024 + 1024].rearrange("p (k n) -> p k n", n=P),
                                                  hi[:, :, tt].bitcast(F32), ALU.subtract).then_inc(sem("o_mix_lo"), 1)
                            for c in range(1, NCUT):
                                weights(c)

                        @block.scalar
                        def _(act):
                            def weights(c):
                                act.wait_ge(sem(f"o_w_loaded{c % 2}"), 16 * (c // 2 + 1))
                                if c >= 2:
                                    act.wait_ge(sem("o_projected"), (c - 1) * NT)
                                act.copy(w_hi[:, c % 2, :, :], raw[:, c % 2, :, :]).then_inc(sem("o_w_hi"), 1)
                            for t in range(NT):
                                if t == FIRST_TURNED:
                                    weights(0)
                                act.wait_ge(sem("o_mix_turned"), t + 1)
                                act.copy(hi[:, :, t * P:(t + 1) * P],
                                         psf[:, t % 2 * 1024:t % 2 * 1024 + 1024].rearrange("p (k n) -> p k n", n=P)).then_inc(sem("o_mix_hi"), 1)
                            weights(1)
                            for j in range(NCUT * NT):
                                c, t = j // NT, j % NT
                                act.wait_ge(sem("o_projected"), j + 1)
                                act.copy(mix[:, t, c * CUT:(c + 1) * CUT], ps[:, 4 + j % 4, 0:CUT]).then_inc(sem("o_copied"), 1)
                                if t == NT - 1 and c + 2 < NCUT:
                                    weights(c + 2)
                                if t == NT - 1 and c == NCUT - 2:
                                    act.wait_ge(sem("m_up_loaded"), 16)
                                    act.copy(up_hi[:, :, :], raw_up[:, :, :]).then_inc(sem("m_up_hi"), 1)

            def mlp():
                NG = D_FF // HID
                KH = HID // P
                UP = 3 * KH
                DOWN = 2 * NT
                w_down = I["w_ffn_down"][l].rearrange("(g k p) n -> g p k n", p=P, k=KH)
                with ExitStack() as own:
                    raw_down = sb("w_down_raw", [P, KH, D], own)
                    down_hi, down_lo = (sb(f"w_down_{x}", [P, KH, D], own, F32R) for x in ("hi", "lo"))
                    u_hi, u_lo = (sb(f"u_{x}", [P, KH, TOK], own, F32R) for x in ("hi", "lo"))
                    relu = sb("relu", [P, 2, 384], own)
                    square = sb("square", [P, 2, 384], own)
                    with nc.Block() as block:
                        @block.sync
                        def _(sp):
                            for g in range(NG):
                                if g >= 1:
                                    sp.wait_ge(sem("m_up_lo"), g)
                                    sp.dma_start(raw_up[:, :, :], w_up[:, :, g * HID:(g + 1) * HID]).then_inc(sem("m_up_loaded"), 16)
                                if g >= 1:
                                    sp.wait_ge(sem("m_down_lo"), g)
                                sp.dma_start(raw_down[:, :, :], w_down[g]).then_inc(sem("m_down_loaded"), 16)

                        @block.gpsimd
                        def _(pool):
                            pool.memset(mix[:, :, :], 0.0).then_inc(sem("m_out_cleared"), 1)

                            def down_low(g):
                                pool.wait_ge(sem("m_down_hi"), g + 1)
                                pool.tensor_tensor(down_lo[:, :, :], raw_down[:, :, :], down_hi[:, :, :].bitcast(F32), ALU.subtract).then_inc(sem("m_down_lo"), 1)

                            with pool.Fori(0, NG - 1) as g:
                                down_low(g)
                                pool.wait_ge(sem("m_up_hi"), g + 2)
                                pool.tensor_tensor(up_lo[:, :, :], raw_up[:, :, :], up_hi[:, :, :].bitcast(F32), ALU.subtract).then_inc(sem("m_up_lo"), 1)
                            down_low(NG - 1)

                        @block.tensor
                        def _(pe):
                            pe.sem_inc(sem("m_down_done"), 1)
                            with pe.Fori(0, NG) as g:
                                pe.wait_ge(sem("m_up_lo"), g + 1)
                                for j in range(UP):
                                    n, m = j // KH, j % KH
                                    if j >= 3:
                                        pe.wait_ge(sem("m_relu"), g * UP + j - 2)
                                    for k in range(KD):
                                        for a, b in ((up_hi, hi), (up_hi, lo), (up_lo, hi)):
                                            mm = pe.matmul(ps[:, j % 3, 0:384], a[:, k, m * P:(m + 1) * P], b[:, k, n * 384:(n + 1) * 384],
                                                           start=(k == 0 and a is up_hi and b is hi), stop=(k == KD - 1 and a is up_lo))
                                    mm.then_inc(sem("m_up_done"), 1)
                                pe.wait_ge(sem("m_down_lo"), g + 1)
                                pe.wait_ge(sem("m_added"), g * DOWN + 1)
                                for j in range(DOWN):
                                    t, n = j // 2, j % 2
                                    if j % 6 == 0:
                                        pe.wait_ge(sem("m_u_lo"), g * UP + KH * (t // 3 + 1))
                                    if j >= 5:
                                        pe.wait_ge(sem("m_added"), g * DOWN + j - 3)
                                    for k in range(KH):
                                        for a, b in ((u_hi, down_hi), (u_hi, down_lo), (u_lo, down_hi)):
                                            mm = pe.matmul(ps[:, 3 + j % 5, :], a[:, k, t * P:(t + 1) * P], b[:, k, n * 512:(n + 1) * 512],
                                                           start=(k == 0 and a is u_hi and b is down_hi), stop=(k == KH - 1 and a is u_lo))
                                    mm.then_inc(sem("m_down_done"), 1)

                        @block.scalar
                        def _(act):
                            def group(g):
                                act.wait_ge(sem("m_down_loaded"), 16 * g + 16)
                                act.wait_ge(sem("m_down_done"), g * DOWN + 1)
                                act.copy(down_hi[:, :, :], raw_down[:, :, :]).then_inc(sem("m_down_hi"), 1)
                                for j in range(UP):
                                    n, m = j // KH, j % KH
                                    act.wait_ge(sem("m_up_done"), g * UP + j + 1)
                                    if j >= 2:
                                        act.wait_ge(sem("m_u_lo"), g * UP + j - 1)
                                    act.activation(relu[:, j % 2, :], ps[:, j % 3, 0:384], ACT.Relu).then_inc(sem("m_relu"), 1)
                                    act.wait_ge(sem("m_relu"), g * UP + j + 1)
                                    act.activation(square[:, j % 2, :], relu[:, j % 2, :], ACT.Square).then_inc(sem("m_square"), 1)
                                    act.wait_ge(sem("m_square"), g * UP + j + 1)
                                    act.copy(u_hi[:, m, n * 384:(n + 1) * 384], square[:, j % 2, :]).then_inc(sem("m_u_hi"), 1)

                            with act.Fori(0, NG - 1) as g:
                                group(g)
                                act.wait_ge(sem("m_up_loaded"), 16 * g + 32)
                                act.wait_ge(sem("m_up_done"), g * UP + UP)
                                act.copy(up_hi[:, :, :], raw_up[:, :, :]).then_inc(sem("m_up_hi"), 1)
                            group(NG - 1)

                        @block.vector
                        def _(dve):
                            dve.wait_ge(sem("m_out_cleared"), 1)
                            dve.sem_inc(sem("m_added"), 1)
                            with dve.Fori(0, NG) as g:
                                for j in range(UP):
                                    n, m = j // KH, j % KH
                                    dve.wait_ge(sem("m_u_hi"), g * UP + j + 1)
                                    dve.tensor_tensor(u_lo[:, m, n * 384:(n + 1) * 384], square[:, j % 2, :],
                                                      u_hi[:, m, n * 384:(n + 1) * 384].bitcast(F32), ALU.subtract).then_inc(sem("m_u_lo"), 1)
                                for j in range(DOWN):
                                    t, n = j // 2, j % 2
                                    y = mix[:, t, n * 512:(n + 1) * 512]
                                    dve.wait_ge(sem("m_down_done"), g * DOWN + j + 2)
                                    dve.tensor_tensor(y, y, ps[:, 3 + j % 5, :], ALU.add).then_inc(sem("m_added"), 1)

            open_section()
            mixer_memory = ExitStack()
            hT = sb("hT", [P, KD, TOK], mixer_memory)
            ring = sb("ring", [P, 2, KD, W_C], mixer_memory)
            input_norm()
            mixer_a()
            close_section()
            for pair in range(3):
                open_section()
                mixer_c(pair)
                close_section()
            open_section()
            mixer_b()
            close_section()
            mixer_memory.close()
            mlp_memory = ExitStack()
            hi = sb("h_hi", [P, KD, TOK], mlp_memory, F32R)
            lo = sb("h_lo", [P, KD, TOK], mlp_memory, F32R)
            raw_up = sb("w_up_raw", [P, KD, HID], mlp_memory)
            up_hi, up_lo = (sb(f"w_up_{x}", [P, KD, HID], mlp_memory, F32R) for x in ("hi", "lo"))
            w_up = I["w_ffn_up"][l].rearrange("(k p) n -> p k n", p=P)
            open_section()
            out_projection()
            residual_norm("mix", 0, True)
            mlp()
            mlp_memory.close()
            residual_norm("mlp", 1, False)
            close_section()

        sem_stack.close()


OUTS = (
    ("y_prompt", (P, D), (1, P, D)),
    ("y_sample", (LAT * P, D), (1, LAT * P, D)),
    ("new_k_attn", (DEPTH, P, 2 * HD), (1, DEPTH, P, 2, HD)),
    ("new_v_attn", (DEPTH, P, 2 * HD), (1, DEPTH, P, 2, HD)),
    ("new_k_nbhd", (DEPTH, P, 6 * HD), (1, DEPTH, P, 6, HD)),
    ("new_v_nbhd", (DEPTH, P, 6 * HD), (1, DEPTH, P, 6, HD)),
    ("new_C", (DEPTH, 2, 4, HD, HD), (1, DEPTH, 2, 4, HD, HD)),
    ("new_n", (DEPTH, 2, 4, HD, 1), (1, DEPTH, 2, 4, HD)),
    ("new_m", (DEPTH, 2, 4, 1), (1, DEPTH, 2, 4)),
)


def kernel(**inputs):
    import concourse.bacc as bacc
    from concourse.bass_utils import run_bass_kernel_spmd

    a = {k: np.asarray(v) for k, v in inputs.items()}
    bias_rows = np.zeros((DEPTH, 6, BIAS_DR, BIAS_W), np.float32)
    bias_rows[:, :, 2:17, GRID_W - NA_COLS:GRID_W + NA_COLS - 1] = a["nbhd_rel_bias"]

    def transposed(v):
        v = v.reshape(v.shape[:-1] + (KD, P))
        return np.moveaxis(v, -1, 0)

    laid = {
        "x_sample": a["x_sample"].reshape(LAT * P, D),
        "x_prompt": a["x_prompt"].reshape(P, D),
        "condT": transposed(np.stack([a["c"].reshape(D), a["c_ctx"]])).transpose(0, 2, 1),
        "w_ada": a["w_ada"], "b_ada": a["b_ada"],
        "g_preT": transposed(np.stack([a["g_pre_mix"], a["g_pre_ffn"]], 1)).transpose(1, 0, 2, 3),
        "g_post": np.stack([a["g_post_mix"], a["g_post_ffn"]], 1),
        "w_in": a["w_in"], "w_out": a["w_out"], "w_ffn_up": a["w_ffn_up"], "w_ffn_down": a["w_ffn_down"],
        "q_norm": a["q_norm_attn"], "k_norm": a["k_norm_attn"],
        "gate_bias": a["mlstm_gate_bias"], "out_norm": a["mlstm_out_norm"].reshape(DEPTH, 256),
        "bias_rows": bias_rows.reshape(DEPTH, 6, BIAS_DR * BIAS_W),
        "cache_k_attn": a["cache_k_attn"].reshape(DEPTH, P, 2 * HD),
        "cache_v_attn": a["cache_v_attn"].reshape(DEPTH, P, 2 * HD),
        "cache_k_nbhd": a["cache_k_nbhd"].reshape(DEPTH, P, 6 * HD),
        "cache_v_nbhd": a["cache_v_nbhd"].reshape(DEPTH, P, 6 * HD),
        "state_C": a["state_mlstm_C"].reshape(DEPTH, 2, 4, HD, HD),
        "state_n": a["state_mlstm_n"].reshape(DEPTH, 2, 4, HD, 1),
        "state_m": a["state_mlstm_m"].reshape(DEPTH, 2, 4, 1),
        **shape_constants(),
    }
    laid = {k: np.ascontiguousarray(v) for k, v in laid.items()}
    nc = bacc.Bacc("TRN2", target_bir_lowering=False, num_devices=1)
    ins = {k: nc.dram_tensor(f"in_{k}", v.shape, F32, kind="ExternalInput").ap() for k, v in laid.items()}
    outs = {k: nc.dram_tensor(f"out_{k}", s, F32, kind="ExternalOutput").ap() for k, s, _ in OUTS}
    with nc.allow_non_contiguous_dma(reason="single columns of the mLSTM state"):
        build(nc, ins, outs)
    r = run_bass_kernel_spmd(nc, [{f"in_{k}": v for k, v in laid.items()}], core_ids=[0])
    return tuple(np.asarray(r.results[0][f"out_{k}"]).reshape(full) for k, _, full in OUTS)
```
